# Optimizing a Trainium2 kernel written in Bass

```python
import jax, jax.numpy as jnp
from jax import lax
import numpy as np

D_MODEL = 1024
BATCH = 1
SEQ = 1024
DEPTH = 1
DEC_BATCH = 1
DEC_SEQ = 64
PAST_LEN = 512

CHUNK = 64
D_MIX = D_MODEL
D_POOL = D_MIX // 2
D_CONV = D_MIX - D_POOL
POOL_WINDOWS = (2, 4, 8, 16)
N_POOL_GROUPS = len(POOL_WINDOWS)
POOL_GROUP_DIM = D_POOL // N_POOL_GROUPS
POOL_STATE = max(POOL_WINDOWS) - 1
CONV_WIDTH = 31
CONV_STATE = CONV_WIDTH - 1
D_IN = D_POOL + 2 * D_CONV
N_EXPERT_GROUPS = 4
EXPERTS_PER_GROUP = 8
N_EXPERTS = N_EXPERT_GROUPS * EXPERTS_PER_GROUP
TOP_K = 2
D_FF_EXPERT = D_MODEL // 2
MOE_BLOCK = 128
EPS = 1e-6

kernel_name = "hybrid_pool_conformer_hmoe_stream_step"

def rms_norm(x, g):
    xf = x.astype(jnp.float32)
    y = xf * lax.rsqrt(jnp.mean(xf * xf, axis=-1, keepdims=True) + EPS)
    return (y * g.astype(jnp.float32)).astype(x.dtype)

def layer_norm(x, g, b):
    xf = x.astype(jnp.float32)
    mu = jnp.mean(xf, axis=-1, keepdims=True)
    var = jnp.mean(jnp.square(xf - mu), axis=-1, keepdims=True)
    y = (xf - mu) * lax.rsqrt(var + EPS)
    return (y * g.astype(jnp.float32) + b.astype(jnp.float32)).astype(x.dtype)

def pool_mix(u, prefix, pos0, pool_lin, pool_scale):
    B, T, _ = u.shape
    ext = jnp.concatenate([prefix.astype(u.dtype), u], axis=1)
    extf = ext.astype(jnp.float32)
    cs = jnp.concatenate([jnp.zeros((B, 1, D_POOL), jnp.float32), jnp.cumsum(extf, axis=1)], axis=1)
    P = POOL_STATE
    end = cs[:, P + 1:P + 1 + T]
    pos = pos0 + jnp.arange(T)
    means = []
    for g, w in enumerate(POOL_WINDOWS):
        sl = slice(g * POOL_GROUP_DIM, (g + 1) * POOL_GROUP_DIM)
        s = end[..., sl] - cs[:, P + 1 - w:P + 1 - w + T, sl]
        cnt = jnp.minimum(pos + 1, w).astype(jnp.float32)
        means.append(s / cnt[None, :, None])
    d = jnp.concatenate(means, axis=-1) - extf[:, P:]
    d = d.astype(u.dtype).reshape(B, T, N_POOL_GROUPS, POOL_GROUP_DIM)
    y = jnp.einsum('btgc,gcd->btgd', d, pool_lin).reshape(B, T, D_POOL) * pool_scale
    return y, ext[:, -POOL_STATE:]

def conv_mix(a, b, prefix, conv_dw, conv_dw_b, ln_g, ln_b):
    v = a * jax.nn.sigmoid(b)
    ext = jnp.concatenate([prefix.astype(v.dtype), v], axis=1)
    h = lax.conv_general_dilated(ext, conv_dw[:, None, :].astype(ext.dtype), window_strides=(1,),
                                 padding='VALID', dimension_numbers=('NWC', 'WIO', 'NWC'),
                                 feature_group_count=D_CONV) + conv_dw_b
    h = layer_norm(h, ln_g, ln_b)
    return h * jax.nn.sigmoid(h), ext[:, -CONV_STATE:]

def hier_moe(h, w_rg, b_rg, w_re, b_re, w_eg, w_eu, w_ed):
    N, D = h.shape
    pg = jax.nn.softmax((h @ w_rg).astype(jnp.float32) + b_rg.astype(jnp.float32), axis=-1)
    p_grp, g_sel = lax.top_k(pg, 1)
    le = jnp.einsum('nd,gde->nge', h, w_re).astype(jnp.float32) + b_re.astype(jnp.float32)
    le = jnp.take_along_axis(le, g_sel[:, :, None], axis=1)[:, 0]
    pe = jax.nn.softmax(le, axis=-1)
    top_p, top_i = lax.top_k(pe, TOP_K)
    gates = p_grp * (top_p / jnp.sum(top_p, axis=-1, keepdims=True))
    eid = g_sel * EXPERTS_PER_GROUP + top_i
    M = N * TOP_K
    flat_e = eid.reshape(-1).astype(jnp.int32)
    flat_tok = jnp.repeat(jnp.arange(N, dtype=jnp.int32), TOP_K)
    flat_gate = gates.reshape(-1)
    order = jnp.argsort(flat_e)
    se = flat_e[order]
    counts = jnp.bincount(flat_e, length=N_EXPERTS)
    padded = (counts + MOE_BLOCK - 1) // MOE_BLOCK * MOE_BLOCK
    pad_end = jnp.cumsum(padded)
    pad_start = pad_end - padded
    start = jnp.cumsum(counts) - counts
    dest = pad_start[se] + jnp.arange(M) - start[se]
    n_blocks = -(-(M + N_EXPERTS * (MOE_BLOCK - 1)) // MOE_BLOCK)
    slots = n_blocks * MOE_BLOCK
    buf_tok = jnp.full((slots,), N, jnp.int32).at[dest].set(flat_tok[order])
    buf_gate = jnp.zeros((slots,), jnp.float32).at[dest].set(flat_gate[order])
    block_e = jnp.minimum(jnp.searchsorted(pad_end, jnp.arange(n_blocks) * MOE_BLOCK, side='right'),
                          N_EXPERTS - 1)
    hp = jnp.concatenate([h, jnp.zeros((1, D), h.dtype)], axis=0)
    xb = hp[buf_tok].reshape(n_blocks, MOE_BLOCK, D)

    def expert(args):
        xblk, e = args
        return (jax.nn.silu(xblk @ w_eg[e]) * (xblk @ w_eu[e])) @ w_ed[e]

    yb = lax.map(expert, (xb, block_e)).reshape(slots, D)
    y = jnp.zeros((N + 1, D), jnp.float32).at[buf_tok].add(yb.astype(jnp.float32) * buf_gate[:, None])
    return y[:N].astype(h.dtype)

def trunk_layer(x, pool_prefix, conv_prefix, pos0, norm1_g, w_in, pool_lin, pool_scale, conv_dw,
                conv_dw_b, conv_ln_g, conv_ln_b, w_out, b_out, norm2_g, w_rg, b_rg, w_re, b_re,
                w_eg, w_eu, w_ed):
    B, T, D = x.shape
    z = rms_norm(x, norm1_g) @ w_in
    u_pool = z[..., :D_POOL]
    a = z[..., D_POOL:D_POOL + D_CONV]
    gate = z[..., D_POOL + D_CONV:]
    y_pool, s_pool = pool_mix(u_pool, pool_prefix, pos0, pool_lin, pool_scale)
    y_conv, s_conv = conv_mix(a, gate, conv_prefix, conv_dw, conv_dw_b, conv_ln_g, conv_ln_b)
    x = x + jnp.concatenate([y_pool, y_conv], axis=-1) @ w_out + b_out
    hm = rms_norm(x, norm2_g).reshape(B * T, D)
    x = x + hier_moe(hm, w_rg, b_rg, w_re, b_re, w_eg, w_eu, w_ed).reshape(B, T, D)
    return x, s_pool, s_conv

def setup_inputs(seed: int = 0) -> dict:
    key = jax.random.key(seed)
    ks = jax.random.split(key, 24)
    f32 = jnp.float32
    nrm = lambda k, shp, s: jax.random.normal(k, shp, f32) * s
    L = DEPTH
    return {
        "x_prompt": nrm(ks[0], (BATCH, SEQ, D_MODEL), 1.0),
        "x_sample": nrm(ks[1], (DEC_BATCH, DEC_SEQ, D_MODEL), 1.0),
        "state_pool": nrm(ks[2], (L, DEC_BATCH, POOL_STATE, D_POOL), 1.0),
        "state_conv": nrm(ks[3], (L, DEC_BATCH, CONV_STATE, D_CONV), 0.5),
        "norm1_g": 1.0 + nrm(ks[4], (L, D_MODEL), 0.02),
        "w_in": nrm(ks[5], (L, D_MODEL, D_IN), D_MODEL ** -0.5),
        "pool_lin": nrm(ks[6], (L, N_POOL_GROUPS, POOL_GROUP_DIM, POOL_GROUP_DIM), POOL_GROUP_DIM ** -0.5),
        "pool_scale": 1.0 + nrm(ks[7], (L, D_POOL), 0.02),
        "conv_dw": nrm(ks[8], (L, CONV_WIDTH, D_CONV), CONV_WIDTH ** -0.5),
        "conv_dw_b": nrm(ks[9], (L, D_CONV), 0.02),
        "conv_ln_g": 1.0 + nrm(ks[10], (L, D_CONV), 0.02),
        "conv_ln_b": nrm(ks[11], (L, D_CONV), 0.02),
        "w_out": nrm(ks[12], (L, D_MIX, D_MODEL), D_MIX ** -0.5),
        "b_out": nrm(ks[13], (L, D_MODEL), 0.02),
        "norm2_g": 1.0 + nrm(ks[14], (L, D_MODEL), 0.02),
        "w_rg": nrm(ks[15], (L, D_MODEL, N_EXPERT_GROUPS), D_MODEL ** -0.5),
        "b_rg": nrm(ks[16], (L, N_EXPERT_GROUPS), 0.01),
        "w_re": nrm(ks[17], (L, N_EXPERT_GROUPS, D_MODEL, EXPERTS_PER_GROUP), D_MODEL ** -0.5),
        "b_re": nrm(ks[18], (L, N_EXPERT_GROUPS, EXPERTS_PER_GROUP), 0.01),
        "w_eg": nrm(ks[19], (L, N_EXPERTS, D_MODEL, D_FF_EXPERT), D_MODEL ** -0.5),
        "w_eu": nrm(ks[20], (L, N_EXPERTS, D_MODEL, D_FF_EXPERT), D_MODEL ** -0.5),
        "w_ed": nrm(ks[21], (L, N_EXPERTS, D_FF_EXPERT, D_MODEL), D_FF_EXPERT ** -0.5),
        "norm_f_g": 1.0 + nrm(ks[22], (D_MODEL,), 0.02),
    }

def reference(x_prompt, x_sample, state_pool, state_conv, norm1_g, w_in, pool_lin, pool_scale,
              conv_dw, conv_dw_b, conv_ln_g, conv_ln_b, w_out, b_out, norm2_g, w_rg, b_rg, w_re,
              b_re, w_eg, w_eu, w_ed, norm_f_g):
    hp, hs = x_prompt, x_sample
    B = x_prompt.shape[0]
    pool_p, conv_p, pool_s, conv_s = [], [], [], []
    for l in range(DEPTH):
        params = (norm1_g[l], w_in[l], pool_lin[l], pool_scale[l], conv_dw[l], conv_dw_b[l],
                  conv_ln_g[l], conv_ln_b[l], w_out[l], b_out[l], norm2_g[l], w_rg[l], b_rg[l],
                  w_re[l], b_re[l], w_eg[l], w_eu[l], w_ed[l])
        zp_pool = jnp.zeros((B, POOL_STATE, D_POOL), hp.dtype)
        zp_conv = jnp.zeros((B, CONV_STATE, D_CONV), hp.dtype)
        hp, sp1, sp2 = trunk_layer(hp, zp_pool, zp_conv, 0, *params)
        hs, ss1, ss2 = trunk_layer(hs, state_pool[l], state_conv[l], PAST_LEN, *params)
        pool_p.append(sp1); conv_p.append(sp2); pool_s.append(ss1); conv_s.append(ss2)
    y_prompt = rms_norm(hp, norm_f_g)
    y_sample = rms_norm(hs, norm_f_g)
    new_state_pool_prompt = jnp.stack(pool_p)
    new_state_conv_prompt = jnp.stack(conv_p)
    new_state_pool_sample = jnp.stack(pool_s)
    new_state_conv_sample = jnp.stack(conv_s)
    return (y_prompt, y_sample, new_state_pool_prompt, new_state_conv_prompt, new_state_pool_sample, new_state_conv_sample)


_drawn_inputs = setup_inputs


def setup_inputs(seed=0):
    import zlib

    import numpy as np

    out = dict(_drawn_inputs(seed))
    spreads = {}
    factors = {'conv_ln_g': 13.426,
     'conv_ln_b': 15.115,
     'b_rg': 58.931,
     'b_re': 18.763,
     'norm_f_g': 22.449,
     'pool_scale': 13.129,
     'norm1_g': 2.686,
     'conv_dw_b': 2.741,
     'b_out': 5.922,
     'norm2_g': 6.252}
    for name, (base, spread) in spreads.items():
        noise = np.random.default_rng([zlib.crc32(name.encode()), seed]).standard_normal(out[name].shape)
        drawn = base * np.exp(spread * noise) if base else spread * noise
        out[name] = __import__('jax').numpy.asarray(drawn.astype(out[name].dtype))
    for name, factor in factors.items():
        out[name] = (out[name] * factor).astype(out[name].dtype)
    return out
```

```python
from contextlib import ExitStack

import concourse.bass as bass
from concourse import mybir

F32 = mybir.dt.float32
F32R = mybir.dt.float32r
I32 = mybir.dt.int32
U32 = mybir.dt.uint32
ALU = mybir.AluOpType
ACT = mybir.ActivationFunctionType
AX_X = mybir.AxisListType.X

P = 128
BANK = 512
EPS = 1e-6
FAR = float(1 << 20)
LOWEST = -3.0e38


def trunk_kernel(nc, x_prompt, x_sample, state_pool, state_conv, norm1_g, w_in, pool_lin, pool_scale,
                 conv_dw, conv_dw_b, conv_ln_g, conv_ln_b, w_out, b_out, norm2_g, w_rg, b_rg, w_re,
                 b_re, w_eg, w_eu, w_ed, norm_f_g,
                 y_prompt, y_sample, pool_state_prompt, conv_state_prompt, pool_state_sample,
                 conv_state_sample):
    SEQ, D = x_prompt.shape[1], x_prompt.shape[2]
    DEC = x_sample.shape[1]
    KD = D // P
    PS, DPOOL = state_pool.shape[2], state_pool.shape[3]
    CS, DCONV = state_conv.shape[2], state_conv.shape[3]
    TAPS = CS + 1
    NG = pool_lin.shape[1]
    NC = DCONV // P
    GROUPS, PER = w_re.shape[1], w_re.shape[3]
    E = GROUPS * PER
    FF = w_eg.shape[3]
    KF = FF // P
    T = SEQ + DEC
    NT = -(-T // P)
    ROWS = [min(P, T - t * P) for t in range(NT)]
    BLOCKS = [(0, BANK), (BANK, BANK), (SEQ, DEC)]
    OVERFLOW = (2 * T - 1) // P
    NBLK = E + OVERFLOW
    LB = GROUPS + E
    assert SEQ == 2 * BANK and NG == NC == 4 and KD == 8 and KF == 4 and PER == 8 and NBLK % 2 == 0
    VW = CS + SEQ + CS + DEC
    HW_ = VW - CS
    UW = PS + SEQ + PS + DEC
    PAIRS = E // 2
    MAX_PAIRS = NBLK // 2

    ctx = ExitStack()
    with ctx:
        def sb(name, shape, dt=F32):
            return ctx.enter_context(nc.sbuf_tensor(name, shape, dt))

        def sem(name):
            return ctx.enter_context(nc.semaphore(name))

        hm_dram = nc.dram_tensor("hm_scratch", [T, D], F32).ap()
        x2_dram = nc.dram_tensor("x2_scratch", [T, D], F32).ap()
        y2_dram = nc.dram_tensor("y2_scratch", [2 * T, D], F32).ap()

        big = sb("big", [P, 2 * KD * T], F32R)
        ring = sb("ring", [P, 4 * D], F32R)
        hTr = sb("hTr", [P, 2 * FF], F32R)
        xT_h = big[:, 0:KD * T].rearrange("p (k t) -> p k t", k=KD)
        xT_l = big[:, KD * T:2 * KD * T].rearrange("p (k t) -> p k t", k=KD)
        wo_h = big[:, 0:KD * D].rearrange("p (k n) -> p k n", k=KD)
        wo_l = big[:, KD * D:2 * KD * D].rearrange("p (k n) -> p k n", k=KD)
        HP = 2048
        we_h = [big[:, s * 2 * HP:s * 2 * HP + HP] for s in range(4)]
        we_l = [big[:, s * 2 * HP + HP:(s + 1) * 2 * HP] for s in range(4)]
        part_h = [ring[:, s * 2 * D:s * 2 * D + D].rearrange("p (k n) -> p k n", k=KD) for s in range(2)]
        part_l = [ring[:, s * 2 * D + D:(s + 1) * 2 * D].rearrange("p (k n) -> p k n", k=KD) for s in range(2)]
        hT_h = hTr[:, 0:FF].rearrange("p (k n) -> p k n", k=KF)
        hT_l = hTr[:, FF:2 * FF].rearrange("p (k n) -> p k n", k=KF)

        SZ_V, SZ_U, SZ_H = NC * VW, NG * UW, NC * HW_
        SZ_S1, SZ_S2, SZ_X, SZ_W, SZ_T = 2 * UW, 2112, 2 * D, 3 * D, D
        arena = sb("arena", [P, SZ_V + SZ_U + SZ_H + SZ_S1 + SZ_S2 + SZ_X + SZ_W + SZ_T])
        at = [0]

        def region(size):
            at[0] += size
            return arena[:, at[0] - size:at[0]]

        r_v, r_u, r_h = region(SZ_V), region(SZ_U), region(SZ_H)
        r_s1, r_s2, r_x, r_w, r_t = region(SZ_S1), region(SZ_S2), region(SZ_X), region(SZ_W), region(SZ_T)
        v_ext = r_v.rearrange("p (c t) -> p c t", c=NC)
        u_ext = r_u.rearrange("p (g t) -> p g t", g=NG)
        hc = r_h.rearrange("p (c t) -> p c t", c=NC)
        win = [r_s1[:, 0:UW], r_s1[:, UW:2 * UW]]
        ln_sd = r_s1[:, 0:T]
        hm = [r_s1[:, 0:D], r_s1[:, D:2 * D]]
        junk = r_s2[:, 0:D]
        sg = r_s2[:, D:D + T]
        sq = r_s2[:, 0:NC * BANK].rearrange("p (c t) -> p c t", c=NC)
        states = r_s2[:, 0:4 * BANK].rearrange("p (s n) -> p s n", s=4)
        M1 = r_s2[:, 0:NT * E].rearrange("p (t e) -> p t e", e=E)
        M2 = r_s2[:, NT * E:2 * NT * E].rearrange("p (t e) -> p t e", e=E)
        MS = r_s2[:, 2 * NT * E:3 * NT * E].rearrange("p (t e) -> p t e", e=E)
        prod = r_s2[:, 3 * NT * E:4 * NT * E].rearrange("p (t e) -> p t e", e=E)
        hot_b = r_s2[:, 0:2 * NT * NBLK].rearrange("p (s b) -> p s b", b=NBLK)
        hot_p = r_w[:, 0:2 * NT * P].rearrange("p (s q) -> p s q", q=P)
        xt = [r_x[:, 0:D], r_x[:, D:2 * D]]
        w_raw = [r_w[:, s * D:(s + 1) * D] for s in range(3)]
        g1_bc = r_t
        hmT = r_t.rearrange("p (k n) -> p k n", k=KD)
        raw = [arena[:, s * HP:(s + 1) * HP] for s in range(6)]
        xe = xt
        ye = [r_s1[:, 0:D], r_s1[:, D:2 * D]]
        act_t = [r_t[:, 0:FF], r_t[:, FF:2 * FF]]
        hid = [r_s2[:, 0:FF], r_s2[:, FF:2 * FF]]
        y_in = [arena[:, s * 2 * D:(s + 1) * 2 * D] for s in range(2)]
        x_in = [arena[:, 4 * D + s * D:4 * D + (s + 1) * D] for s in range(2)]
        gf_bc = arena[:, 6 * D:7 * D]
        junk_f = arena[:, 7 * D:8 * D]

        ident = sb("ident", [P, P])
        tri = sb("tri", [P, P])
        ones = sb("ones", [P, P])
        mean_w = sb("mean_w", [P, P])
        iota_i = r_s1[:, BANK:BANK + P].bitcast(I32)
        iota = sb("iota", [P, P])
        grp = sb("grp", [P, E])
        tok_i = r_s1[:, BANK + P:BANK + P + 2 * NT].bitcast(I32)
        tokv = sb("tokv", [P, 2 * NT])
        inv_cnt = sb("inv_cnt", [P, PS])
        eps = sb("eps", [P, 1])
        NROW = TAPS + 4 + PS + CS
        rows = r_s1[0:NROW, 0:BANK]
        cols = sb("cols", [P, NC, NROW])
        R_B, R_LG, R_LB, R_SC = TAPS, TAPS + 1, TAPS + 2, TAPS + 3
        R_SP, R_SV = TAPS + 4, TAPS + 4 + PS
        plin = sb("plin", [P, NG, P])
        w_rt = sb("w_rt", [P, KD, LB])
        b_rt = sb("b_rt", [P, LB])
        g2_bc = sb("g2_bc", [P, D])
        bo_bc = sb("bo_bc", [P, D])
        stat = sb("stat", [P, 6, NT])
        fix = sb("fix", [P, PS])
        lgt = sb("lgt", [P, 8 + E])
        top = sb("top", [P, 2, 8])
        topi = sb("topi", [P, 2, 8], U32)
        gsel = sb("gsel", [P, 1])
        pen = sb("pen", [P, E])
        le = sb("le", [P, E])
        eid = sb("eid", [P, NT, 2])
        gdif = sb("gdif", [P, NT, GROUPS])
        edif = sb("edif", [P, NT])
        gates = sb("gates", [P, 2, NT])
        gtmp = sb("gtmp", [P, 2, NT])
        pref = sb("pref", [P, NT + 1, E])
        rk = sb("rk", [P, NT + 1, E])
        cum = [sb("cum0", [P, 16 + E]), sb("cum1", [P, 16 + E])]
        nb = sb("nb", [P, E])
        base = sb("base", [P, E])
        sl = sb("sl", [P, 6, 2 * NT])
        sl_i = sb("sl_i", [P, 3, 2 * NT], I32)
        cmp_ = sb("cmp_", [1, OVERFLOW, E])
        eob_f = sb("eob_f", [1, OVERFLOW + 2])
        eob = sb("eob", [1, OVERFLOW + 2], I32)
        idx_f = sb("idx_f", [P, 2, NBLK])
        s_idx = sb("s_idx", [P, 1 + NBLK], U32)
        g_idx = sb("g_idx", [P, NBLK + 2], U32)
        cur = sb("cur", [P, 4], U32)

        ps = ctx.enter_context(nc.psum_tensor("ps", [P, 8 * BANK], F32))

        def banks(a, n):
            return ps[:, a * BANK:(a + n) * BANK]

        z_ps = [banks(0, 3), banks(3, 3)]
        x_ps = banks(6, 2).rearrange("p (k n) -> p k n", k=KD)
        cols_ps = banks(7, 1)[:, 0:NC * NROW].rearrange("p (c r) -> p c r", c=NC)
        st_ps = [banks(6, 1), banks(7, 1)]
        mean_ps = [banks(0, 1), banks(1, 1), banks(2, 1)]
        var_ps = [banks(3, 1), banks(4, 1), banks(5, 1)]
        out_ps = [banks(2, 2), banks(4, 2)]
        lg_ps = banks(0, 1)[:, 0:LB]
        rk_ps = banks(1, 1)[:, 0:(NT + 1) * E].rearrange("p (t e) -> p t e", e=E)
        ix_ps = banks(0, 1)[:, 0:NBLK]
        xe_ps = banks(0, 2).rearrange("p (k n) -> p k n", k=KD)
        gate_ps, up_ps = banks(2, 1), banks(3, 1)
        h_ps = banks(4, 1).rearrange("p (k n) -> p k n", k=KF)
        ye_ps = banks(5, 2)

        const_done = sem("const_done")
        rows_in, g1_in, consts_in, rows_tr, cols_done = map(sem, ("rows_in", "g1_in", "consts_in", "rows_tr", "cols_done"))
        xt_in = [sem("xt_in0"), sem("xt_in1")]
        w_in_s = [sem(f"w_raw_in{s}") for s in range(3)]
        sum1_done, sd1_done, rs1_done, xs_done, xtr_done, xh_done, xl_done = map(sem, (
            "sum1_done", "sd1_done", "rs1_done", "xs_done", "xtr_done", "xh_done", "xl_done"))
        wh_done, wl_done, z_done, sg_done, v_done, u_done, pad_done = map(sem, (
            "wh_done", "wl_done", "z_done", "sg_done", "v_done", "u_done", "pad_done"))
        conv_step, conv_done, st_tr, st_done, st_out, win_step, d_done, pl_done, yp_done = map(sem, (
            "conv_step", "conv_done", "st_tr", "st_done", "st_out", "win_step", "d_done", "pl_done", "yp_done"))
        mean_done, cen_done, sq_done, var_done, lnsd_done, lnrs_done, nrm_done, mix_done = map(sem, (
            "mean_done", "cen_done", "sq_done", "var_done", "lnsd_done", "lnrs_done", "nrm_done", "mix_done"))
        mh_done, ml_done, out_done, xb_done, x2_done, sum2_done, sd2_done, rs2_done, hm_done = map(sem, (
            "mh_done", "ml_done", "out_done", "xb_done", "x2_done", "sum2_done", "sd2_done", "rs2_done", "hm_done"))
        x2_out = [sem("x2_out0"), sem("x2_out1")]
        hm_out = [sem("hm_out0"), sem("hm_out1")]
        hmtr_done, hmT_done, lg_done, lg_read, rt_step, rt_done, exp_done = map(sem, (
            "hmtr_done", "hmT_done", "lg_done", "lg_read", "rt_step", "rt_done", "exp_done"))
        pref_done, rk_done, hot_done, ix_done, plan_done, idx_done = map(sem, (
            "pref_done", "rk_done", "hot_done", "ix_done", "plan_done", "idx_done"))
        raw_in = [sem(f"raw_in{s}") for s in range(6)]
        high_done, low_dve, low_pool, piece_used = map(sem, ("high_done", "low_dve", "low_pool", "piece_used"))
        gath = [sem("gath0"), sem("gath1")]
        scat = [sem("scat0"), sem("scat1")]
        xe_tr, xe_high, xe_low, silu_done, act_done, h_tr, h_high, h_low, ye_done, cur_done, zero_done = map(sem, (
            "xe_tr", "xe_high", "xe_low", "silu_done", "act_done", "h_tr", "h_high", "h_low", "ye_done", "cur_done",
            "zero_done"))
        f_in = [sem("f_in0"), sem("f_in1")]
        gf_in, f_acc, f_sum, f_sd, f_rs, f_y = map(sem, ("gf_in", "f_acc", "f_sum", "f_sd", "f_rs", "f_y"))
        f_out = [sem("f_out0"), sem("f_out1")]
        sc_all, cur_seen = sem("scattered"), sem("cur_seen")

        def x_rows(t):
            return x_prompt[0, t * P:(t + 1) * P, :] if t * P < SEQ else x_sample[0, :, :]

        CHUNKS = [DPOOL + off + c * P for c in range(NC) for off in (0, DCONV)] + [g * P for g in range(NG)]
        NCH = len(CHUNKS)
        def hc_at(tok):
            return tok if tok < SEQ else tok + CS

        PIECES = [(0, "g", 0), (0, "g", 1), (0, "u", 0), (0, "u", 1), (1, "g", 0), (1, "g", 1),
                  (0, "d", 0), (0, "d", 1), (1, "u", 0), (1, "u", 1), (1, "d", 0), (1, "d", 1)]
        NP = len(PIECES)
        POOL_PIECES = (5, 11)

        def low_count(n):
            mine = [m for m in range(NP) if (m in POOL_PIECES) == (n in POOL_PIECES)]
            return (low_pool if n in POOL_PIECES else low_dve), len(mine), mine.index(n) + 1

        def wait_low(eng, j, n):
            s, per, k = low_count(n % NP)
            eng.wait_ge(s, j * per + (per if n >= 0 else 0) + k)

        def load_pairs(eng):
            eng.wait_ge(plan_done, 1)
            return eng.value_load(eob[0:1, OVERFLOW:OVERFLOW + 1], min_val=PAIRS, max_val=MAX_PAIRS)

        def pair_loop(eng, body, n_pairs):
            with eng.Fori(0, PAIRS) as j:
                body(j, False)
            with eng.Fori(PAIRS, MAX_PAIRS) as j:
                with eng.If(n_pairs > j):
                    body(j, True)
                eng.nop()

        block = ctx.enter_context(nc.Block())

        @block.sync
        def _(sp):
            r0 = 0
            for src in (conv_dw[0], conv_dw_b, conv_ln_g, conv_ln_b, pool_scale, state_pool[0, 0], state_conv[0, 0]):
                n = src.shape[0]
                sp.dma_start(rows[r0:r0 + n, :], src).then_inc(rows_in, 16)
                r0 += n
            sp.dma_start(xt[0], x_rows(0)).then_inc(xt_in[0], 16)
            sp.dma_start(g1_bc, norm1_g[0].partition_broadcast(P)).then_inc(g1_in, 16)
            sp.dma_start(xt[1], x_rows(1)).then_inc(xt_in[1], 16)

            def load_w_in(j):
                if j >= 3:
                    sp.wait_ge(wl_done, j - 2)
                src = w_in[0, :, CHUNKS[j]:CHUNKS[j] + P].rearrange("(k p) n -> p k n", p=P)
                sp.dma_start(w_raw[j % 3].rearrange("p (k n) -> p k n", k=KD), src).then_inc(w_in_s[j % 3], 16)

            for j in range(3):
                load_w_in(j)
            for t in range(2, NT):
                sp.wait_ge(xtr_done, t - 1)
                sp.dma_start(xt[t % 2][0:ROWS[t], :], x_rows(t)).then_inc(xt_in[t % 2], 16)
            sp.dma_start(plin[:, :, :], pool_lin[0].rearrange("g c d -> c g d")).then_inc(consts_in, 16)
            sp.dma_start(w_rt[:, :, 0:GROUPS], w_rg[0].rearrange("(p k) n -> p k n", p=P)).then_inc(consts_in, 16)
            for g in range(GROUPS):
                at_g = GROUPS + g * PER
                sp.dma_start(w_rt[:, :, at_g:at_g + PER],
                             w_re[0, g].rearrange("(p k) n -> p k n", p=P)).then_inc(consts_in, 16)
            sp.dma_start(b_rt[:, 0:GROUPS], b_rg[0].partition_broadcast(P)).then_inc(consts_in, 16)
            sp.dma_start(b_rt[:, GROUPS:LB],
                         b_re[0].rearrange("g e -> (g e)").partition_broadcast(P)).then_inc(consts_in, 16)
            sp.dma_start(g2_bc[:, :], norm2_g[0].partition_broadcast(P)).then_inc(consts_in, 16)
            sp.dma_start(bo_bc[:, :], b_out[0].partition_broadcast(P)).then_inc(consts_in, 16)
            for j in range(3, NCH):
                load_w_in(j)
            for k in range(KD):
                j = NCH + k
                sp.wait_ge(wl_done, j - 2)
                sp.dma_start(w_raw[j % 3], w_out[0, k * P:(k + 1) * P, :]).then_inc(w_in_s[j % 3], 16)
            dst = (pool_state_prompt[0, 0], pool_state_sample[0, 0], conv_state_prompt[0, 0], conv_state_sample[0, 0])
            for s in range(4):
                sp.wait_ge(st_done, s + 1)
                sp.dma_start(dst[s], states[0:(PS if s < 2 else CS), s, :]).then_inc(st_out, 16)

            def load_residual(t):
                sp.dma_start(xt[t % 2][0:ROWS[t], :], x_rows(t)).then_inc(xt_in[t % 2], 16)

            sp.wait_ge(xtr_done, NT)
            load_residual(0)
            load_residual(1)
            for t in range(NT):
                sp.wait_ge(x2_done, t + 1)
                sp.dma_start(x2_dram[t * P:t * P + ROWS[t], :], xt[t % 2][0:ROWS[t], :]).then_inc(x2_out[t % 2], 16)
                sp.wait_ge(hm_done, t + 1)
                sp.dma_start(hm_dram[t * P:t * P + ROWS[t], :], hm[t % 2][0:ROWS[t], :]).then_inc(hm_out[t % 2], 16)
                if t + 2 < NT:
                    sp.wait_ge(x2_out[t % 2], 16 * (t // 2 + 1))
                    load_residual(t + 2)
            sp.wait_ge(mh_done, NT)
            sp.wait_ge(ml_done, NT)
            sp.wait_ge(st_tr, 4)

            def weights(j, overflow):
                if overflow:
                    e = [sp.value_load(eob[0:1, bass.ds(2 * j + b - E, 1)], min_val=0, max_val=E - 1) for b in (0, 1)]
                else:
                    e = [2 * j, 2 * j + 1]
                for n, (b, m, half) in enumerate(PIECES):
                    w = {"g": w_eg, "u": w_eu, "d": w_ed}[m]
                    src = w[0, bass.ds(e[b], 1), :, :].rearrange("a (p k) n -> p (a k n)", p=P)
                    wait_low(sp, j, n - 6)
                    sp.dma_start(raw[n % 6], src[:, half * HP:(half + 1) * HP]).then_inc(raw_in[n % 6], 16)

            with sp.Fori(0, PAIRS) as j:
                weights(j, False)
            n_pairs = load_pairs(sp)
            with sp.Fori(PAIRS, MAX_PAIRS) as j:
                with sp.If(n_pairs > j):
                    weights(j, True)
                sp.nop()
            wait_low(sp, n_pairs - 1, NP - 2)
            wait_low(sp, n_pairs - 1, NP - 1)
            sp.dma_start(gf_bc, norm_f_g.partition_broadcast(P)).then_inc(gf_in, 16)
            sp.wait_ge(sc_all, 1)
            for s in range(2):
                sp.wait_ge(x2_out[s], 16 * len(range(s, NT, 2)))

            def load_final(t):
                r = ROWS[t]
                sp.dma_start(y_in[t % 2][0:r, :], y2_dram[2 * t * P:2 * (t * P + r), :]
                             .rearrange("(p k) n -> p (k n)", k=2)).then_inc(f_in[t % 2], 16)
                sp.dma_start(x_in[t % 2][0:r, :], x2_dram[t * P:t * P + r, :]).then_inc(f_in[t % 2], 16)

            load_final(0)
            load_final(1)
            for t in range(NT):
                sp.wait_ge(f_y, t + 1)
                dst = y_prompt[0, t * P:(t + 1) * P, :] if t * P < SEQ else y_sample[0, :, :]
                sp.dma_start(dst, x_in[t % 2][0:ROWS[t], :]).then_inc(f_out[t % 2], 16)
                if t + 2 < NT:
                    sp.wait_ge(f_out[t % 2], 16 * (t // 2 + 1))
                    load_final(t + 2)
            sp.wait_ge(st_out, 64)
            for s in range(2):
                sp.wait_ge(f_out[s], 16 * len(range(s, NT, 2)))

        @block.scalar
        def _(act):
            act.sem_inc(high_done, NP)
            act.sem_inc(xe_high, 2)
            act.sem_inc(silu_done, 2)
            act.sem_inc(h_high, 2)
            act.sem_inc(ye_done, 2)

            def w_high(j):
                act.wait_ge(w_in_s[j % 3], 16 * (j // 3 + 1))
                if j < NCH:
                    if j >= 2:
                        act.wait_ge(z_done, j - 1)
                    out, src = part_h[j % 2], w_raw[j % 3].rearrange("p (k n) -> p k n", k=KD)
                else:
                    act.wait_ge(z_done, NCH)
                    out, src = wo_h[:, j - NCH, :], w_raw[j % 3]
                act.activation(out, src, ACT.Copy).then_inc(wh_done, 1)

            act.wait_ge(rows_tr, 1)
            act.activation(cols[:, :, :], cols_ps, ACT.Copy).then_inc(cols_done, 1)

            def x_high(t):
                act.wait_ge(xtr_done, t + 1)
                act.activation(xT_h[:, :, t * P:t * P + ROWS[t]], x_ps[:, :, 0:ROWS[t]], ACT.Copy).then_inc(xh_done, 1)

            act.wait_ge(const_done, 1)
            for t in range(NT):
                r = ROWS[t]
                act.wait_ge(xt_in[t % 2], 16 * (t // 2 + 1))
                if t:
                    act.wait_ge(sum1_done, t)
                act.activation(junk[0:r, :], xt[t % 2][0:r, :], ACT.Square,
                               accum_out=stat[0:r, 0, t:t + 1]).then_inc(sum1_done, 1)
                act.wait_ge(sum1_done, t + 1)
                act.activation(stat[0:r, 1, t:t + 1], stat[0:r, 0, t:t + 1], ACT.Sqrt, bias=eps[0:r, :],
                               scale=1.0 / D).then_inc(sd1_done, 1)
                if t >= 1:
                    x_high(t - 1)
                if t < 2:
                    w_high(t)
            x_high(NT - 1)
            for c in range(NC):
                w_high(2 * c + 2)
                act.wait_ge(z_done, 2 * c + 2)
                if c:
                    act.wait_ge(v_done, c)
                act.activation(sg, z_ps[1][:, 0:T], ACT.Sigmoid).then_inc(sg_done, 1)
                w_high(2 * c + 3)
            act.wait_ge(pad_done, 1)
            for g in range(NG):
                act.wait_ge(z_done, 2 * NC + g + 1)
                act.activation(u_ext[:, g, PS:PS + SEQ], z_ps[g % 2][:, 0:SEQ], ACT.Copy)
                act.activation(u_ext[:, g, PS + SEQ + PS:UW], z_ps[g % 2][:, SEQ:T], ACT.Copy).then_inc(u_done, 1)
                if g < 2:
                    w_high(2 * NC + 2 + g)
            for s in range(2):
                act.wait_ge(st_tr, s + 1)
                act.activation(states[0:PS, s, :], st_ps[s][0:PS, :], ACT.Copy).then_inc(st_done, 1)
            for s in range(2):
                act.wait_ge(st_tr, s + 3)
                act.activation(states[0:CS, 2 + s, :], st_ps[s][0:CS, :], ACT.Copy).then_inc(st_done, 1)
            for k in range(3):
                w_high(NCH + k)
            for g in range(NG):
                act.wait_ge(pl_done, g + 1)
                act.activation(u_ext[:, g, 0:T], z_ps[g % 2][:, 0:T], ACT.Copy,
                               scale=cols[:, g, R_SC:R_SC + 1]).then_inc(yp_done, 1)
            for k in range(3, KD):
                w_high(NCH + k)
            act.wait_ge(st_out, 64)

            def ln_square(n):
                tok, w = BLOCKS[n]
                act.wait_ge(cen_done, n + 1)
                if n:
                    act.wait_ge(var_done, n)
                act.activation(sq[:, :, 0:w], hc[:, :, hc_at(tok):hc_at(tok) + w], ACT.Square).then_inc(sq_done, 1)

            def ln_deviation(n):
                tok, w = BLOCKS[n]
                act.wait_ge(var_done, n + 1)
                act.activation(ln_sd[:, tok:tok + w], var_ps[n][:, 0:w], ACT.Sqrt, bias=eps[:, :]).then_inc(lnsd_done, 1)

            def ln_swish(n):
                tok, w = BLOCKS[n]
                act.wait_ge(nrm_done, n + 1)
                for c in range(NC):
                    y = hc[:, c, hc_at(tok):hc_at(tok) + w]
                    act.activation(y, y, ACT.Silu, scale=cols[:, c, R_LG:R_LG + 1],
                                   bias=cols[:, c, R_LB:R_LB + 1]).then_inc(mix_done, 1)

            for n in range(3):
                ln_square(n)
                ln_deviation(n)
            for n in range(3):
                ln_swish(n)

            def mix_high(t):
                r, tok = ROWS[t], t * P
                act.wait_ge(mix_done, NC * (min(tok // BANK, 2) + 1))
                if t >= 2:
                    act.wait_ge(out_done, t - 1)
                act.activation(part_h[t % 2][:, 0:NG, 0:r], u_ext[:, :, tok:tok + r], ACT.Copy)
                act.activation(part_h[t % 2][:, NG:KD, 0:r], hc[:, :, hc_at(tok):hc_at(tok) + r],
                               ACT.Copy).then_inc(mh_done, 1)

            def hm_turned(t):
                act.wait_ge(hmtr_done, t + 1)
                if t:
                    act.wait_ge(lg_done, t)
                act.activation(hmT[:, :, 0:ROWS[t]], x_ps[:, :, 0:ROWS[t]], ACT.Copy).then_inc(hmT_done, 1)

            act.wait_ge(yp_done, NG)
            mix_high(0)
            mix_high(1)
            for t in range(NT):
                r = ROWS[t]
                act.wait_ge(x2_done, t + 1)
                if t:
                    act.wait_ge(sum2_done, t)
                else:
                    act.wait_ge(var_done, 3)
                act.activation(junk[0:r, :], xt[t % 2][0:r, :], ACT.Square,
                               accum_out=stat[0:r, 3, t:t + 1]).then_inc(sum2_done, 1)
                act.wait_ge(sum2_done, t + 1)
                act.activation(stat[0:r, 4, t:t + 1], stat[0:r, 3, t:t + 1], ACT.Sqrt, bias=eps[0:r, :],
                               scale=1.0 / D).then_inc(sd2_done, 1)
                if t + 2 < NT:
                    mix_high(t + 2)
                if t >= 1:
                    hm_turned(t - 1)
            hm_turned(NT - 1)
            act.wait_ge(rt_done, NT)
            act.activation(gdif[:, :, :], gdif[:, :, :], ACT.Exp).then_inc(exp_done, 1)
            act.activation(edif[:, :], edif[:, :], ACT.Exp).then_inc(exp_done, 1)

            n_pairs = load_pairs(act)

            def high(j, n):
                act.wait_ge(raw_in[n % 6], 32 * j + 16 * (n // 6 + 1))
                act.wait_ge(piece_used, NP * j + n + 1 + (NP - 4))
                act.activation(we_h[n % 4], raw[n % 6], ACT.Copy).then_inc(high_done, 1)

            def rows_high(j, b):
                act.wait_ge(xe_tr, 2 * j + 3 + b)
                act.activation(part_h[b], xe_ps, ACT.Copy).then_inc(xe_high, 1)

            def silu(j, b):
                act.wait_ge(piece_used, NP * (j + 1) + (2, 6)[b])
                act.wait_ge(h_tr, 2 * j + 1 + b)
                act.activation(act_t[b], gate_ps, ACT.Silu).then_inc(silu_done, 1)

            def hidden_high(j, b):
                act.wait_ge(h_tr, 2 * j + 3 + b)
                act.wait_ge(piece_used, NP * j + (12, 20)[b])
                act.activation(hT_h, h_ps, ACT.Copy).then_inc(h_high, 1)

            def result(j, b):
                act.wait_ge(piece_used, NP * j + (NP + 8, NP)[b])
                act.wait_ge(scat[b], 16 * (j + 1))
                act.activation(ye[b], ye_ps, ACT.Copy).then_inc(ye_done, 1)

            def body(j, overflow):
                for n in (0, 1, 2):
                    high(j, n)
                rows_high(j, 0)
                result(j, 1)
                for n in (3, 4, 5):
                    high(j, n)
                silu(j, 0)
                rows_high(j, 1)
                for n in (6, 7, 8):
                    high(j, n)
                hidden_high(j, 0)
                high(j, 9)
                silu(j, 1)
                high(j, 10)
                high(j, 11)
                result(j, 0)
                hidden_high(j, 1)

            pair_loop(act, body, n_pairs)
            result(n_pairs, 1)
            for t in range(NT):
                r = ROWS[t]
                act.wait_ge(f_acc, 2 * t + 2)
                if t:
                    act.wait_ge(f_sum, t)
                act.activation(junk_f[0:r, :], x_in[t % 2][0:r, :], ACT.Square,
                               accum_out=stat[0:r, 0, t:t + 1]).then_inc(f_sum, 1)
                act.wait_ge(f_sum, t + 1)
                act.activation(stat[0:r, 1, t:t + 1], stat[0:r, 0, t:t + 1], ACT.Sqrt, bias=eps[0:r, :],
                               scale=1.0 / D).then_inc(f_sd, 1)

        @block.tensor
        def _(pe):
            def product(out, parts, last):
                for i, (sh, sl_, mh, ml) in enumerate(parts):
                    pe.matmul(out, sh, mh, start=(i == 0), stop=False)
                    pe.matmul(out, sh, ml, start=False, stop=False)
                    ins = pe.matmul(out, sl_, mh, start=False, stop=(i == len(parts) - 1 and last))
                return ins

            pe.wait_ge(const_done, 1)
            pe.wait_ge(rows_in, 16 * 7)
            for c in range(NC):
                ins = pe.transpose(cols_ps[:, c, :], rows[:, c * P:(c + 1) * P], ident[0:NROW, 0:NROW])
            ins.then_inc(rows_tr, 1)
            pe.wait_ge(cols_done, 1)

            def turn_x(t):
                r = ROWS[t]
                pe.wait_ge(xs_done, t + 1)
                if t:
                    pe.wait_ge(xl_done, t)
                for k in range(KD):
                    ins = pe.transpose(x_ps[:, k, 0:r], xt[t % 2][0:r, k * P:(k + 1) * P], ident[0:r, 0:r])
                ins.then_inc(xtr_done, 1)

            def in_proj(j, n):
                tok, w = BLOCKS[n]
                ins = product(z_ps[j % 2][:, tok:tok + w],
                              [(part_h[j % 2][:, k, :], part_l[j % 2][:, k, :], xT_h[:, k, tok:tok + w],
                                xT_l[:, k, tok:tok + w]) for k in range(KD)], True)
                if n == 2:
                    ins.then_inc(z_done, 1)

            per_block = BANK // P
            for n in range(3):
                for t in range(n * per_block, min((n + 1) * per_block, NT)):
                    turn_x(t)
                pe.wait_ge(xl_done, min((n + 1) * per_block, NT))
                if n == 0:
                    pe.wait_ge(wl_done, 1)
                in_proj(0, n)
            for j in range(1, NCH):
                pe.wait_ge(wl_done, j + 1)
                if j >= 2 * NC + 2:
                    pe.wait_ge(u_done, j - 2 * NC - 1)
                elif j >= 2:
                    pe.wait_ge((v_done, sg_done)[j % 2], (j - 2) // 2 + 1)
                for n in range(3):
                    in_proj(j, n)

            def turn_state(s):
                src, n = (u_ext, PS) if s < 2 else (v_ext, CS)
                end = n + SEQ if s % 2 == 0 else n + SEQ + n + DEC
                for c in range(NC):
                    ins = pe.transpose(st_ps[s % 2][0:n, c * P:(c + 1) * P], src[:, c, end - n:end], ident[:, :])
                ins.then_inc(st_tr, 1)

            pe.wait_ge(u_done, NG)
            turn_state(0)
            turn_state(1)
            for s in (2, 3):
                pe.wait_ge(st_done, s - 1)
                turn_state(s)
            pe.wait_ge(consts_in, 16 * (6 + GROUPS))
            for g in range(NG):
                pe.wait_ge(d_done, g + 1)
                if g >= 2:
                    pe.wait_ge(yp_done, g - 1)
                else:
                    pe.wait_ge(u_done, g + 3)
                for n, (tok, w) in enumerate(BLOCKS):
                    off = PS + tok if tok < SEQ else PS + tok + PS
                    ins = pe.matmul(z_ps[g % 2][:, tok:tok + w], plin[:, g, :], u_ext[:, g, off:off + w],
                                    start=True, stop=True)
                ins.then_inc(pl_done, 1)
            pe.wait_ge(yp_done, NG)
            for n, (tok, w) in enumerate(BLOCKS):
                pe.wait_ge(conv_done, NC)
                for c in range(NC):
                    ins = pe.matmul(mean_ps[n][:, 0:w], mean_w[:, :], hc[:, c, hc_at(tok):hc_at(tok) + w],
                                    start=(c == 0), stop=(c == NC - 1))
                ins.then_inc(mean_done, 1)
            for n, (tok, w) in enumerate(BLOCKS):
                pe.wait_ge(sq_done, n + 1)
                for c in range(NC):
                    ins = pe.matmul(var_ps[n][:, 0:w], mean_w[:, :], sq[:, c, 0:w], start=(c == 0), stop=(c == NC - 1))
                ins.then_inc(var_done, 1)

            def out_proj(t):
                r = ROWS[t]
                pe.wait_ge(ml_done, t + 1)
                if t == 0:
                    pe.wait_ge(wl_done, NCH + KD)
                    pe.wait_ge(cen_done, 3)
                    pe.wait_ge(lnsd_done, 3)
                if t >= 2:
                    pe.wait_ge(x2_done, t - 1)
                for half in range(2):
                    c0 = half * BANK
                    ins = product(out_ps[t % 2][0:r, c0:c0 + BANK],
                                  [(part_h[t % 2][:, k, 0:r], part_l[t % 2][:, k, 0:r], wo_h[:, k, c0:c0 + BANK],
                                    wo_l[:, k, c0:c0 + BANK]) for k in range(KD)], True)
                ins.then_inc(out_done, 1)

            def turn_hm(t):
                r = ROWS[t]
                pe.wait_ge(hm_done, t + 1)
                if t:
                    pe.wait_ge(hmT_done, t)
                for k in range(KD):
                    ins = pe.transpose(x_ps[:, k, 0:r], hm[t % 2][0:r, k * P:(k + 1) * P], ident[0:r, 0:r])
                ins.then_inc(hmtr_done, 1)

            def logits(t):
                r = ROWS[t]
                pe.wait_ge(hmT_done, t + 1)
                if t:
                    pe.wait_ge(lg_read, t)
                for k in range(KD):
                    ins = pe.matmul(lg_ps[0:r, :], hmT[:, k, 0:r], w_rt[:, k, :], start=(k == 0), stop=(k == KD - 1))
                ins.then_inc(lg_done, 1)

            for t in range(NT + 2):
                if t < NT:
                    out_proj(t)
                if 1 <= t <= NT:
                    turn_hm(t - 1)
                if t >= 2:
                    logits(t - 2)
            pe.wait_ge(pref_done, 1)
            pe.wait_ge(const_done, 1)
            for t in range(NT + 1):
                if t < NT:
                    pe.matmul(rk_ps[:, t, :], tri[:, :], MS[:, t, :], start=True, stop=False)
                ins = pe.matmul(rk_ps[:, t, :], ones[:, :], pref[:, t, :], start=(t == NT), stop=True)
            ins.then_inc(rk_done, 1)
            pe.wait_ge(hot_done, 1)
            for s in range(2 * NT):
                ins = pe.matmul(ix_ps, hot_p[:, s, :], hot_b[:, s, :], start=(s == 0), stop=(s == 2 * NT - 1))
            ins.then_inc(ix_done, 1)

            pe.sem_inc(piece_used, NP)
            pe.sem_inc(xe_tr, 2)
            pe.sem_inc(h_tr, 2)
            n_pairs = load_pairs(pe)
            pe.wait_ge(idx_done, 1)

            def turn_rows(j, b):
                pe.wait_ge(gath[b], 16 * (j + 1))
                pe.wait_ge(xe_low, 2 * j + 2 + b)
                for k in range(KD):
                    ins = pe.transpose(xe_ps[:, k, :], xe[b][:, k * P:(k + 1) * P], ident[:, :])
                ins.then_inc(xe_tr, 1)

            def expert_in(j, n, out):
                b, _, half = PIECES[n]
                wait_low(pe, j, n)
                wh = we_h[n % 4].rearrange("p (k n) -> p k n", n=FF)
                wl = we_l[n % 4].rearrange("p (k n) -> p k n", n=FF)
                for i in range(4):
                    k = half * 4 + i
                    pe.matmul(out, part_h[b][:, k, :], wh[:, i, :], start=(k == 0), stop=False)
                    pe.matmul(out, part_h[b][:, k, :], wl[:, i, :], start=False, stop=False)
                    ins = pe.matmul(out, part_l[b][:, k, :], wh[:, i, :], start=False, stop=(k == KD - 1))
                ins.then_inc(piece_used, 1)

            def expert_out(j, n):
                b, _, half = PIECES[n]
                wait_low(pe, j, n)
                wh = we_h[n % 4].rearrange("p (k n) -> p k n", n=D)
                wl = we_l[n % 4].rearrange("p (k n) -> p k n", n=D)
                for i in range(2):
                    k = half * 2 + i
                    for c0 in (0, BANK):
                        out = ye_ps[:, c0:c0 + BANK]
                        pe.matmul(out, hT_h[:, k, :], wh[:, i, c0:c0 + BANK], start=(k == 0), stop=False)
                        pe.matmul(out, hT_h[:, k, :], wl[:, i, c0:c0 + BANK], start=False, stop=False)
                        ins = pe.matmul(out, hT_l[:, k, :], wh[:, i, c0:c0 + BANK], start=False, stop=(k == KF - 1))
                ins.then_inc(piece_used, 1)

            def turn_hidden(j, b):
                pe.wait_ge(act_done, 2 * j + 3 + b)
                pe.wait_ge(h_low, 2 * j + 2 + b)
                for k in range(KF):
                    ins = pe.transpose(h_ps[:, k, :], hid[b][:, k * P:(k + 1) * P], ident[:, :])
                ins.then_inc(h_tr, 1)

            def body(j, overflow):
                turn_rows(j, 0)
                pe.wait_ge(xe_low, 2 * j + 3)
                pe.wait_ge(silu_done, 2 * j + 2)
                expert_in(j, 0, gate_ps)
                expert_in(j, 1, gate_ps)
                turn_rows(j, 1)
                pe.wait_ge(act_done, 2 * j + 2)
                expert_in(j, 2, up_ps)
                expert_in(j, 3, up_ps)
                pe.wait_ge(xe_low, 2 * j + 4)
                pe.wait_ge(silu_done, 2 * j + 3)
                expert_in(j, 4, gate_ps)
                expert_in(j, 5, gate_ps)
                turn_hidden(j, 0)
                pe.wait_ge(h_low, 2 * j + 3)
                pe.wait_ge(ye_done, 2 * j + 2)
                expert_out(j, 6)
                expert_out(j, 7)
                pe.wait_ge(act_done, 2 * j + 3)
                expert_in(j, 8, up_ps)
                expert_in(j, 9, up_ps)
                turn_hidden(j, 1)
                pe.wait_ge(h_low, 2 * j + 4)
                pe.wait_ge(ye_done, 2 * j + 4)
                expert_out(j, 10)
                expert_out(j, 11)

            pair_loop(pe, body, n_pairs)

        @block.vector
        def _(dve):
            n_dve = NP - len(POOL_PIECES)
            dve.sem_inc(low_dve, n_dve)
            dve.sem_inc(xe_low, 2)
            dve.sem_inc(act_done, 2)
            dve.sem_inc(h_low, 2)
            dve.wait_ge(g1_in, 16)

            def x_scaled(t):
                r = ROWS[t]
                dve.wait_ge(sd1_done, t + 1)
                dve.reciprocal(stat[0:r, 2, t:t + 1], stat[0:r, 1, t:t + 1]).then_inc(rs1_done, 1)
                dve.wait_ge(rs1_done, t + 1)
                dve.scalar_tensor_tensor(xt[t % 2][0:r, :], xt[t % 2][0:r, :], stat[0:r, 2, t:t + 1], g1_bc[0:r, :],
                                         ALU.mult, ALU.mult).then_inc(xs_done, 1)

            def x_low(t):
                r, tok = ROWS[t], t * P
                dve.wait_ge(xh_done, t + 1)
                dve.tensor_tensor(xT_l[:, :, tok:tok + r], x_ps[:, :, 0:r], xT_h[:, :, tok:tok + r].bitcast(F32),
                                  ALU.subtract).then_inc(xl_done, 1)

            for t in range(NT):
                x_scaled(t)
                if t:
                    x_low(t - 1)
            x_low(NT - 1)

            dve.wait_ge(cols_done, 1)
            half_w = HW_ // 2
            todo = [(c, j, h) for c in range(NC) for j in range(TAPS) for h in range(2)]
            steps = [0]

            def conv_ops(n, upto):
                for _ in range(n):
                    if not todo or todo[0][0] >= upto:
                        return
                    c, j, h = todo.pop(0)
                    a, b = h * half_w, (half_w, HW_)[h]
                    if j:
                        dve.wait_ge(conv_step, steps[0] - 1)
                        dve.scalar_tensor_tensor(hc[:, c, a:b], v_ext[:, c, a + j:b + j], cols[:, c, j:j + 1],
                                                 hc[:, c, a:b], ALU.mult, ALU.add).then_inc(conv_step, 1)
                    else:
                        dve.tensor_scalar(hc[:, c, a:b], v_ext[:, c, a:b], cols[:, c, 0:1],
                                          cols[:, c, R_B:R_B + 1], ALU.mult, ALU.add).then_inc(conv_step, 1)
                    steps[0] += 1

            dve.wait_ge(pad_done, 1)
            for c in range(NC):
                dve.wait_ge(sg_done, c + 1)
                dve.tensor_tensor(v_ext[:, c, CS:CS + SEQ], z_ps[0][:, 0:SEQ], sg[:, 0:SEQ], ALU.mult).then_inc(conv_step, 1)
                dve.tensor_tensor(v_ext[:, c, CS + SEQ + CS:VW], z_ps[0][:, SEQ:T], sg[:, SEQ:T],
                                  ALU.mult).then_inc(v_done, 1)
                steps[0] += 1
                dve.wait_ge(v_done, c + 1)
                conv_ops(32 if c < NC - 1 else len(todo), c + 1)
            dve.wait_ge(conv_step, steps[0])
            dve.engine_nop().then_inc(conv_done, NC)

            for n, (tok, w) in enumerate(BLOCKS):
                y = hc[:, :, hc_at(tok):hc_at(tok) + w]
                dve.wait_ge(mean_done, n + 1)
                dve.tensor_tensor(y, y, mean_ps[n][:, 0:w].unsqueeze(1).to_broadcast([P, NC, w]),
                                  ALU.subtract).then_inc(cen_done, 1)
            for n, (tok, w) in enumerate(BLOCKS):
                y = hc[:, :, hc_at(tok):hc_at(tok) + w]
                rs = ln_sd[:, tok:tok + w]
                dve.wait_ge(lnsd_done, n + 1)
                dve.reciprocal(rs, rs).then_inc(lnrs_done, 1)
                dve.wait_ge(lnrs_done, n + 1)
                dve.wait_ge(cen_done, n + 1)
                dve.tensor_tensor(y, y, rs.unsqueeze(1).to_broadcast([P, NC, w]), ALU.mult).then_inc(nrm_done, 1)

            def mix_low(t):
                r, tok = ROWS[t], t * P
                dve.wait_ge(mh_done, t + 1)
                dve.tensor_tensor(part_l[t % 2][:, 0:NG, 0:r], u_ext[:, :, tok:tok + r],
                                  part_h[t % 2][:, 0:NG, 0:r].bitcast(F32), ALU.subtract)
                dve.tensor_tensor(part_l[t % 2][:, NG:KD, 0:r], hc[:, :, hc_at(tok):hc_at(tok) + r],
                                  part_h[t % 2][:, NG:KD, 0:r].bitcast(F32), ALU.subtract).then_inc(ml_done, 1)

            def residual(t):
                r = ROWS[t]
                dve.wait_ge(out_done, t + 1)
                dve.wait_ge(xb_done, t + 1)
                dve.tensor_tensor(xt[t % 2][0:r, :], out_ps[t % 2][0:r, :], xt[t % 2][0:r, :],
                                  ALU.add).then_inc(x2_done, 1)

            def hm_row(t):
                r = ROWS[t]
                dve.wait_ge(sd2_done, t + 1)
                dve.reciprocal(stat[0:r, 5, t:t + 1], stat[0:r, 4, t:t + 1]).then_inc(rs2_done, 1)
                dve.wait_ge(rs2_done, t + 1)
                if t >= 2:
                    dve.wait_ge(hm_out[t % 2], 16 * (t // 2))
                    dve.wait_ge(hmtr_done, t - 1)
                dve.scalar_tensor_tensor(hm[t % 2][0:r, :].rearrange("p (k q) -> p q k", k=KD),
                                         xt[t % 2][0:r, :].rearrange("p (q k) -> p q k", k=KD), stat[0:r, 5, t:t + 1],
                                         g2_bc[0:r, :].rearrange("p (q k) -> p q k", k=KD),
                                         ALU.mult, ALU.mult).then_inc(hm_done, 1)

            done = [0]

            def step(ins):
                done[0] += 1
                ins.then_inc(rt_step, 1)
                dve.wait_ge(rt_step, done[0])

            def route(t):
                r = ROWS[t]
                dve.wait_ge(lg_done, t + 1)
                dve.tensor_tensor(lgt[0:r, 0:GROUPS], lg_ps[0:r, 0:GROUPS], b_rt[0:r, 0:GROUPS], ALU.add)
                step(dve.tensor_tensor(lgt[0:r, 8:8 + E], lg_ps[0:r, GROUPS:LB], b_rt[0:r, GROUPS:LB], ALU.add))
                dve.engine_nop().then_inc(lg_read, 1)
                step(dve.max(top[0:r, 0, :], lgt[0:r, 0:8]))
                step(dve.max_index(topi[0:r, 0, :], top[0:r, 0, :], lgt[0:r, 0:8]))
                step(dve.tensor_copy(gsel[0:r, :], topi[0:r, 0, 0:1]))
                step(dve.tensor_scalar(pen[0:r, :], grp[0:r, :], gsel[0:r, :], None, ALU.is_equal))
                step(dve.tensor_scalar(pen[0:r, :], pen[0:r, :], -LOWEST, LOWEST, ALU.mult, ALU.add))
                step(dve.tensor_tensor(le[0:r, :], lgt[0:r, 8:8 + E], pen[0:r, :], ALU.add))
                step(dve.max(top[0:r, 1, :], le[0:r, :]))
                step(dve.max_index(topi[0:r, 1, :], top[0:r, 1, :], le[0:r, :]))
                dve.tensor_copy(eid[0:r, t, :], topi[0:r, 1, 0:2])
                dve.tensor_scalar(gdif[0:r, t, :], lgt[0:r, 0:GROUPS], top[0:r, 0, 0:1], None, ALU.subtract)
                step(dve.tensor_scalar(edif[0:r, t:t + 1], top[0:r, 1, 1:2], top[0:r, 1, 0:1], None, ALU.subtract))
                dve.engine_nop().then_inc(rt_done, 1)

            dve.wait_ge(consts_in, 16 * (6 + GROUPS))
            dve.wait_ge(const_done, 1)
            step(dve.memset(gdif[:, :, :], 0.0))
            step(dve.memset(edif[:, :], 0.0))
            mix_low(0)
            mix_low(1)
            residual(0)
            for t in range(NT):
                if t + 2 < NT:
                    mix_low(t + 2)
                if t + 1 < NT:
                    residual(t + 1)
                hm_row(t)
                if t >= 1:
                    route(t - 1)
            route(NT - 1)

            e_row = iota[:, 0:E].unsqueeze(1).to_broadcast([P, NT, E])
            dve.wait_ge(sum2_done, NT)
            step(dve.tensor_tensor(M1, e_row, eid[:, :, 0:1].to_broadcast([P, NT, E]), ALU.is_equal))
            step(dve.tensor_tensor(M2, e_row, eid[:, :, 1:2].to_broadcast([P, NT, E]), ALU.is_equal))
            step(dve.tensor_tensor(MS, M1, M2, ALU.add))
            step(dve.memset(pref[:, 0, :], 0.0))
            for t in range(NT):
                step(dve.tensor_tensor(pref[:, t + 1, :], pref[:, t, :], MS[:, t, :], ALU.add))
            dve.engine_nop().then_inc(pref_done, 1)
            dve.wait_ge(exp_done, 2)
            step(dve.tensor_reduce(gtmp[:, 0, :], gdif[:, :, :], AX_X, ALU.add))
            step(dve.tensor_scalar(gtmp[:, 1, :], edif[:, :], 1.0, None, ALU.add))
            step(dve.tensor_tensor(gtmp[:, 0, :], gtmp[:, 0, :], gtmp[:, 1, :], ALU.mult))
            step(dve.reciprocal(gates[:, 0, :], gtmp[:, 0, :]))
            step(dve.tensor_tensor(gates[:, 1, :], gates[:, 0, :], edif[:, :], ALU.mult))
            dve.wait_ge(rk_done, 1)
            step(dve.tensor_copy(rk[:, :, :], rk_ps))
            count = rk[:, NT, :]
            step(dve.tensor_scalar(nb[:, :], count, float(P), None, ALU.is_gt))
            for m in range(2, -(-T // P)):
                step(dve.scalar_tensor_tensor(nb[:, :], count, float(m * P), nb[:, :], ALU.is_gt, ALU.add))
            step(dve.memset(cum[0][:, :], 0.0))
            step(dve.memset(cum[1][:, :], 0.0))
            step(dve.tensor_copy(cum[0][:, 16:16 + E], nb[:, :]))
            for i, s in enumerate((1, 2, 4, 8, 16)):
                src, dst = cum[i % 2], cum[(i + 1) % 2]
                step(dve.tensor_tensor(dst[:, 16:16 + E], src[:, 16:16 + E], src[:, 16 - s:16 - s + E], ALU.add))
            ends = cum[1][:, 16:16 + E]
            step(dve.tensor_tensor(base[:, :], ends, nb[:, :], ALU.subtract))
            step(dve.tensor_tensor(cmp_[:, :, :], ends[0:1, :].unsqueeze(1).to_broadcast([1, OVERFLOW, E]),
                                   iota[0:1, 0:OVERFLOW].unsqueeze(2).to_broadcast([1, OVERFLOW, E]), ALU.is_le))
            step(dve.tensor_reduce(eob_f[:, 0:OVERFLOW], cmp_[:, :, :], AX_X, ALU.add))
            step(dve.tensor_scalar(eob_f[:, 0:OVERFLOW], eob_f[:, 0:OVERFLOW], float(E - 1), None, ALU.min))
            evens = iota[0:1, 0:OVERFLOW:2]
            step(dve.tensor_scalar(cmp_[:, 0, 0:OVERFLOW // 2], evens, ends[0:1, E - 1:E], None, ALU.is_lt))
            step(dve.tensor_reduce(eob_f[:, OVERFLOW:OVERFLOW + 1], cmp_[:, 0, 0:OVERFLOW // 2], AX_X, ALU.add))
            step(dve.tensor_scalar(eob_f[:, OVERFLOW:OVERFLOW + 1], eob_f[:, OVERFLOW:OVERFLOW + 1], float(PAIRS), None,
                                   ALU.add))
            dve.tensor_copy(eob[:, 0:OVERFLOW + 1], eob_f[:, 0:OVERFLOW + 1]).then_inc(plan_done, 1)
            s_r, s_b, s_e, s_o, s_s = (sl[:, i, :] for i in range(5))

            def by_choice(x, k):
                return x.rearrange("p (t k) -> p t k", k=2)[:, :, k]

            for k, M in enumerate((M1, M2)):
                step(dve.tensor_tensor(prod, M, rk[:, 0:NT, :], ALU.mult))
                step(dve.tensor_reduce(by_choice(s_r, k), prod, AX_X, ALU.add))
                step(dve.tensor_tensor(prod, M, base[:, :].unsqueeze(1).to_broadcast([P, NT, E]), ALU.mult))
                step(dve.tensor_reduce(by_choice(s_b, k), prod, AX_X, ALU.add))
                step(dve.tensor_copy(by_choice(s_e, k), eid[:, :, k]))
            step(dve.tensor_scalar(s_o, s_r, float(P), None, ALU.is_ge))
            step(dve.tensor_tensor(s_b, s_b, s_e, ALU.subtract))
            step(dve.scalar_tensor_tensor(s_b, s_b, float(E - 1), s_o, ALU.add, ALU.mult))
            step(dve.tensor_tensor(s_b, s_b, s_e, ALU.add))
            step(dve.scalar_tensor_tensor(s_s, s_b, float(P), s_r, ALU.mult, ALU.add))
            step(dve.tensor_copy(sl_i[:, 0, :], s_s))
            step(dve.tensor_scalar(sl_i[:, 1, :], sl_i[:, 0, :], P - 1, None, ALU.bitwise_and))
            step(dve.tensor_scalar(sl_i[:, 2, :], sl_i[:, 0, :], 7, None, ALU.arith_shift_right))
            step(dve.tensor_copy(s_r, sl_i[:, 1, :]))
            step(dve.tensor_copy(s_e, sl_i[:, 2, :]))
            dve.wait_ge(wl_done, NCH + KD)
            step(dve.tensor_tensor(hot_p, iota[:, :].unsqueeze(1).to_broadcast([P, 2 * NT, P]),
                                   s_r.unsqueeze(2).to_broadcast([P, 2 * NT, P]), ALU.is_equal))
            step(dve.tensor_tensor(hot_b, iota[:, 0:NBLK].unsqueeze(1).to_broadcast([P, 2 * NT, NBLK]),
                                   s_e.unsqueeze(2).to_broadcast([P, 2 * NT, NBLK]), ALU.is_equal))
            step(dve.tensor_tensor(hot_b, hot_b, tokv[:, :].unsqueeze(2).to_broadcast([P, 2 * NT, NBLK]), ALU.mult))
            dve.engine_nop().then_inc(hot_done, 1)
            dve.wait_ge(ix_done, 1)
            step(dve.tensor_scalar(idx_f[:, 1, :], ix_ps, 0.0, FAR, ALU.is_equal, ALU.mult))
            step(dve.scalar_tensor_tensor(idx_f[:, 0, :], ix_ps, -1.0, idx_f[:, 1, :], ALU.add, ALU.add))
            step(dve.tensor_copy(s_idx[:, 1:1 + NBLK], idx_f[:, 0, :]))
            step(dve.tensor_scalar(g_idx[:, 0:NBLK], s_idx[:, 1:1 + NBLK], 1, None, ALU.logical_shift_right))
            step(dve.memset(ye_ps, 0.0))
            dve.engine_nop().then_inc(idx_done, 1)

            n_pairs = load_pairs(dve)

            def low(j, n):
                dve.wait_ge(high_done, NP * (j + 1) + n + 1)
                dve.tensor_tensor(we_l[n % 4], raw[n % 6], we_h[n % 4].bitcast(F32), ALU.subtract).then_inc(low_dve, 1)

            def rows_low(j, b):
                dve.wait_ge(xe_high, 2 * j + 3 + b)
                dve.tensor_tensor(part_l[b], xe_ps, part_h[b].bitcast(F32), ALU.subtract).then_inc(xe_low, 1)

            def hidden(j, b):
                dve.wait_ge(silu_done, 2 * j + 3 + b)
                dve.wait_ge(piece_used, NP * (j + 1) + (4, 10)[b])
                dve.tensor_tensor(hid[b].rearrange("p (k q) -> p q k", k=KF),
                                  act_t[b].rearrange("p (q k) -> p q k", k=KF),
                                  up_ps.rearrange("p (q k) -> p q k", k=KF), ALU.mult).then_inc(act_done, 1)

            def hidden_low(j, b):
                dve.wait_ge(h_high, 2 * j + 3 + b)
                dve.tensor_tensor(hT_l, h_ps, hT_h.bitcast(F32), ALU.subtract).then_inc(h_low, 1)

            def body(j, overflow):
                for n in (0, 1, 2):
                    low(j, n)
                rows_low(j, 0)
                low(j, 3)
                low(j, 4)
                rows_low(j, 1)
                low(j, 6)
                hidden(j, 0)
                low(j, 7)
                low(j, 8)
                hidden_low(j, 0)
                low(j, 9)
                low(j, 10)
                hidden(j, 1)
                hidden_low(j, 1)

            pair_loop(dve, body, n_pairs)
            dve.wait_ge(gf_in, 16)
            for t in range(NT):
                r, s = ROWS[t], t % 2
                dve.wait_ge(f_in[s], 32 * (t // 2 + 1))
                for k in range(2):
                    dve.scalar_tensor_tensor(x_in[s][0:r, :], y_in[s][0:r, k * D:(k + 1) * D], gates[0:r, k, t:t + 1],
                                             x_in[s][0:r, :], ALU.mult, ALU.add).then_inc(f_acc, 1)
                    dve.wait_ge(f_acc, 2 * t + k + 1)
                dve.wait_ge(f_sd, t + 1)
                dve.reciprocal(stat[0:r, 2, t:t + 1], stat[0:r, 1, t:t + 1]).then_inc(f_rs, 1)
                dve.wait_ge(f_rs, t + 1)
                dve.scalar_tensor_tensor(x_in[s][0:r, :], x_in[s][0:r, :], stat[0:r, 2, t:t + 1], gf_bc[0:r, :],
                                         ALU.mult, ALU.mult).then_inc(f_y, 1)

        @block.gpsimd
        def _(pool):
            done = [0]

            def step(ins):
                done[0] += 1
                ins.then_inc(zero_done, 1)
                pool.wait_ge(zero_done, done[0])

            for m in (ident, tri):
                step(pool.memset(m[:, :], 0.0 if m is ident else 1.0))
            step(pool.affine_select(out=ident[:, :], in_=ident[:, :], compare_op=ALU.not_equal, fill=1.0, base=0,
                                    pattern=[[-1, P]], channel_multiplier=1))
            step(pool.affine_select(out=tri[:, :], in_=tri[:, :], compare_op=ALU.is_gt, fill=0.0, base=0,
                                    pattern=[[1, P]], channel_multiplier=-1))
            pool.memset(ones[:, :], 1.0)
            pool.memset(mean_w[:, :], 1.0 / DCONV)
            pool.memset(eps[:, :], EPS)
            for g in range(GROUPS):
                pool.memset(grp[:, g * PER:(g + 1) * PER], float(g))
            for i in range(PS):
                pool.memset(inv_cnt[:, i:i + 1], 1.0 / (i + 1))
            pool.memset(lgt[:, GROUPS:8], LOWEST)
            pool.memset(eid[:, :, :], 99.0)
            pool.memset(s_idx[:, 0:1], int(FAR))
            pool.memset(g_idx[:, NBLK:NBLK + 2], int(FAR))
            step(pool.iota(iota_i, pattern=[[1, P]], base=0, channel_multiplier=0))
            step(pool.iota(tok_i, pattern=[[2 * P, NT], [1, 2]], base=1, channel_multiplier=2))
            step(pool.tensor_copy(iota[:, :], iota_i))
            step(pool.tensor_copy(tokv[:, :], tok_i))
            pool.sem_inc(const_done, 1)
            for c in range(NC):
                pool.memset(v_ext[:, c, 0:CS], 0.0)
                pool.memset(u_ext[:, c, 0:PS], 0.0)

            def w_low(j):
                pool.wait_ge(wh_done, j + 1)
                if j < NCH:
                    hi, lo, src = part_h[j % 2], part_l[j % 2], w_raw[j % 3].rearrange("p (k n) -> p k n", k=KD)
                else:
                    hi, lo, src = wo_h[:, j - NCH, :], wo_l[:, j - NCH, :], w_raw[j % 3]
                pool.tensor_tensor(lo, src, hi.bitcast(F32), ALU.subtract).then_inc(wl_done, 1)

            w_low(0)
            pool.wait_ge(cols_done, 1)
            for c in range(NC):
                pool.tensor_copy(v_ext[:, c, CS + SEQ:CS + SEQ + CS], cols[:, c, R_SV:R_SV + CS])
                step(pool.tensor_copy(u_ext[:, c, PS + SEQ:PS + SEQ + PS], cols[:, c, R_SP:R_SP + PS]))
            pool.sem_inc(pad_done, 1)
            for j in range(1, NCH):
                w_low(j)
            n_win = [0]

            def win_op(ins):
                n_win[0] += 1
                ins.then_inc(win_step, 1)
                pool.wait_ge(win_step, n_win[0])

            for g in range(NG):
                w = 2 << g
                pool.wait_ge(u_done, g + 1)
                src, lo = u_ext[:, g, :], 0
                for i in range(g + 1):
                    s = 1 << i
                    lo += s
                    win_op(pool.tensor_tensor(win[i % 2][:, lo:UW], src[:, lo:UW], src[:, lo - s:UW - s], ALU.add))
                    src = win[i % 2]
                win_op(pool.tensor_tensor(fix[:, 0:w - 1], src[:, PS:PS + w - 1], inv_cnt[:, 0:w - 1], ALU.mult))
                win_op(pool.tensor_tensor(fix[:, 0:w - 1], fix[:, 0:w - 1], u_ext[:, g, PS:PS + w - 1], ALU.subtract))
                pool.wait_ge(st_tr, 2)
                win_op(pool.tensor_scalar(src[:, PS:UW], src[:, PS:UW], 1.0 / w, None, ALU.mult))
                win_op(pool.tensor_tensor(u_ext[:, g, PS:UW], src[:, PS:UW], u_ext[:, g, PS:UW], ALU.subtract))
                pool.tensor_copy(u_ext[:, g, PS:PS + w - 1], fix[:, 0:w - 1]).then_inc(d_done, 1)
                pool.wait_ge(d_done, g + 1)
            for j in range(NCH, NCH + KD):
                w_low(j)
            pool.wait_ge(consts_in, 16 * (6 + GROUPS))
            uses = [len(range(s, NT, 2)) for s in range(2)]
            for t in range(NT):
                r = ROWS[t]
                pool.wait_ge(xt_in[t % 2], 16 * (uses[t % 2] + t // 2 + 1))
                pool.tensor_tensor(xt[t % 2][0:r, :], xt[t % 2][0:r, :], bo_bc[0:r, :], ALU.add).then_inc(xb_done, 1)

            pool.sem_inc(low_pool, len(POOL_PIECES))
            for s in range(2):
                pool.wait_ge(hm_out[s], 16 * uses[s])
                pool.wait_ge(x2_out[s], 16 * uses[s])
            pool.memset(xe[0], 0.0)
            pool.memset(xe[1], 0.0)
            pool.wait_ge(hmtr_done, NT)
            pool.memset(ye[0], 0.0)
            step(pool.memset(ye[1], 0.0))
            pool.wait_ge(idx_done, 1)
            pool.tensor_copy(cur[:, 0:2], g_idx[:, 0:2])
            step(pool.tensor_copy(cur[:, 2:4], s_idx[:, 0:1].to_broadcast([P, 2])))

            last_token, last_row = pool.to_reg(T - 1), pool.to_reg(2 * T - 1)

            def gather(b):
                pool.indirect_dma_start(out=xe[b], out_offset=None, in_=hm_dram,
                                        in_offset=bass.IndirectOffsetOnAxis(ap=cur[:, b:b + 1], axis=0),
                                        bounds_check=last_token, oob_is_err=False).then_inc(gath[b], 16)

            def scatter(b):
                pool.indirect_dma_start(out=y2_dram,
                                        out_offset=bass.IndirectOffsetOnAxis(ap=cur[:, 2 + b:3 + b], axis=0),
                                        in_=ye[b], in_offset=None,
                                        bounds_check=last_row, oob_is_err=False).then_inc(scat[b], 16)

            gather(0)
            gather(1)
            for b in range(2):
                scatter(b)
            n_pairs = load_pairs(pool)

            def low(j, n):
                pool.wait_ge(high_done, NP * (j + 1) + n + 1)
                pool.tensor_tensor(we_l[n % 4], raw[n % 6], we_h[n % 4].bitcast(F32), ALU.subtract).then_inc(low_pool, 1)

            def next_rows(j, b):
                pool.wait_ge(xe_tr, 2 * j + 3 + b)
                pool.wait_ge(idx_done, 1)
                pool.tensor_copy(cur[:, b:b + 1], g_idx[:, bass.ds(2 * j + 2 + b, 1)]).then_inc(cur_done, 1)
                pool.wait_ge(cur_done, 4 * j + (1, 3)[b])
                pool.sem_inc(cur_seen, 1)
                gather(b)

            def store_rows(j, b, last=False):
                pool.wait_ge(ye_done, 2 * j + (4, 3)[b])
                pool.wait_ge(scat[b], 16 * (j + 1))
                pool.wait_ge(idx_done, 1)
                pool.tensor_copy(cur[:, 2 + b:3 + b], s_idx[:, bass.ds(2 * j + (1, 0)[b], 1)]).then_inc(cur_done, 1)
                pool.wait_ge(cur_done, 4 * j + (1 if last else (4, 2)[b]))
                pool.sem_inc(cur_seen, 1)
                scatter(b)

            def body(j, overflow):
                next_rows(j, 0)
                store_rows(j, 1)
                next_rows(j, 1)
                low(j, 5)
                low(j, 11)
                store_rows(j, 0)

            pair_loop(pool, body, n_pairs)
            store_rows(n_pairs, 1, last=True)
            pool.wait_ge(scat[0], 16 * n_pairs + 16)
            pool.wait_ge(scat[1], 16 * n_pairs + 32)
            for b in (0, 1):
                pool.wait_ge(gath[b], 16 * n_pairs + 16)
            pool.sem_inc(sc_all, 1)


_INS = ["x_prompt", "x_sample", "state_pool", "state_conv", "norm1_g", "w_in", "pool_lin", "pool_scale", "conv_dw",
        "conv_dw_b", "conv_ln_g", "conv_ln_b", "w_out", "b_out", "norm2_g", "w_rg", "b_rg", "w_re", "b_re", "w_eg",
        "w_eu", "w_ed", "norm_f_g"]


def kernel(**inputs):
    import numpy as np
    import concourse.bacc as bacc
    from concourse.bass_utils import run_bass_kernel_spmd

    nc = bacc.Bacc("TRN2", target_bir_lowering=False, num_devices=1)
    arrays, args = {}, []
    for name in _INS:
        a = np.ascontiguousarray(inputs[name])
        arrays[f"in_{name}"] = a
        args.append(nc.dram_tensor(f"in_{name}", a.shape, mybir.dt.from_np(a.dtype), kind="ExternalInput").ap())
    sp, sc = inputs["state_pool"].shape, inputs["state_conv"].shape
    batch = inputs["x_prompt"].shape[0]
    shapes = [inputs["x_prompt"].shape, inputs["x_sample"].shape, (sp[0], batch) + tuple(sp[2:]),
              (sc[0], batch) + tuple(sc[2:]), sp, sc]
    outs = [nc.dram_tensor(f"out_{i}", list(s), F32, kind="ExternalOutput").ap() for i, s in enumerate(shapes)]
    trunk_kernel(nc, *args, *outs)
    r = run_bass_kernel_spmd(nc, [arrays], core_ids=[0])
    return tuple(r.results[0][f"out_{i}"] for i in range(len(shapes)))
```

```python
from contextlib import ExitStack

import concourse.bass as bass
from concourse import mybir

F32 = mybir.dt.float32
F32R = mybir.dt.float32r
I32 = mybir.dt.int32
U32 = mybir.dt.uint32
ALU = mybir.AluOpType
ACT = mybir.ActivationFunctionType
AX_X = mybir.AxisListType.X

P = 128
BANK = 512
EPS = 1e-6
FAR = float(1 << 20)
LOWEST = -3.0e38


def trunk_kernel(nc, x_prompt, x_sample, state_pool, state_conv, norm1_g, w_in, pool_lin, pool_scale,
                 conv_dw, conv_dw_b, conv_ln_g, conv_ln_b, w_out, b_out, norm2_g, w_rg, b_rg, w_re,
                 b_re, w_eg, w_eu, w_ed, norm_f_g,
                 y_prompt, y_sample, pool_state_prompt, conv_state_prompt, pool_state_sample,
                 conv_state_sample):
    SEQ, D = x_prompt.shape[1], x_prompt.shape[2]
    DEC = x_sample.shape[1]
    KD = D // P
    PS, DPOOL = state_pool.shape[2], state_pool.shape[3]
    CS, DCONV = state_conv.shape[2], state_conv.shape[3]
    TAPS = CS + 1
    NG = pool_lin.shape[1]
    NC = DCONV // P
    GROUPS, PER = w_re.shape[1], w_re.shape[3]
    E = GROUPS * PER
    FF = w_eg.shape[3]
    KF = FF // P
    T = SEQ + DEC
    NT = -(-T // P)
    ROWS = [min(P, T - t * P) for t in range(NT)]
    BLOCKS = [(0, BANK), (BANK, BANK), (SEQ, DEC)]
    OVERFLOW = (2 * T - 1) // P
    NBLK = E + OVERFLOW
    LB = GROUPS + E
    assert SEQ == 2 * BANK and NG == NC == 4 and KD == 8 and KF == 4 and PER == 8 and NBLK % 2 == 0
    VW = CS + SEQ + CS + DEC
    HW_ = VW - CS
    UW = PS + SEQ + PS + DEC
    PAIRS = E // 2
    MAX_PAIRS = NBLK // 2

    ctx = ExitStack()
    with ctx:
        def sb(name, shape, dt=F32):
            return ctx.enter_context(nc.sbuf_tensor(name, shape, dt))

        def sem(name):
            return ctx.enter_context(nc.semaphore(name))

        hm_dram = nc.dram_tensor("hm_scratch", [T, D], F32).ap()
        x2_dram = nc.dram_tensor("x2_scratch", [T, D], F32).ap()
        y2_dram = nc.dram_tensor("y2_scratch", [2 * T, D], F32).ap()

        big = sb("big", [P, 2 * KD * T], F32R)
        ring = sb("ring", [P, 4 * D], F32R)
        hTr = sb("hTr", [P, 2 * FF], F32R)
        xT_h = big[:, 0:KD * T].rearrange("p (k t) -> p k t", k=KD)
        xT_l = big[:, KD * T:2 * KD * T].rearrange("p (k t) -> p k t", k=KD)
        wo_h = big[:, 0:KD * D].rearrange("p (k n) -> p k n", k=KD)
        wo_l = big[:, KD * D:2 * KD * D].rearrange("p (k n) -> p k n", k=KD)
        HP = 2048
        we_h = [big[:, s * 2 * HP:s * 2 * HP + HP] for s in range(4)]
        we_l = [big[:, s * 2 * HP + HP:(s + 1) * 2 * HP] for s in range(4)]
        part_h = [ring[:, s * 2 * D:s * 2 * D + D].rearrange("p (k n) -> p k n", k=KD) for s in range(2)]
        part_l = [ring[:, s * 2 * D + D:(s + 1) * 2 * D].rearrange("p (k n) -> p k n", k=KD) for s in range(2)]
        hT_h = hTr[:, 0:FF].rearrange("p (k n) -> p k n", k=KF)
        hT_l = hTr[:, FF:2 * FF].rearrange("p (k n) -> p k n", k=KF)

        SZ_V, SZ_U, SZ_H = NC * VW, NG * UW, NC * HW_
        SZ_S1, SZ_S2, SZ_X, SZ_W, SZ_T = 2 * UW, 2112, 2 * D, 3 * D, D
        arena = sb("arena", [P, SZ_V + SZ_U + SZ_H + SZ_S1 + SZ_S2 + SZ_X + SZ_W + SZ_T])
        at = [0]

        def region(size):
            at[0] += size
            return arena[:, at[0] - size:at[0]]

        r_v, r_u, r_h = region(SZ_V), region(SZ_U), region(SZ_H)
        r_s1, r_s2, r_x, r_w, r_t = region(SZ_S1), region(SZ_S2), region(SZ_X), region(SZ_W), region(SZ_T)
        v_ext = r_v.rearrange("p (c t) -> p c t", c=NC)
        u_ext = r_u.rearrange("p (g t) -> p g t", g=NG)
        hc = r_h.rearrange("p (c t) -> p c t", c=NC)
        win = [r_s1[:, 0:UW], r_s1[:, UW:2 * UW]]
        ln_sd = r_s1[:, 0:T]
        hm = [r_s1[:, 0:D], r_s1[:, D:2 * D]]
        junk = r_s2[:, 0:D]
        sg = r_s2[:, D:D + T]
        sq = r_s2[:, 0:NC * BANK].rearrange("p (c t) -> p c t", c=NC)
        states = r_s2[:, 0:4 * BANK].rearrange("p (s n) -> p s n", s=4)
        Mx = r_s2[:, D:D + 2 * NT * E].rearrange("p (s e) -> p s e", e=E)
        MS = sb("MS", [P, NT, E])
        prod_t = r_s2[:, D + 2 * NT * E:D + 2 * NT * E + 2 * E].rearrange("p (k e) -> p k e", e=E)
        prod = r_s2[:, 0:2 * NT * E].rearrange("p (s e) -> p s e", e=E)
        assert 2 * T < 4096 and NT == KD + 1 and 2 * KD * (T - D) >= KD * P and SEQ == KD * P
        hots = ([big[:, 2 * KD * D + i * P:2 * KD * D + (i + 1) * P] for i in range(KD)] +
                [hTr[:, i * P:(i + 1) * P] for i in range(KD)] +
                [ring[:, 3 * D + i * P:3 * D + (i + 1) * P] for i in range(2 * NT - 2 * KD)])
        hot_b = ring[:, 2 * D:2 * D + 2 * NT * NBLK].rearrange("p (s b) -> p s b", b=NBLK)
        xt = [r_x[:, 0:D], r_x[:, D:2 * D]]
        xa = (xt + [r_h[:, i * D:(i + 1) * D] for i in range(4)] + [r_u[:, i * D:(i + 1) * D] for i in range(4)])[:NT]
        w_raw = [r_w[:, s * D:(s + 1) * D] for s in range(3)]
        g1_bc = r_t
        hmT = r_t.rearrange("p (k n) -> p k n", k=KD)
        raw = [arena[:, s * HP:(s + 1) * HP] for s in range(6)]
        xe = xt
        ye = [r_s1[:, 0:D], r_s1[:, D:2 * D]]
        act_t = [r_t[:, 0:FF], r_t[:, FF:2 * FF]]
        hid = [r_s2[:, 0:FF], r_s2[:, FF:2 * FF]]
        FB = 7
        x_in = [arena[:, s * D:(s + 1) * D] for s in range(FB)]
        y_in = [arena[:, FB * D + s * 2 * D:FB * D + (s + 1) * 2 * D] for s in range(FB)]
        gf_bc = arena[:, 3 * FB * D:(3 * FB + 1) * D]
        junk_f = arena[:, (3 * FB + 1) * D:(3 * FB + 2) * D]

        ident = sb("ident", [P, P])
        tri = sb("tri", [P, P])
        ones = sb("ones", [P, P])
        mean_w = sb("mean_w", [P, P])
        iota_i = r_s1[:, BANK:BANK + P].bitcast(I32)
        iota = sb("iota", [P, P])
        grp = sb("grp", [P, E])
        tok_i = r_s1[:, BANK + P:BANK + P + 2 * NT].bitcast(I32)
        tokv = sb("tokv", [P, 2 * NT])
        inv_cnt = sb("inv_cnt", [P, PS])
        eps = sb("eps", [P, 1])
        NROW = TAPS + 4 + PS + CS
        rows = r_s1[0:NROW, 0:BANK]
        cols = sb("cols", [P, NC, NROW])
        R_B, R_LG, R_LB, R_SC = TAPS, TAPS + 1, TAPS + 2, TAPS + 3
        R_SP, R_SV = TAPS + 4, TAPS + 4 + PS
        plin = sb("plin", [P, NG, P])
        w_rt = sb("w_rt", [P, KD, LB])
        b_rt = sb("b_rt", [P, LB])
        g2_bc = sb("g2_bc", [P, D])
        bo_bc = sb("bo_bc", [P, D])
        stat = sb("stat", [P, 6, NT])
        fix = sb("fix", [P, PS])
        lgt = sb("lgt", [P, 8 + E])
        top = sb("top", [P, 2, 8])
        topi = sb("topi", [P, 2, 8], U32)
        gsel = sb("gsel", [P, 1])
        pen = sb("pen", [P, E])
        le = sb("le", [P, E])
        eid = sb("eid", [P, NT, 2])
        gdif = sb("gdif", [P, NT, GROUPS])
        edif = sb("edif", [P, NT])
        gates = sb("gates", [P, 2, NT])
        gtmp = sb("gtmp", [P, 2, NT])
        pref = sb("pref", [P, NT + 1, E])
        rk_n = sb("rk_n", [P, E])
        cum = [sb("cum0", [P, 16 + E]), sb("cum1", [P, 16 + E])]
        nb = sb("nb", [P, E])
        base = sb("base", [P, E])
        sl = sb("sl", [P, 6, 2 * NT])
        sl_i = sb("sl_i", [P, 3, 2 * NT], I32)
        cmp_ = sb("cmp_", [1, OVERFLOW, E])
        eob_f = sb("eob_f", [1, OVERFLOW + 2])
        eob = sb("eob", [1, OVERFLOW + 2], I32)
        idx_f = sb("idx_f", [P, 2, NBLK])
        s_idx = sb("s_idx", [P, 1 + NBLK], U32)
        g_idx = sb("g_idx", [P, NBLK + 2], U32)
        cur = sb("cur", [P, 4], U32)
        warm = sb("warm", [P, 1])

        ps = ctx.enter_context(nc.psum_tensor("ps", [P, 8 * BANK], F32))

        def banks(a, n):
            return ps[:, a * BANK:(a + n) * BANK]

        z_ps = [banks(0, 3), banks(3, 3)]
        x_ps = banks(6, 2).rearrange("p (k n) -> p k n", k=KD)
        xa_ps = [x_ps, banks(4, 2).rearrange("p (k n) -> p k n", k=KD)]
        cols_ps = banks(3, 1)[:, 0:NC * NROW].rearrange("p (c r) -> p c r", c=NC)
        st_ps = [banks(6, 1), banks(7, 1)]
        mean_ps = [banks(0, 1), banks(1, 1), banks(2, 1)]
        var_ps = [banks(3, 1), banks(4, 1), banks(5, 1)]
        out_ps = [banks(2, 2), banks(4, 2)]
        lg_ps = banks(0, 1)[:, 0:LB]
        rk_ps = banks(1, 1)[:, 0:(NT + 1) * E].rearrange("p (t e) -> p t e", e=E)
        ix_ps = banks(0, 1)[:, 0:NBLK]
        xe_ps = banks(0, 2).rearrange("p (k n) -> p k n", k=KD)
        gate_ps, up_ps = banks(2, 1), banks(3, 1)
        h_ps = banks(4, 1).rearrange("p (k n) -> p k n", k=KF)
        ye_ps = banks(5, 2)

        const_done = sem("const_done")
        rows_in, g1_in, consts_in, rows_tr, cols_done = map(sem, ("rows_in", "g1_in", "consts_in", "rows_tr", "cols_done"))
        xt_in = [sem("xt_in0"), sem("xt_in1")]
        xa_in = [sem(f"xa_in{t}") for t in range(NT)]
        w_in_s = [sem(f"w_raw_in{s}") for s in range(3)]
        sum1_done, sd1_done, rs1_done, xs_done, xtr_done, xh_done, xl_done = map(sem, (
            "sum1_done", "sd1_done", "rs1_done", "xs_done", "xtr_done", "xh_done", "xl_done"))
        wh_done, wl_done, z_done, sg_done, v_done, u_done, pad_done = map(sem, (
            "wh_done", "wl_done", "z_done", "sg_done", "v_done", "u_done", "pad_done"))
        conv_step, conv_done, st_tr, st_done, st_out, win_step, d_done, pl_done, yp_done = map(sem, (
            "conv_step", "conv_done", "st_tr", "st_done", "st_out", "win_step", "d_done", "pl_done", "yp_done"))
        mean_done, cen_done, sq_done, var_done, lnsd_done, lnrs_done, nrm_done, mix_done = map(sem, (
            "mean_done", "cen_done", "sq_done", "var_done", "lnsd_done", "lnrs_done", "nrm_done", "mix_done"))
        mh_done, ml_done, out_done, xb_done, x2_done, sum2_done, sd2_done, rs2_done, hm_done = map(sem, (
            "mh_done", "ml_done", "out_done", "xb_done", "x2_done", "sum2_done", "sd2_done", "rs2_done", "hm_done"))
        x2_out = [sem("x2_out0"), sem("x2_out1")]
        hm_out = [sem("hm_out0"), sem("hm_out1")]
        hmtr_done, hmT_done, lg_done, lg_read, rt_step, rt_done, exp_done = map(sem, (
            "hmtr_done", "hmT_done", "lg_done", "lg_read", "rt_step", "rt_done", "exp_done"))
        counted, rk_done, hot_done, ix_done, plan_done, idx_done = map(sem, (
            "counted", "rk_done", "hot_done", "ix_done", "plan_done", "idx_done"))
        raw_in = [sem(f"raw_in{s}") for s in range(6)]
        high_done, low_dve, low_pool, piece_used = map(sem, ("high_done", "low_dve", "low_pool", "piece_used"))
        gath = [sem("gath0"), sem("gath1")]
        scat = [sem("scat0"), sem("scat1")]
        xe_tr, xe_high, xe_low, silu_done, act_done, h_tr, h_high, h_low, ye_done, cur_done, zero_done = map(sem, (
            "xe_tr", "xe_high", "xe_low", "silu_done", "act_done", "h_tr", "h_high", "h_low", "ye_done", "cur_done",
            "zero_done"))
        f_x = [sem(f"f_x{s}") for s in range(FB)]
        f_in = [sem(f"f_in{s}") for s in range(FB)]
        gf_in, f_acc, f_sum, f_sd, f_rs, f_y = map(sem, ("gf_in", "f_acc", "f_sum", "f_sd", "f_rs", "f_y"))
        f_out = [sem(f"f_out{s}") for s in range(FB)]
        sc_all, cur_seen, placed = sem("scattered"), sem("cur_seen"), sem("placed")

        def x_rows(t):
            return x_prompt[0, t * P:(t + 1) * P, :] if t * P < SEQ else x_sample[0, :, :]

        CHUNKS = [DPOOL + off + c * P for c in range(NC) for off in (DCONV, 0)] + [g * P for g in range(NG)]
        NCH = len(CHUNKS)
        def hc_at(tok):
            return tok if tok < SEQ else tok + CS

        PIECES = [(0, "g", 0), (0, "g", 1), (0, "u", 0), (0, "u", 1), (1, "g", 0), (1, "g", 1),
                  (0, "d", 0), (0, "d", 1), (1, "u", 0), (1, "u", 1), (1, "d", 0), (1, "d", 1)]
        NP = len(PIECES)
        POOL_PIECES = (5, 11)

        def low_count(n):
            mine = [m for m in range(NP) if (m in POOL_PIECES) == (n in POOL_PIECES)]
            return (low_pool if n in POOL_PIECES else low_dve), len(mine), mine.index(n) + 1

        def wait_low(eng, j, n):
            s, per, k = low_count(n % NP)
            eng.wait_ge(s, j * per + (per if n >= 0 else 0) + k)

        def pair_loop(eng, body):
            with eng.Fori(0, PAIRS) as j:
                body(j, False)
            eng.wait_ge(plan_done, 1)
            n_pairs = eng.value_load(eob[0:1, OVERFLOW:OVERFLOW + 1], min_val=PAIRS, max_val=MAX_PAIRS)
            with eng.Fori(PAIRS, MAX_PAIRS) as j:
                with eng.If(n_pairs > j):
                    body(j, True)
                eng.nop()
            return n_pairs

        block = ctx.enter_context(nc.Block())

        @block.sync
        def _(sp):
            def load_x(t):
                sp.dma_start(xa[t][0:ROWS[t], :], x_rows(t)).then_inc(xa_in[t], 16)

            load_x(0)
            sp.dma_start(g1_bc, norm1_g[0].partition_broadcast(P)).then_inc(g1_in, 16)
            load_x(1)
            load_x(2)
            r0 = 0
            for src in (conv_dw[0], conv_dw_b, conv_ln_g, conv_ln_b, pool_scale, state_pool[0, 0], state_conv[0, 0]):
                n = src.shape[0]
                sp.dma_start(rows[r0:r0 + n, :], src).then_inc(rows_in, 16)
                r0 += n

            def load_w_in(j):
                if j >= 3:
                    sp.wait_ge(wl_done, j - 2)
                src = w_in[0, :, CHUNKS[j]:CHUNKS[j] + P].rearrange("(k p) n -> p k n", p=P)
                sp.dma_start(w_raw[j % 3].rearrange("p (k n) -> p k n", k=KD), src).then_inc(w_in_s[j % 3], 16)

            for t in range(3, NT):
                load_x(t)
                if t % 2 == 0:
                    load_w_in(t // 2 - 2)
            sp.dma_start(plin[:, :, :], pool_lin[0].rearrange("g c d -> c g d")).then_inc(consts_in, 16)
            sp.dma_start(w_rt[:, :, 0:GROUPS], w_rg[0].rearrange("(p k) n -> p k n", p=P)).then_inc(consts_in, 16)
            for g in range(GROUPS):
                at_g = GROUPS + g * PER
                sp.dma_start(w_rt[:, :, at_g:at_g + PER],
                             w_re[0, g].rearrange("(p k) n -> p k n", p=P)).then_inc(consts_in, 16)
            sp.dma_start(b_rt[:, 0:GROUPS], b_rg[0].partition_broadcast(P)).then_inc(consts_in, 16)
            sp.dma_start(b_rt[:, GROUPS:LB],
                         b_re[0].rearrange("g e -> (g e)").partition_broadcast(P)).then_inc(consts_in, 16)
            sp.dma_start(g2_bc[:, :], norm2_g[0].partition_broadcast(P)).then_inc(consts_in, 16)
            sp.dma_start(bo_bc[:, :], b_out[0].partition_broadcast(P)).then_inc(consts_in, 16)
            for j in range(3, NCH):
                load_w_in(j)
            for k in range(KD):
                j = NCH + k
                sp.wait_ge(wl_done, j - 2)
                sp.dma_start(w_raw[j % 3], w_out[0, k * P:(k + 1) * P, :]).then_inc(w_in_s[j % 3], 16)
            dst = (pool_state_prompt[0, 0], pool_state_sample[0, 0], conv_state_prompt[0, 0], conv_state_sample[0, 0])
            for s in range(4):
                sp.wait_ge(st_done, s + 1)
                sp.dma_start(dst[s], states[0:(PS if s < 2 else CS), s, :]).then_inc(st_out, 16)

            def load_residual(t):
                sp.dma_start(xt[t % 2][0:ROWS[t], :], x_rows(t)).then_inc(xt_in[t % 2], 16)

            sp.wait_ge(xtr_done, NT)
            load_residual(0)
            load_residual(1)
            for t in range(NT):
                sp.wait_ge(x2_done, t + 1)
                sp.dma_start(x2_dram[t * P:t * P + ROWS[t], :], xt[t % 2][0:ROWS[t], :]).then_inc(x2_out[t % 2], 16)
                sp.wait_ge(hm_done, t + 1)
                sp.dma_start(hm_dram[t * P:t * P + ROWS[t], :], hm[t % 2][0:ROWS[t], :]).then_inc(hm_out[t % 2], 16)
                if t + 2 < NT:
                    sp.wait_ge(x2_out[t % 2], 16 * (t // 2 + 1))
                    load_residual(t + 2)
            sp.wait_ge(mh_done, NT)
            sp.wait_ge(ml_done, NT)
            sp.wait_ge(st_tr, 4)

            def weights(j, overflow):
                if overflow:
                    e = [sp.value_load(eob[0:1, bass.ds(2 * j + b - E, 1)], min_val=0, max_val=E - 1) for b in (0, 1)]
                else:
                    e = [2 * j, 2 * j + 1]
                for n, (b, m, half) in enumerate(PIECES):
                    w = {"g": w_eg, "u": w_eu, "d": w_ed}[m]
                    src = w[0, bass.ds(e[b], 1), :, :].rearrange("a (p k) n -> p (a k n)", p=P)
                    wait_low(sp, j, n - 6)
                    sp.dma_start(raw[n % 6], src[:, half * HP:(half + 1) * HP]).then_inc(raw_in[n % 6], 16)

            n_pairs = pair_loop(sp, weights)
            wait_low(sp, n_pairs - 1, NP - 2)
            wait_low(sp, n_pairs - 1, NP - 1)
            for s in range(2):
                sp.wait_ge(x2_out[s], 16 * len(range(s, NT, 2)))

            def load_x2(t):
                sp.dma_start(x_in[t % FB][0:ROWS[t], :], x2_dram[t * P:t * P + ROWS[t], :]).then_inc(f_x[t % FB], 16)

            def load_y2(t):
                r = ROWS[t]
                sp.dma_start(y_in[t % FB][0:r, :], y2_dram[2 * t * P:2 * (t * P + r), :]
                             .rearrange("(p k) n -> p (k n)", k=2)).then_inc(f_in[t % FB], 16)

            for t in range(FB):
                load_x2(t)
            sp.wait_ge(sc_all, 1)
            load_y2(0)
            sp.dma_start(gf_bc, norm_f_g.partition_broadcast(P)).then_inc(gf_in, 16)
            for t in range(1, FB):
                load_y2(t)
            for t in range(NT):
                sp.wait_ge(f_y, t + 1)
                dst = y_prompt[0, t * P:(t + 1) * P, :] if t * P < SEQ else y_sample[0, :, :]
                sp.dma_start(dst, x_in[t % FB][0:ROWS[t], :]).then_inc(f_out[t % FB], 16)
                if t + FB < NT:
                    load_y2(t + FB)
                    sp.wait_ge(f_out[t % FB], 16)
                    load_x2(t + FB)
            sp.wait_ge(st_out, 64)
            for s in range(FB):
                sp.wait_ge(f_out[s], 16 * len(range(s, NT, FB)))

        @block.scalar
        def _(act):
            act.sem_inc(high_done, NP)
            act.sem_inc(silu_done, 2)
            act.sem_inc(ye_done, 2)

            def w_high(j):
                act.wait_ge(w_in_s[j % 3], 16 * (j // 3 + 1))
                if j < NCH:
                    if j >= 2:
                        act.wait_ge(z_done, j - 1)
                    out, src = part_h[j % 2], w_raw[j % 3].rearrange("p (k n) -> p k n", k=KD)
                else:
                    act.wait_ge(z_done, NCH)
                    out, src = wo_h[:, j - NCH, :], w_raw[j % 3]
                act.activation(out, src, ACT.Copy).then_inc(wh_done, 1)

            def x_high(t):
                act.wait_ge(xtr_done, t + 1)
                act.activation(xT_h[:, :, t * P:t * P + ROWS[t]], xa_ps[t % 2][:, :, 0:ROWS[t]],
                               ACT.Copy).then_inc(xh_done, 1)

            act.wait_ge(const_done, 1)
            for t in range(NT):
                r = ROWS[t]
                act.wait_ge(xa_in[t], 16)
                if t:
                    act.wait_ge(sum1_done, t)
                act.activation(junk[0:r, :], xa[t][0:r, :], ACT.Square,
                               accum_out=stat[0:r, 0, t:t + 1]).then_inc(sum1_done, 1)
                act.wait_ge(sum1_done, t + 1)
                act.activation(stat[0:r, 1, t:t + 1], stat[0:r, 0, t:t + 1], ACT.Sqrt, bias=eps[0:r, :],
                               scale=1.0 / D).then_inc(sd1_done, 1)
                if t >= 2:
                    x_high(t - 2)
                if t == 3:
                    act.wait_ge(rows_tr, 1)
                    act.activation(cols[:, :, :], cols_ps, ACT.Copy).then_inc(cols_done, 1)
                if t in (4, 6):
                    w_high(t // 2 - 2)
            x_high(NT - 2)
            x_high(NT - 1)
            for c in range(NC):
                act.wait_ge(z_done, 2 * c + 1)
                if c:
                    act.wait_ge(v_done, c)
                act.activation(sg, z_ps[0][:, 0:T], ACT.Sigmoid).then_inc(sg_done, 1)
                w_high(2 * c + 2)
                w_high(2 * c + 3)
            act.wait_ge(pad_done, 1)
            for g in range(NG):
                act.wait_ge(z_done, 2 * NC + g + 1)
                act.activation(u_ext[:, g, PS:PS + SEQ], z_ps[g % 2][:, 0:SEQ], ACT.Copy)
                act.activation(u_ext[:, g, PS + SEQ + PS:UW], z_ps[g % 2][:, SEQ:T], ACT.Copy).then_inc(u_done, 1)
                if g < 2:
                    w_high(2 * NC + 2 + g)
            for s in range(2):
                act.wait_ge(st_tr, s + 1)
                act.activation(states[0:PS, s, :], st_ps[s][0:PS, :], ACT.Copy).then_inc(st_done, 1)
            for s in range(2):
                act.wait_ge(st_tr, s + 3)
                act.activation(states[0:CS, 2 + s, :], st_ps[s][0:CS, :], ACT.Copy).then_inc(st_done, 1)
            for k in range(3):
                w_high(NCH + k)
            for g in range(NG):
                act.wait_ge(pl_done, g + 1)
                act.activation(u_ext[:, g, 0:T], z_ps[g % 2][:, 0:T], ACT.Copy,
                               scale=cols[:, g, R_SC:R_SC + 1]).then_inc(yp_done, 1)
            for k in range(3, KD):
                w_high(NCH + k)
            act.wait_ge(st_out, 64)

            def ln_square(n):
                tok, w = BLOCKS[n]
                act.wait_ge(cen_done, n + 1)
                if n:
                    act.wait_ge(var_done, n)
                act.activation(sq[:, :, 0:w], hc[:, :, hc_at(tok):hc_at(tok) + w], ACT.Square).then_inc(sq_done, 1)

            def ln_deviation(n):
                tok, w = BLOCKS[n]
                act.wait_ge(var_done, n + 1)
                act.activation(ln_sd[:, tok:tok + w], var_ps[n][:, 0:w], ACT.Sqrt, bias=eps[:, :]).then_inc(lnsd_done, 1)

            def ln_swish(n):
                tok, w = BLOCKS[n]
                act.wait_ge(nrm_done, n + 1)
                for c in range(NC):
                    y = hc[:, c, hc_at(tok):hc_at(tok) + w]
                    act.activation(y, y, ACT.Silu, scale=cols[:, c, R_LG:R_LG + 1],
                                   bias=cols[:, c, R_LB:R_LB + 1]).then_inc(mix_done, 1)

            for n in range(3):
                ln_square(n)
                ln_deviation(n)
            for n in range(3):
                ln_swish(n)

            def mix_high(t):
                r, tok = ROWS[t], t * P
                act.wait_ge(mix_done, NC * (min(tok // BANK, 2) + 1))
                if t >= 2:
                    act.wait_ge(out_done, t - 1)
                act.activation(part_h[t % 2][:, 0:NG, 0:r], u_ext[:, :, tok:tok + r], ACT.Copy)
                act.activation(part_h[t % 2][:, NG:KD, 0:r], hc[:, :, hc_at(tok):hc_at(tok) + r],
                               ACT.Copy).then_inc(mh_done, 1)

            def hm_turned(t):
                act.wait_ge(hmtr_done, t + 1)
                if t:
                    act.wait_ge(lg_done, t)
                act.activation(hmT[:, :, 0:ROWS[t]], x_ps[:, :, 0:ROWS[t]], ACT.Copy).then_inc(hmT_done, 1)

            act.wait_ge(yp_done, NG)
            mix_high(0)
            mix_high(1)
            for t in range(NT):
                r = ROWS[t]
                act.wait_ge(x2_done, t + 1)
                if t:
                    act.wait_ge(sum2_done, t)
                else:
                    act.wait_ge(var_done, 3)
                act.activation(junk[0:r, :], xt[t % 2][0:r, :], ACT.Square,
                               accum_out=stat[0:r, 3, t:t + 1]).then_inc(sum2_done, 1)
                act.wait_ge(sum2_done, t + 1)
                act.activation(stat[0:r, 4, t:t + 1], stat[0:r, 3, t:t + 1], ACT.Sqrt, bias=eps[0:r, :],
                               scale=1.0 / D).then_inc(sd2_done, 1)
                if t + 2 < NT:
                    mix_high(t + 2)
                if t >= 1:
                    hm_turned(t - 1)
            hm_turned(NT - 1)
            act.wait_ge(rt_done, NT)
            act.activation(gdif[:, :, :], gdif[:, :, :], ACT.Exp).then_inc(exp_done, 1)
            act.activation(edif[:, :], edif[:, :], ACT.Exp).then_inc(exp_done, 1)

            def high(j, n):
                act.wait_ge(raw_in[n % 6], 32 * j + 16 * (n // 6 + 1))
                act.wait_ge(piece_used, NP * j + n + 1 + (NP - 4))
                act.activation(we_h[n % 4], raw[n % 6], ACT.Copy).then_inc(high_done, 1)

            def rows_high(j, b):
                act.wait_ge(xe_tr, 2 * j + 1 + b)
                act.activation(part_h[b], xe_ps, ACT.Copy).then_inc(xe_high, 1)

            def silu(j, b):
                act.wait_ge(piece_used, NP * (j + 1) + (2, 6)[b])
                act.wait_ge(h_tr, 2 * j + 1 + b)
                act.activation(act_t[b], gate_ps, ACT.Silu).then_inc(silu_done, 1)

            def result(j, b):
                act.wait_ge(piece_used, NP * j + (NP + 8, NP)[b])
                act.wait_ge(scat[b], 16 * (j + 1))
                act.activation(ye[b], ye_ps, ACT.Copy).then_inc(ye_done, 1)

            def body(j, overflow):
                act.activation(warm[:, :], eps[:, :], ACT.Silu)
                high(j, 0)
                high(j, 1)
                rows_high(j, 0)
                high(j, 2)
                result(j, 1)
                for n in (3, 4, 5):
                    high(j, n)
                silu(j, 0)
                rows_high(j, 1)
                for n in (6, 7, 8, 9):
                    high(j, n)
                silu(j, 1)
                high(j, 10)
                high(j, 11)
                result(j, 0)

            n_pairs = pair_loop(act, body)
            result(n_pairs, 1)
            for t in range(NT):
                r = ROWS[t]
                act.wait_ge(f_acc, 2 * t + 2)
                if t:
                    act.wait_ge(f_sum, t)
                act.activation(junk_f[0:r, :], x_in[t % FB][0:r, :], ACT.Square,
                               accum_out=stat[0:r, 0, t:t + 1]).then_inc(f_sum, 1)
                act.wait_ge(f_sum, t + 1)
                act.activation(stat[0:r, 1, t:t + 1], stat[0:r, 0, t:t + 1], ACT.Sqrt, bias=eps[0:r, :],
                               scale=1.0 / D).then_inc(f_sd, 1)

        @block.tensor
        def _(pe):
            def product(out, parts, last):
                for i, (sh, sl_, mh, ml) in enumerate(parts):
                    pe.matmul(out, sh, mh, start=(i == 0), stop=False)
                    pe.matmul(out, sh, ml, start=False, stop=False)
                    ins = pe.matmul(out, sl_, mh, start=False, stop=(i == len(parts) - 1 and last))
                return ins

            pe.wait_ge(const_done, 1)

            def turn_x(t):
                r = ROWS[t]
                pe.wait_ge(xs_done, t + 1)
                if t >= 2:
                    pe.wait_ge(xl_done, t - 1)
                for k in range(KD):
                    ins = pe.transpose(xa_ps[t % 2][:, k, 0:r], xa[t][0:r, k * P:(k + 1) * P], ident[0:r, 0:r])
                ins.then_inc(xtr_done, 1)

            def in_proj(j, n):
                tok, w = BLOCKS[n]
                ins = product(z_ps[j % 2][:, tok:tok + w],
                              [(part_h[j % 2][:, k, :], part_l[j % 2][:, k, :], xT_h[:, k, tok:tok + w],
                                xT_l[:, k, tok:tok + w]) for k in range(KD)], True)
                if n == 2:
                    ins.then_inc(z_done, 1)

            per_block = BANK // P
            for t in range(NT):
                turn_x(t)
                if t == 1:
                    pe.wait_ge(rows_in, 16 * 7)
                    for c in range(NC):
                        ins = pe.transpose(cols_ps[:, c, :], rows[:, c * P:(c + 1) * P], ident[0:NROW, 0:NROW])
                    ins.then_inc(rows_tr, 1)
                if t == per_block + 1:
                    pe.wait_ge(wl_done, 1)
                    pe.wait_ge(xl_done, per_block)
                    in_proj(0, 0)
            for n in (1, 2):
                pe.wait_ge(xl_done, min((n + 1) * per_block, NT))
                in_proj(0, n)
            pe.wait_ge(cols_done, 1)
            for j in range(1, NCH):
                pe.wait_ge(wl_done, j + 1)
                if j >= 2 * NC + 2:
                    pe.wait_ge(u_done, j - 2 * NC - 1)
                elif j >= 2:
                    pe.wait_ge((sg_done, v_done)[j % 2], (j - 2) // 2 + 1)
                for n in range(3):
                    in_proj(j, n)

            def turn_state(s):
                src, n = (u_ext, PS) if s < 2 else (v_ext, CS)
                end = n + SEQ if s % 2 == 0 else n + SEQ + n + DEC
                for c in range(NC):
                    ins = pe.transpose(st_ps[s % 2][0:n, c * P:(c + 1) * P], src[:, c, end - n:end], ident[:, :])
                ins.then_inc(st_tr, 1)

            pe.wait_ge(u_done, NG)
            turn_state(0)
            turn_state(1)
            for s in (2, 3):
                pe.wait_ge(st_done, s - 1)
                turn_state(s)
            pe.wait_ge(consts_in, 16 * (6 + GROUPS))
            for g in range(NG):
                pe.wait_ge(d_done, g + 1)
                if g >= 2:
                    pe.wait_ge(yp_done, g - 1)
                else:
                    pe.wait_ge(u_done, g + 3)
                for n, (tok, w) in enumerate(BLOCKS):
                    off = PS + tok if tok < SEQ else PS + tok + PS
                    ins = pe.matmul(z_ps[g % 2][:, tok:tok + w], plin[:, g, :], u_ext[:, g, off:off + w],
                                    start=True, stop=True)
                ins.then_inc(pl_done, 1)
            pe.wait_ge(yp_done, NG)
            for n, (tok, w) in enumerate(BLOCKS):
                pe.wait_ge(conv_done, NC)
                for c in range(NC):
                    ins = pe.matmul(mean_ps[n][:, 0:w], mean_w[:, :], hc[:, c, hc_at(tok):hc_at(tok) + w],
                                    start=(c == 0), stop=(c == NC - 1))
                ins.then_inc(mean_done, 1)
            for n, (tok, w) in enumerate(BLOCKS):
                pe.wait_ge(sq_done, n + 1)
                for c in range(NC):
                    ins = pe.matmul(var_ps[n][:, 0:w], mean_w[:, :], sq[:, c, 0:w], start=(c == 0), stop=(c == NC - 1))
                ins.then_inc(var_done, 1)

            def out_proj(t):
                r = ROWS[t]
                pe.wait_ge(ml_done, t + 1)
                if t == 0:
                    pe.wait_ge(wl_done, NCH + KD)
                    pe.wait_ge(cen_done, 3)
                    pe.wait_ge(lnsd_done, 3)
                if t >= 2:
                    pe.wait_ge(x2_done, t - 1)
                for half in range(2):
                    c0 = half * BANK
                    ins = product(out_ps[t % 2][0:r, c0:c0 + BANK],
                                  [(part_h[t % 2][:, k, 0:r], part_l[t % 2][:, k, 0:r], wo_h[:, k, c0:c0 + BANK],
                                    wo_l[:, k, c0:c0 + BANK]) for k in range(KD)], True)
                ins.then_inc(out_done, 1)

            def turn_hm(t):
                r = ROWS[t]
                pe.wait_ge(hm_done, t + 1)
                if t:
                    pe.wait_ge(hmT_done, t)
                for k in range(KD):
                    ins = pe.transpose(x_ps[:, k, 0:r], hm[t % 2][0:r, k * P:(k + 1) * P], ident[0:r, 0:r])
                ins.then_inc(hmtr_done, 1)

            def logits(t):
                r = ROWS[t]
                pe.wait_ge(hmT_done, t + 1)
                if t:
                    pe.wait_ge(lg_read, t)
                for k in range(KD):
                    ins = pe.matmul(lg_ps[0:r, :], hmT[:, k, 0:r], w_rt[:, k, :], start=(k == 0), stop=(k == KD - 1))
                ins.then_inc(lg_done, 1)

            def ranks(t):
                pe.wait_ge(counted, t + 1)
                if t:
                    pe.wait_ge(placed, t)
                else:
                    pe.wait_ge(const_done, 1)
                pe.matmul(rk_ps[:, t, :], tri[:, :], MS[:, t, :], start=True, stop=False)
                ins = pe.matmul(rk_ps[:, t, :], ones[:, :], pref[:, t, :], start=False, stop=True)
                if t == NT - 1:
                    ins = pe.matmul(rk_ps[:, NT, :], ones[:, :], pref[:, NT, :], start=True, stop=True)
                ins.then_inc(rk_done, 1)

            for t in range(NT + 3):
                if t < NT:
                    out_proj(t)
                elif t == NT:
                    pe.sem_inc(piece_used, NP)
                if 1 <= t <= NT:
                    turn_hm(t - 1)
                if 2 <= t < NT + 2:
                    logits(t - 2)
                if t >= 3:
                    ranks(t - 3)
            pe.wait_ge(hot_done, 1)
            for s in range(2 * NT):
                ins = pe.matmul(ix_ps, hots[s], hot_b[:, s, :], start=(s == 0), stop=(s == 2 * NT - 1))
            ins.then_inc(ix_done, 1)

            pe.sem_inc(h_tr, 2)
            pe.wait_ge(idx_done, 1)

            def turn_rows(j, b, first=False):
                pe.wait_ge(gath[b], 16 * (j + 1))
                if not first:
                    pe.wait_ge(xe_low, 2 * j + b)
                for k in range(KD):
                    ins = pe.transpose(xe_ps[:, k, :], xe[b][:, k * P:(k + 1) * P], ident[:, :])
                ins.then_inc(xe_tr, 1)

            def expert_in(j, n, out):
                b, _, half = PIECES[n]
                wait_low(pe, j, n)
                wh = we_h[n % 4].rearrange("p (k n) -> p k n", n=FF)
                wl = we_l[n % 4].rearrange("p (k n) -> p k n", n=FF)
                for i in range(4):
                    k = half * 4 + i
                    pe.matmul(out, part_h[b][:, k, :], wh[:, i, :], start=(k == 0), stop=False)
                    pe.matmul(out, part_h[b][:, k, :], wl[:, i, :], start=False, stop=False)
                    ins = pe.matmul(out, part_l[b][:, k, :], wh[:, i, :], start=False, stop=(k == KD - 1))
                ins.then_inc(piece_used, 1)

            def expert_out(j, n):
                b, _, half = PIECES[n]
                wait_low(pe, j, n)
                wh = we_h[n % 4].rearrange("p (k n) -> p k n", n=D)
                wl = we_l[n % 4].rearrange("p (k n) -> p k n", n=D)
                for i in range(2):
                    k = half * 2 + i
                    for c0 in (0, BANK):
                        out = ye_ps[:, c0:c0 + BANK]
                        pe.matmul(out, hT_h[:, k, :], wh[:, i, c0:c0 + BANK], start=(k == 0), stop=False)
                        pe.matmul(out, hT_h[:, k, :], wl[:, i, c0:c0 + BANK], start=False, stop=False)
                        ins = pe.matmul(out, hT_l[:, k, :], wh[:, i, c0:c0 + BANK], start=False, stop=(k == KF - 1))
                ins.then_inc(piece_used, 1)

            def turn_hidden(j, b):
                pe.wait_ge(act_done, 2 * j + 3 + b)
                pe.wait_ge(h_low, 2 * j + 2 + b)
                for k in range(KF):
                    ins = pe.transpose(h_ps[:, k, :], hid[b][:, k * P:(k + 1) * P], ident[:, :])
                ins.then_inc(h_tr, 1)

            turn_rows(0, 0, first=True)

            def body(j, overflow):
                pe.wait_ge(xe_low, 2 * j + 1)
                pe.wait_ge(silu_done, 2 * j + 2)
                expert_in(j, 0, gate_ps)
                expert_in(j, 1, gate_ps)
                turn_rows(j, 1)
                pe.wait_ge(act_done, 2 * j + 2)
                expert_in(j, 2, up_ps)
                expert_in(j, 3, up_ps)
                pe.wait_ge(xe_low, 2 * j + 2)
                pe.wait_ge(silu_done, 2 * j + 3)
                expert_in(j, 4, gate_ps)
                expert_in(j, 5, gate_ps)
                turn_hidden(j, 0)
                pe.wait_ge(h_low, 2 * j + 3)
                pe.wait_ge(ye_done, 2 * j + 2)
                expert_out(j, 6)
                expert_out(j, 7)
                pe.wait_ge(act_done, 2 * j + 3)
                expert_in(j, 8, up_ps)
                expert_in(j, 9, up_ps)
                turn_rows(j + 1, 0)
                turn_hidden(j, 1)
                pe.wait_ge(h_low, 2 * j + 4)
                pe.wait_ge(ye_done, 2 * j + 4)
                expert_out(j, 10)
                expert_out(j, 11)

            n_pairs = pair_loop(pe, body)

        @block.vector
        def _(dve):
            n_dve = NP - len(POOL_PIECES)
            dve.sem_inc(low_dve, n_dve)
            dve.sem_inc(act_done, 2)
            dve.sem_inc(h_low, 2)
            dve.wait_ge(g1_in, 16)

            def x_scaled(t):
                r = ROWS[t]
                dve.wait_ge(sd1_done, t + 1)
                dve.reciprocal(stat[0:r, 2, t:t + 1], stat[0:r, 1, t:t + 1]).then_inc(rs1_done, 1)
                dve.wait_ge(rs1_done, t + 1)
                dve.scalar_tensor_tensor(xa[t][0:r, :], xa[t][0:r, :], stat[0:r, 2, t:t + 1], g1_bc[0:r, :],
                                         ALU.mult, ALU.mult).then_inc(xs_done, 1)

            def x_low(t):
                r, tok = ROWS[t], t * P
                dve.wait_ge(xh_done, t + 1)
                dve.tensor_tensor(xT_l[:, :, tok:tok + r], xa_ps[t % 2][:, :, 0:r], xT_h[:, :, tok:tok + r].bitcast(F32),
                                  ALU.subtract).then_inc(xl_done, 1)

            for t in range(NT):
                x_scaled(t)
                if t >= 2:
                    x_low(t - 2)
            x_low(NT - 2)
            x_low(NT - 1)

            dve.wait_ge(cols_done, 1)
            half_w = HW_ // 2
            todo = [(c, j, h) for c in range(NC) for j in range(TAPS) for h in range(2)]
            steps = [0]

            def conv_ops(n, upto):
                for _ in range(n):
                    if not todo or todo[0][0] >= upto:
                        return
                    c, j, h = todo.pop(0)
                    a, b = h * half_w, (half_w, HW_)[h]
                    if j:
                        dve.wait_ge(conv_step, steps[0] - 1)
                        dve.scalar_tensor_tensor(hc[:, c, a:b], v_ext[:, c, a + j:b + j], cols[:, c, j:j + 1],
                                                 hc[:, c, a:b], ALU.mult, ALU.add).then_inc(conv_step, 1)
                    else:
                        dve.tensor_scalar(hc[:, c, a:b], v_ext[:, c, a:b], cols[:, c, 0:1],
                                          cols[:, c, R_B:R_B + 1], ALU.mult, ALU.add).then_inc(conv_step, 1)
                    steps[0] += 1

            dve.wait_ge(pad_done, 1)
            for c in range(NC):
                dve.wait_ge(sg_done, c + 1)
                dve.wait_ge(z_done, 2 * c + 2)
                dve.tensor_tensor(v_ext[:, c, CS:CS + SEQ], z_ps[1][:, 0:SEQ], sg[:, 0:SEQ], ALU.mult).then_inc(conv_step, 1)
                dve.tensor_tensor(v_ext[:, c, CS + SEQ + CS:VW], z_ps[1][:, SEQ:T], sg[:, SEQ:T],
                                  ALU.mult).then_inc(v_done, 1)
                steps[0] += 1
                dve.wait_ge(v_done, c + 1)
                conv_ops(32 if c < NC - 1 else len(todo), c + 1)
            dve.wait_ge(conv_step, steps[0])
            dve.engine_nop().then_inc(conv_done, NC)

            for n, (tok, w) in enumerate(BLOCKS):
                y = hc[:, :, hc_at(tok):hc_at(tok) + w]
                dve.wait_ge(mean_done, n + 1)
                dve.tensor_tensor(y, y, mean_ps[n][:, 0:w].unsqueeze(1).to_broadcast([P, NC, w]),
                                  ALU.subtract).then_inc(cen_done, 1)
            for n, (tok, w) in enumerate(BLOCKS):
                y = hc[:, :, hc_at(tok):hc_at(tok) + w]
                rs = ln_sd[:, tok:tok + w]
                dve.wait_ge(lnsd_done, n + 1)
                dve.reciprocal(rs, rs).then_inc(lnrs_done, 1)
                dve.wait_ge(lnrs_done, n + 1)
                dve.wait_ge(cen_done, n + 1)
                dve.tensor_tensor(y, y, rs.unsqueeze(1).to_broadcast([P, NC, w]), ALU.mult).then_inc(nrm_done, 1)

            def mix_low(t):
                r, tok = ROWS[t], t * P
                dve.wait_ge(mh_done, t + 1)
                dve.tensor_tensor(part_l[t % 2][:, 0:NG, 0:r], u_ext[:, :, tok:tok + r],
                                  part_h[t % 2][:, 0:NG, 0:r].bitcast(F32), ALU.subtract)
                dve.tensor_tensor(part_l[t % 2][:, NG:KD, 0:r], hc[:, :, hc_at(tok):hc_at(tok) + r],
                                  part_h[t % 2][:, NG:KD, 0:r].bitcast(F32), ALU.subtract).then_inc(ml_done, 1)

            def residual(t):
                r = ROWS[t]
                dve.wait_ge(out_done, t + 1)
                dve.wait_ge(xb_done, t + 1)
                dve.tensor_tensor(xt[t % 2][0:r, :], out_ps[t % 2][0:r, :], xt[t % 2][0:r, :],
                                  ALU.add).then_inc(x2_done, 1)

            def hm_row(t):
                r = ROWS[t]
                dve.wait_ge(sd2_done, t + 1)
                dve.reciprocal(stat[0:r, 5, t:t + 1], stat[0:r, 4, t:t + 1]).then_inc(rs2_done, 1)
                dve.wait_ge(rs2_done, t + 1)
                if t >= 2:
                    dve.wait_ge(hm_out[t % 2], 16 * (t // 2))
                    dve.wait_ge(hmtr_done, t - 1)
                dve.scalar_tensor_tensor(hm[t % 2][0:r, :].rearrange("p (k q) -> p q k", k=KD),
                                         xt[t % 2][0:r, :].rearrange("p (q k) -> p q k", k=KD), stat[0:r, 5, t:t + 1],
                                         g2_bc[0:r, :].rearrange("p (q k) -> p q k", k=KD),
                                         ALU.mult, ALU.mult).then_inc(hm_done, 1)

            done = [0]

            def step(ins):
                done[0] += 1
                ins.then_inc(rt_step, 1)
                dve.wait_ge(rt_step, done[0])

            def route(t):
                r = ROWS[t]
                dve.wait_ge(lg_done, t + 1)
                dve.tensor_tensor(lgt[0:r, 0:GROUPS], lg_ps[0:r, 0:GROUPS], b_rt[0:r, 0:GROUPS], ALU.add)
                step(dve.tensor_tensor(lgt[0:r, 8:8 + E], lg_ps[0:r, GROUPS:LB], b_rt[0:r, GROUPS:LB], ALU.add))
                dve.engine_nop().then_inc(lg_read, 1)
                step(dve.max(top[0:r, 0, :], lgt[0:r, 0:8]))
                step(dve.max_index(topi[0:r, 0, :], top[0:r, 0, :], lgt[0:r, 0:8]))
                step(dve.tensor_copy(gsel[0:r, :], topi[0:r, 0, 0:1]))
                step(dve.tensor_scalar(pen[0:r, :], grp[0:r, :], gsel[0:r, :], LOWEST, ALU.not_equal, ALU.mult))
                step(dve.tensor_tensor(le[0:r, :], lgt[0:r, 8:8 + E], pen[0:r, :], ALU.add))
                step(dve.max(top[0:r, 1, :], le[0:r, :]))
                step(dve.max_index(topi[0:r, 1, :], top[0:r, 1, :], le[0:r, :]))
                dve.tensor_copy(eid[0:r, t, :], topi[0:r, 1, 0:2])
                dve.tensor_scalar(gdif[0:r, t, :], lgt[0:r, 0:GROUPS], top[0:r, 0, 0:1], None, ALU.subtract)
                step(dve.tensor_scalar(edif[0:r, t:t + 1], top[0:r, 1, 1:2], top[0:r, 1, 0:1], None, ALU.subtract))
                dve.engine_nop().then_inc(rt_done, 1)

            s_r, s_b, s_q, s_o, s_w = (sl[:, i, :] for i in range(5))
            lane = sl[:, 5, :]
            slots_e = eid.rearrange("p t k -> p (t k)")

            def count(t):
                step(dve.tensor_tensor(Mx[:, 2 * t:2 * t + 2, :], iota[:, 0:E].unsqueeze(1).to_broadcast([P, 2, E]),
                                       eid[:, t, :].unsqueeze(2).to_broadcast([P, 2, E]), ALU.is_equal))
                step(dve.tensor_tensor(MS[:, t, :], Mx[:, 2 * t, :], Mx[:, 2 * t + 1, :], ALU.add))
                dve.tensor_tensor(pref[:, t + 1, :], pref[:, t, :], MS[:, t, :], ALU.add).then_inc(counted, 1)
                dve.wait_ge(counted, t + 1)

            def place(t):
                a, b = 2 * t, 2 * t + 2
                dve.wait_ge(rk_done, t + 1)
                if t == NT - 1:
                    step(dve.tensor_copy(rk_n[:, :], rk_ps[:, NT, :]))
                step(dve.tensor_tensor(prod_t, Mx[:, a:b, :], rk_ps[:, t, :].unsqueeze(1).to_broadcast([P, 2, E]),
                                       ALU.mult))
                dve.engine_nop().then_inc(placed, 1)
                step(dve.tensor_reduce(s_r[:, a:b], prod_t, AX_X, ALU.add))
                step(dve.tensor_copy(sl_i[:, 0, a:b], s_r[:, a:b]))
                dve.tensor_scalar(sl_i[:, 1, a:b], sl_i[:, 0, a:b], P - 1, None, ALU.bitwise_and)
                step(dve.tensor_scalar(sl_i[:, 2, a:b], sl_i[:, 0, a:b], 7, None, ALU.arith_shift_right))
                dve.tensor_copy(lane[:, a:b], sl_i[:, 1, a:b])
                step(dve.tensor_copy(s_q[:, a:b], sl_i[:, 2, a:b]))
                dve.tensor_scalar(s_o[:, a:b], s_r[:, a:b], float(P), None, ALU.is_ge)
                dve.tensor_scalar(s_w[:, a:b], slots_e[:, a:b], -1.0, float(E - 1), ALU.mult, ALU.add)
                dve.tensor_tensor(s_q[:, a:b], s_q[:, a:b], slots_e[:, a:b], ALU.add)
                if t == NT - 1:
                    dve.wait_ge(out_done, NT - 1)
                for s in (a, b - 1):
                    ins = dve.tensor_scalar(hots[s], iota[:, :], lane[:, s:s + 1], tokv[:, s:s + 1], ALU.is_equal,
                                            ALU.mult)
                step(ins)

            dve.wait_ge(consts_in, 16 * (6 + GROUPS))
            dve.wait_ge(const_done, 1)
            step(dve.memset(pref[:, 0, :], 0.0))
            step(dve.memset(cum[0][:, :], 0.0))
            step(dve.memset(cum[1][:, :], 0.0))
            step(dve.memset(gdif[:, :, :], 0.0))
            step(dve.memset(edif[:, :], 0.0))
            mix_low(0)
            mix_low(1)
            for t in range(NT + 3):
                if t < NT:
                    residual(t)
                    hm_row(t)
                if t + 2 < NT:
                    mix_low(t + 2)
                if 2 <= t < NT + 2:
                    route(t - 2)
                    count(t - 2)
                if t >= 3:
                    place(t - 3)

            step(dve.tensor_scalar(nb[:, :], rk_n[:, :], float(P), None, ALU.is_gt))
            for m in range(2, -(-T // P)):
                step(dve.scalar_tensor_tensor(nb[:, :], rk_n[:, :], float(m * P), nb[:, :], ALU.is_gt, ALU.add))
            step(dve.tensor_copy(cum[0][:, 16:16 + E], nb[:, :]))
            for i, s in enumerate((1, 2, 4, 8, 16)):
                src, dst = cum[i % 2], cum[(i + 1) % 2]
                step(dve.tensor_tensor(dst[:, 16:16 + E], src[:, 16:16 + E], src[:, 16 - s:16 - s + E], ALU.add))
            ends = cum[1][:, 16:16 + E]
            step(dve.tensor_tensor(base[:, :], ends, nb[:, :], ALU.subtract))
            step(dve.tensor_tensor(prod, Mx, base[:, :].unsqueeze(1).to_broadcast([P, 2 * NT, E]), ALU.mult))
            step(dve.tensor_reduce(s_b, prod, AX_X, ALU.add))
            step(dve.tensor_tensor(s_b, s_b, s_w, ALU.add))
            step(dve.tensor_tensor(s_b, s_b, s_o, ALU.mult))
            step(dve.tensor_tensor(s_b, s_b, s_q, ALU.add))
            dve.tensor_tensor(hot_b, iota[:, 0:NBLK].unsqueeze(1).to_broadcast([P, 2 * NT, NBLK]),
                              s_b.unsqueeze(2).to_broadcast([P, 2 * NT, NBLK]), ALU.is_equal).then_inc(hot_done, 1)
            dve.memset(ye_ps, 0.0)
            dve.wait_ge(ix_done, 1)
            step(dve.tensor_scalar(idx_f[:, 1, :], ix_ps, 0.0, FAR, ALU.is_equal, ALU.mult))
            step(dve.scalar_tensor_tensor(idx_f[:, 0, :], ix_ps, -1.0, idx_f[:, 1, :], ALU.add, ALU.add))
            step(dve.tensor_copy(s_idx[:, 1:1 + NBLK], idx_f[:, 0, :]))
            step(dve.tensor_scalar(g_idx[:, 0:NBLK], s_idx[:, 1:1 + NBLK], 1, None, ALU.logical_shift_right))
            dve.engine_nop().then_inc(idx_done, 1)
            step(dve.tensor_tensor(cmp_[:, :, :], ends[0:1, :].unsqueeze(1).to_broadcast([1, OVERFLOW, E]),
                                   iota[0:1, 0:OVERFLOW].unsqueeze(2).to_broadcast([1, OVERFLOW, E]), ALU.is_le))
            step(dve.tensor_reduce(eob_f[:, 0:OVERFLOW], cmp_[:, :, :], AX_X, ALU.add))
            step(dve.tensor_scalar(eob_f[:, 0:OVERFLOW], eob_f[:, 0:OVERFLOW], float(E - 1), None, ALU.min))
            evens = iota[0:1, 0:OVERFLOW:2]
            step(dve.tensor_scalar(cmp_[:, 0, 0:OVERFLOW // 2], evens, ends[0:1, E - 1:E], None, ALU.is_lt))
            step(dve.tensor_reduce(eob_f[:, OVERFLOW:OVERFLOW + 1], cmp_[:, 0, 0:OVERFLOW // 2], AX_X, ALU.add))
            step(dve.tensor_scalar(eob_f[:, OVERFLOW:OVERFLOW + 1], eob_f[:, OVERFLOW:OVERFLOW + 1], float(PAIRS), None,
                                   ALU.add))
            dve.tensor_copy(eob[:, 0:OVERFLOW + 1], eob_f[:, 0:OVERFLOW + 1]).then_inc(plan_done, 1)
            dve.wait_ge(exp_done, 2)
            step(dve.tensor_reduce(gtmp[:, 0, :], gdif[:, :, :], AX_X, ALU.add))
            step(dve.tensor_scalar(gtmp[:, 1, :], edif[:, :], 1.0, None, ALU.add))
            step(dve.tensor_tensor(gtmp[:, 0, :], gtmp[:, 0, :], gtmp[:, 1, :], ALU.mult))
            step(dve.reciprocal(gates[:, 0, :], gtmp[:, 0, :]))
            step(dve.tensor_tensor(gates[:, 1, :], gates[:, 0, :], edif[:, :], ALU.mult))

            def low(j, n):
                dve.wait_ge(high_done, NP * (j + 1) + n + 1)
                dve.tensor_tensor(we_l[n % 4], raw[n % 6], we_h[n % 4].bitcast(F32), ALU.subtract).then_inc(low_dve, 1)

            def rows_low(j, b):
                dve.wait_ge(xe_high, 2 * j + 1 + b)
                dve.tensor_tensor(part_l[b], xe_ps, part_h[b].bitcast(F32), ALU.subtract).then_inc(xe_low, 1)

            def hidden(j, b):
                dve.wait_ge(silu_done, 2 * j + 3 + b)
                dve.wait_ge(piece_used, NP * (j + 1) + (4, 10)[b])
                dve.tensor_tensor(hid[b].rearrange("p (k q) -> p q k", k=KF),
                                  act_t[b].rearrange("p (q k) -> p q k", k=KF),
                                  up_ps.rearrange("p (q k) -> p q k", k=KF), ALU.mult).then_inc(act_done, 1)

            def hidden_parts(j, b):
                dve.wait_ge(h_tr, 2 * j + 3 + b)
                dve.wait_ge(piece_used, NP * j + (12, 20)[b])
                dve.tensor_copy(hT_h, h_ps).then_inc(h_high, 1)
                dve.wait_ge(h_high, 2 * j + 1 + b)
                dve.tensor_tensor(hT_l, h_ps, hT_h.bitcast(F32), ALU.subtract).then_inc(h_low, 1)

            def body(j, overflow):
                low(j, 0)
                low(j, 1)
                rows_low(j, 0)
                for n in (2, 3, 4):
                    low(j, n)
                rows_low(j, 1)
                low(j, 6)
                hidden(j, 0)
                low(j, 7)
                low(j, 8)
                hidden_parts(j, 0)
                low(j, 9)
                low(j, 10)
                hidden(j, 1)
                hidden_parts(j, 1)

            n_pairs = pair_loop(dve, body)
            def combine(t):
                r, s = ROWS[t], t % FB
                dve.wait_ge(f_x[s], 16 * (t // FB + 1))
                dve.wait_ge(f_in[s], 16 * (t // FB + 1))
                for k in range(2):
                    dve.scalar_tensor_tensor(x_in[s][0:r, :], y_in[s][0:r, k * D:(k + 1) * D], gates[0:r, k, t:t + 1],
                                             x_in[s][0:r, :], ALU.mult, ALU.add).then_inc(f_acc, 1)
                    dve.wait_ge(f_acc, 2 * t + k + 1)

            def final(t):
                r, s = ROWS[t], t % FB
                dve.wait_ge(f_sd, t + 1)
                dve.reciprocal(stat[0:r, 2, t:t + 1], stat[0:r, 1, t:t + 1]).then_inc(f_rs, 1)
                dve.wait_ge(f_rs, t + 1)
                dve.scalar_tensor_tensor(x_in[s][0:r, :], x_in[s][0:r, :], stat[0:r, 2, t:t + 1], gf_bc[0:r, :],
                                         ALU.mult, ALU.mult).then_inc(f_y, 1)

            for t in range(NT):
                combine(t)
                if t == 0:
                    dve.wait_ge(gf_in, 16)
                else:
                    final(t - 1)
            final(NT - 1)

        @block.gpsimd
        def _(pool):
            done = [0]

            def step(ins):
                done[0] += 1
                ins.then_inc(zero_done, 1)
                pool.wait_ge(zero_done, done[0])

            for m in (ident, tri):
                step(pool.memset(m[:, :], 0.0 if m is ident else 1.0))
            step(pool.affine_select(out=ident[:, :], in_=ident[:, :], compare_op=ALU.not_equal, fill=1.0, base=0,
                                    pattern=[[-1, P]], channel_multiplier=1))
            step(pool.affine_select(out=tri[:, :], in_=tri[:, :], compare_op=ALU.is_gt, fill=0.0, base=0,
                                    pattern=[[1, P]], channel_multiplier=-1))
            pool.memset(ones[:, :], 1.0)
            pool.memset(mean_w[:, :], 1.0 / DCONV)
            pool.memset(eps[:, :], EPS)
            for g in range(GROUPS):
                pool.memset(grp[:, g * PER:(g + 1) * PER], float(g))
            for i in range(PS):
                pool.memset(inv_cnt[:, i:i + 1], 1.0 / (i + 1))
            pool.memset(lgt[:, GROUPS:8], LOWEST)
            pool.memset(eid[:, :, :], 99.0)
            pool.memset(s_idx[:, 0:1], int(FAR))
            pool.memset(g_idx[:, NBLK:NBLK + 2], int(FAR))
            step(pool.iota(iota_i, pattern=[[1, P]], base=0, channel_multiplier=0))
            step(pool.iota(tok_i, pattern=[[2 * P, NT], [1, 2]], base=1, channel_multiplier=2))
            step(pool.tensor_copy(iota[:, :], iota_i))
            step(pool.tensor_copy(tokv[:, :], tok_i))
            pool.sem_inc(const_done, 1)

            def w_low(j):
                pool.wait_ge(wh_done, j + 1)
                if j < NCH:
                    hi, lo, src = part_h[j % 2], part_l[j % 2], w_raw[j % 3].rearrange("p (k n) -> p k n", k=KD)
                else:
                    hi, lo, src = wo_h[:, j - NCH, :], wo_l[:, j - NCH, :], w_raw[j % 3]
                pool.tensor_tensor(lo, src, hi.bitcast(F32), ALU.subtract).then_inc(wl_done, 1)

            w_low(0)
            w_low(1)
            pool.wait_ge(cols_done, 1)
            pool.wait_ge(xtr_done, NT)
            for c in range(NC):
                pool.memset(v_ext[:, c, 0:CS], 0.0)
                pool.memset(u_ext[:, c, 0:PS], 0.0)
                pool.tensor_copy(v_ext[:, c, CS + SEQ:CS + SEQ + CS], cols[:, c, R_SV:R_SV + CS])
                step(pool.tensor_copy(u_ext[:, c, PS + SEQ:PS + SEQ + PS], cols[:, c, R_SP:R_SP + PS]))
            pool.sem_inc(pad_done, 1)
            for j in range(2, NCH):
                w_low(j)
            n_win = [0]

            def win_op(ins):
                n_win[0] += 1
                ins.then_inc(win_step, 1)
                pool.wait_ge(win_step, n_win[0])

            for g in range(NG):
                w = 2 << g
                pool.wait_ge(u_done, g + 1)
                src, lo = u_ext[:, g, :], 0
                for i in range(g + 1):
                    s = 1 << i
                    lo += s
                    win_op(pool.tensor_tensor(win[i % 2][:, lo:UW], src[:, lo:UW], src[:, lo - s:UW - s], ALU.add))
                    src = win[i % 2]
                win_op(pool.tensor_tensor(fix[:, 0:w - 1], src[:, PS:PS + w - 1], inv_cnt[:, 0:w - 1], ALU.mult))
                win_op(pool.tensor_tensor(fix[:, 0:w - 1], fix[:, 0:w - 1], u_ext[:, g, PS:PS + w - 1], ALU.subtract))
                pool.wait_ge(st_tr, 2)
                win_op(pool.tensor_scalar(src[:, PS:UW], src[:, PS:UW], 1.0 / w, None, ALU.mult))
                win_op(pool.tensor_tensor(u_ext[:, g, PS:UW], src[:, PS:UW], u_ext[:, g, PS:UW], ALU.subtract))
                pool.tensor_copy(u_ext[:, g, PS:PS + w - 1], fix[:, 0:w - 1]).then_inc(d_done, 1)
                pool.wait_ge(d_done, g + 1)
            for j in range(NCH, NCH + KD):
                w_low(j)
            pool.wait_ge(consts_in, 16 * (6 + GROUPS))
            uses = [len(range(s, NT, 2)) for s in range(2)]
            for t in range(NT):
                r = ROWS[t]
                pool.wait_ge(xt_in[t % 2], 16 * (t // 2 + 1))
                pool.tensor_tensor(xt[t % 2][0:r, :], xt[t % 2][0:r, :], bo_bc[0:r, :], ALU.add).then_inc(xb_done, 1)

            pool.sem_inc(low_pool, len(POOL_PIECES))
            for s in range(2):
                pool.wait_ge(hm_out[s], 16 * uses[s])
                pool.wait_ge(x2_out[s], 16 * uses[s])
            pool.memset(xe[0], 0.0)
            pool.memset(xe[1], 0.0)
            pool.wait_ge(hmtr_done, NT)
            pool.memset(ye[0], 0.0)
            step(pool.memset(ye[1], 0.0))
            last_token, last_row = pool.to_reg(T - 1), pool.to_reg(2 * T - 1)

            def gather(b, at=cur):
                pool.indirect_dma_start(out=xe[b], out_offset=None, in_=hm_dram,
                                        in_offset=bass.IndirectOffsetOnAxis(ap=at[:, b:b + 1], axis=0),
                                        bounds_check=last_token, oob_is_err=False).then_inc(gath[b], 16)

            def scatter(b, at):
                pool.indirect_dma_start(out=y2_dram,
                                        out_offset=bass.IndirectOffsetOnAxis(ap=at, axis=0),
                                        in_=ye[b], in_offset=None,
                                        bounds_check=last_row, oob_is_err=False).then_inc(scat[b], 16)

            for b in range(2):
                scatter(b, s_idx[:, 0:1])
            pool.wait_ge(idx_done, 1)
            gather(0, g_idx)
            gather(1, g_idx)

            def low(j, n):
                pool.wait_ge(high_done, NP * (j + 1) + n + 1)
                pool.tensor_tensor(we_l[n % 4], raw[n % 6], we_h[n % 4].bitcast(F32), ALU.subtract).then_inc(low_pool, 1)

            def next_rows(j, b):
                pool.wait_ge(xe_tr, 2 * j + 1 + b)
                pool.wait_ge(idx_done, 1)
                pool.tensor_copy(cur[:, b:b + 1], g_idx[:, bass.ds(2 * j + 2 + b, 1)]).then_inc(cur_done, 1)
                pool.wait_ge(cur_done, 4 * j + (1, 3)[b])
                pool.sem_inc(cur_seen, 1)
                gather(b)

            def store_rows(j, b, last=False):
                pool.wait_ge(ye_done, 2 * j + (4, 3)[b])
                pool.wait_ge(scat[b], 16 * (j + 1))
                pool.wait_ge(idx_done, 1)
                pool.tensor_copy(cur[:, 2 + b:3 + b], s_idx[:, bass.ds(2 * j + (1, 0)[b], 1)]).then_inc(cur_done, 1)
                pool.wait_ge(cur_done, 4 * j + (1 if last else (4, 2)[b]))
                pool.sem_inc(cur_seen, 1)
                scatter(b, cur[:, 2 + b:3 + b])

            def body(j, overflow):
                next_rows(j, 0)
                store_rows(j, 1)
                next_rows(j, 1)
                low(j, 5)
                low(j, 11)
                store_rows(j, 0)

            n_pairs = pair_loop(pool, body)
            store_rows(n_pairs, 1, last=True)
            pool.wait_ge(scat[0], 16 * n_pairs + 16)
            pool.wait_ge(scat[1], 16 * n_pairs + 32)
            for b in (0, 1):
                pool.wait_ge(gath[b], 16 * n_pairs + 16)
            pool.sem_inc(sc_all, 1)


_INS = ["x_prompt", "x_sample", "state_pool", "state_conv", "norm1_g", "w_in", "pool_lin", "pool_scale", "conv_dw",
        "conv_dw_b", "conv_ln_g", "conv_ln_b", "w_out", "b_out", "norm2_g", "w_rg", "b_rg", "w_re", "b_re", "w_eg",
        "w_eu", "w_ed", "norm_f_g"]


def kernel(**inputs):
    import numpy as np
    import concourse.bacc as bacc
    from concourse.bass_utils import run_bass_kernel_spmd

    nc = bacc.Bacc("TRN2", target_bir_lowering=False, num_devices=1)
    arrays, args = {}, []
    for name in _INS:
        a = np.ascontiguousarray(inputs[name])
        arrays[f"in_{name}"] = a
        args.append(nc.dram_tensor(f"in_{name}", a.shape, mybir.dt.from_np(a.dtype), kind="ExternalInput").ap())
    sp, sc = inputs["state_pool"].shape, inputs["state_conv"].shape
    batch = inputs["x_prompt"].shape[0]
    shapes = [inputs["x_prompt"].shape, inputs["x_sample"].shape, (sp[0], batch) + tuple(sp[2:]),
              (sc[0], batch) + tuple(sc[2:]), sp, sc]
    outs = [nc.dram_tensor(f"out_{i}", list(s), F32, kind="ExternalOutput").ap() for i, s in enumerate(shapes)]
    trunk_kernel(nc, *args, *outs)
    r = run_bass_kernel_spmd(nc, [arrays], core_ids=[0])
    return tuple(r.results[0][f"out_{i}"] for i in range(len(shapes)))
```

```python
from contextlib import ExitStack

import concourse.bass as bass
from concourse import mybir

F32 = mybir.dt.float32
F32R = mybir.dt.float32r
I32 = mybir.dt.int32
U32 = mybir.dt.uint32
ALU = mybir.AluOpType
ACT = mybir.ActivationFunctionType
AX_X = mybir.AxisListType.X

P = 128
BANK = 512
EPS = 1e-6
FAR = float(1 << 20)
LOWEST = -3.0e38


def trunk_kernel(nc, x_prompt, x_sample, state_pool, state_conv, norm1_g, w_in, pool_lin, pool_scale,
                 conv_dw, conv_dw_b, conv_ln_g, conv_ln_b, w_out, b_out, norm2_g, w_rg, b_rg, w_re,
                 b_re, w_eg, w_eu, w_ed, norm_f_g,
                 y_prompt, y_sample, pool_state_prompt, conv_state_prompt, pool_state_sample,
                 conv_state_sample):
    SEQ, D = x_prompt.shape[1], x_prompt.shape[2]
    DEC = x_sample.shape[1]
    KD = D // P
    PS, DPOOL = state_pool.shape[2], state_pool.shape[3]
    CS, DCONV = state_conv.shape[2], state_conv.shape[3]
    TAPS = CS + 1
    NG = pool_lin.shape[1]
    NC = DCONV // P
    GROUPS, PER = w_re.shape[1], w_re.shape[3]
    E = GROUPS * PER
    FF = w_eg.shape[3]
    KF = FF // P
    T = SEQ + DEC
    NT = -(-T // P)
    ROWS = [min(P, T - t * P) for t in range(NT)]
    BLOCKS = [(0, BANK), (BANK, BANK), (SEQ, DEC)]
    OVERFLOW = (2 * T - 1) // P
    NBLK = E + OVERFLOW
    LB = GROUPS + E
    assert SEQ == 2 * BANK and NC + DPOOL // P == KD and NG == NC == 4 and KD == 8 and KF == 4 and PER == 8 and NBLK % 2 == 0
    VW = CS + SEQ + CS + DEC
    HW_ = VW - CS
    UW = PS + SEQ + PS + DEC
    PAIRS = E // 2
    MAX_PAIRS = NBLK // 2

    ctx = ExitStack()
    with ctx:
        def sb(name, shape, dt=F32):
            return ctx.enter_context(nc.sbuf_tensor(name, shape, dt))

        def sem(name):
            return ctx.enter_context(nc.semaphore(name))

        hm_dram = nc.dram_tensor("hm_scratch", [T, D], F32).ap()
        x2_dram = nc.dram_tensor("x2_scratch", [T, D], F32).ap()
        y2_dram = nc.dram_tensor("y2_scratch", [2 * T, D], F32).ap()

        big = sb("big", [P, 2 * KD * T], F32R)
        ring = sb("ring", [P, 4 * D], F32R)
        hTr = sb("hTr", [P, 2 * FF], F32R)
        hot_mem = sb("hot_mem", [P, 2 * NT * E + (2 * NT - 2 * KD) * P], F32R)
        xT_h = big[:, 0:KD * T].rearrange("p (k t) -> p k t", k=KD)
        xT_l = big[:, KD * T:2 * KD * T].rearrange("p (k t) -> p k t", k=KD)
        wo_h = big[:, 0:KD * D].rearrange("p (k n) -> p k n", k=KD)
        wo_l = big[:, KD * D:2 * KD * D].rearrange("p (k n) -> p k n", k=KD)
        HP = 2048
        we_h = [big[:, s * 2 * HP:s * 2 * HP + HP] for s in range(4)]
        we_l = [big[:, s * 2 * HP + HP:(s + 1) * 2 * HP] for s in range(4)]
        part_h = [ring[:, s * 2 * D:s * 2 * D + D].rearrange("p (k n) -> p k n", k=KD) for s in range(2)]
        part_l = [ring[:, s * 2 * D + D:(s + 1) * 2 * D].rearrange("p (k n) -> p k n", k=KD) for s in range(2)]
        hT_h = hTr[:, 0:FF].rearrange("p (k n) -> p k n", k=KF)
        hT_l = hTr[:, FF:2 * FF].rearrange("p (k n) -> p k n", k=KF)

        SZ_V, SZ_U, SZ_H = NC * VW, NG * UW, NC * HW_
        SZ_S1, SZ_S2, SZ_X, SZ_W, SZ_T = 2 * UW, 2112, 2 * D, 3 * D, D
        arena = sb("arena", [P, SZ_V + SZ_U + SZ_H + SZ_S1 + SZ_S2 + SZ_X + SZ_W + SZ_T])
        at = [0]

        def region(size):
            at[0] += size
            return arena[:, at[0] - size:at[0]]

        r_v, r_u, r_h, r_w = region(SZ_V), region(SZ_U), region(SZ_H), region(SZ_W)
        r_s1, r_s2, r_x, r_t = region(SZ_S1), region(SZ_S2), region(SZ_X), region(SZ_T)
        v_ext = r_v.rearrange("p (c t) -> p c t", c=NC)
        u_ext = r_u.rearrange("p (g t) -> p g t", g=NG)
        hc = r_h.rearrange("p (c t) -> p c t", c=NC)
        win = [r_s1[:, 0:UW], r_s1[:, UW:2 * UW]]
        ln_sd = [win[1][:, 0:BANK], r_w[:, 0:BANK], r_w[:, BANK:BANK + DEC]]
        hm = [r_s1[:, 0:D], r_s1[:, D:2 * D]]
        junk = r_s2[:, 0:D]
        sg = r_s2[:, D:D + T]
        sq = [r[:, 0:NC * BANK].rearrange("p (c t) -> p c t", c=NC) for r in (r_x, r_s2)] + [
            r_w[:, D:D + NC * DEC].rearrange("p (c t) -> p c t", c=NC)]
        taps_pr = [[r_x[:, s * D:s * D + HW_ - BANK] for s in range(2)],
                   [r_s2[:, D + s * BANK:D + (s + 1) * BANK] for s in range(2)]]
        states = r_s2[:, 0:4 * BANK].rearrange("p (s n) -> p s n", s=4)
        Mx = r_s2[:, D:D + 2 * NT * E].rearrange("p (s e) -> p s e", e=E)
        MS = sb("MS", [P, NT, E])
        prod_t = r_s2[:, D + 2 * NT * E:D + 2 * NT * E + 2 * E].rearrange("p (k e) -> p k e", e=E)
        prod = r_s2[:, 0:2 * NT * E].rearrange("p (s e) -> p s e", e=E)
        assert 2 * T < 4096 and NT == KD + 1 and 2 * KD * (T - D) >= KD * P and SEQ == KD * P
        hots = ([big[:, 2 * KD * D + i * P:2 * KD * D + (i + 1) * P] for i in range(KD)] +
                [hTr[:, i * P:(i + 1) * P] for i in range(KD)] +
                [hot_mem[:, 2 * NT * E + i * P:2 * NT * E + (i + 1) * P] for i in range(2 * NT - 2 * KD)])
        hot_own = hot_mem[:, 0:2 * NT * E].rearrange("p (s b) -> p s b", b=E)
        hot_over = hot_mem[:, 0:2 * NT * OVERFLOW].rearrange("p (s b) -> p s b", b=OVERFLOW)
        xt = [r_x[:, 0:D], r_x[:, D:2 * D]]
        xa = (xt + [r_h[:, i * D:(i + 1) * D] for i in range(4)] + [r_u[:, i * D:(i + 1) * D] for i in range(4)])[:NT]
        w_raw = [r_w[:, s * D:(s + 1) * D] for s in range(3)]
        wo_raw = w_raw + [r_t]
        g1_bc = r_t
        hmT = r_t.rearrange("p (k n) -> p k n", k=KD)
        raw = [arena[:, s * HP:(s + 1) * HP] for s in range(8)]
        xe = xt
        ye = [r_s1[:, 0:D], r_s1[:, D:2 * D]]
        act_t = [r_t[:, 0:FF], r_t[:, FF:2 * FF]]
        hid = [r_s2[:, 0:FF], r_s2[:, FF:2 * FF]]
        FB = 6
        x_in = [arena[:, t * D:(t + 1) * D] for t in range(NT)]
        gf_bc = arena[:, NT * D:(NT + 1) * D]
        y_in = [arena[:, (NT + 1 + 2 * s) * D:(NT + 3 + 2 * s) * D] for s in range(FB)]
        junk_f = arena[:, (NT + 1 + 2 * FB) * D:(NT + 2 + 2 * FB) * D]

        ident = sb("ident", [P, P])
        tri = sb("tri", [P, P])
        ones = sb("ones", [P, P])
        mean_w = sb("mean_w", [P, P])
        iota_i = r_s1[:, BANK:BANK + P].bitcast(I32)
        iota = sb("iota", [P, P])
        grp = sb("grp", [P, E])
        tok_i = r_s1[:, BANK + P:BANK + P + 2 * NT].bitcast(I32)
        tokv = sb("tokv", [P, 2 * NT])
        inv_cnt = sb("inv_cnt", [P, PS])
        eps = sb("eps", [P, 1])
        NROW = TAPS + 4 + PS + CS
        rows = r_s1[0:NROW, 0:BANK]
        cols = sb("cols", [P, NC, NROW])
        R_B, R_LG, R_LB, R_SC = TAPS, TAPS + 1, TAPS + 2, TAPS + 3
        R_SP, R_SV = TAPS + 4, TAPS + 4 + PS
        plin = sb("plin", [P, NG, P])
        w_rt = sb("w_rt", [P, KD, LB])
        b_rt = sb("b_rt", [P, LB])
        g2_bc = sb("g2_bc", [P, D])
        bo_bc = sb("bo_bc", [P, D])
        stat = sb("stat", [P, 6, NT])
        fix = sb("fix", [P, NG, PS])
        u_end = sb("u_end", [P, NG, 2, PS])
        lgt = sb("lgt", [P, 8 + E])
        top = sb("top", [P, 2, 8])
        topi = sb("topi", [P, 2, 8], U32)
        gsel = sb("gsel", [P, 1])
        pen = sb("pen", [P, E])
        le = sb("le", [P, E])
        eid = sb("eid", [P, NT, 2])
        gdif = sb("gdif", [P, NT, GROUPS])
        edif = sb("edif", [P, NT])
        gates = sb("gates", [P, 2, NT])
        gtmp = sb("gtmp", [P, 2, NT])
        pref = sb("pref", [P, NT + 1, E])
        rk_n = sb("rk_n", [P, E])
        cum = [sb("cum0", [P, 16 + E]), sb("cum1", [P, 16 + E])]
        nb = sb("nb", [P, E])
        base = sb("base", [P, E])
        sl = sb("sl", [P, 6, 2 * NT])
        sl_i = sb("sl_i", [P, 3, 2 * NT], I32)
        cmp_ = r_s2[0:1, BANK:BANK + OVERFLOW * E].rearrange("p (b e) -> p b e", e=E)
        eob_f = sb("eob_f", [1, OVERFLOW + 2])
        eob = sb("eob", [1, OVERFLOW + 2], I32)
        idx_f = sb("idx_f", [P, 2, NBLK])
        s_idx = sb("s_idx", [P, 1 + NBLK], U32)
        g_idx = sb("g_idx", [P, NBLK + 2], U32)
        cur = sb("cur", [P, 4], U32)
        warm = sb("warm", [P, 1])

        ps = ctx.enter_context(nc.psum_tensor("ps", [P, 8 * BANK], F32))

        def banks(a, n):
            return ps[:, a * BANK:(a + n) * BANK]

        z_ps = [banks(0, 3), banks(3, 3)]
        x_ps = banks(6, 2).rearrange("p (k n) -> p k n", k=KD)
        xa_ps = [x_ps, banks(4, 2).rearrange("p (k n) -> p k n", k=KD)]
        cols_ps = banks(3, 1)[:, 0:NC * NROW].rearrange("p (c r) -> p c r", c=NC)
        st_ps = [banks(6, 1), banks(7, 1)]
        mean_ps = [banks(6, 1), banks(0, 1), banks(1, 1)]
        var_ps = [banks(7, 1), banks(1, 1), banks(0, 1)]
        out_ps = [banks(2, 2), banks(4, 2)]
        lg_ps = banks(0, 1)[:, 0:LB]
        rk_ps = banks(1, 1)[:, 0:(NT + 1) * E].rearrange("p (t e) -> p t e", e=E)
        ix_ps = banks(7, 1)[:, 0:NBLK]
        xe_ps = banks(0, 2).rearrange("p (k n) -> p k n", k=KD)
        gate_ps, up_ps = banks(2, 1), banks(3, 1)
        h_ps = banks(4, 1).rearrange("p (k n) -> p k n", k=KF)
        ye_ps = banks(5, 2)

        const_done = sem("const_done")
        rows_in, g1_in, consts_in, rows_tr, cols_done = map(sem, ("rows_in", "g1_in", "consts_in", "rows_tr", "cols_done"))
        xt_in = [sem("xt_in0"), sem("xt_in1")]
        xa_in = [sem(f"xa_in{t}") for t in range(NT)]
        wo_in = [sem(f"wo_in{s}") for s in range(4)]
        w_in_s = [sem(f"w_raw_in{s}") for s in range(3)]
        sum1_done, sd1_done, rs1_done, xs_done, xtr_done, xh_done, xl_done = map(sem, (
            "sum1_done", "sd1_done", "rs1_done", "xs_done", "xtr_done", "xh_done", "xl_done"))
        wh_done, wl_done, z_done, sg_done, v_done, u_done, pad_done = map(sem, (
            "wh_done", "wl_done", "z_done", "sg_done", "v_done", "u_done", "pad_done"))
        conv_step, conv_done, st_tr, st_done, st_out, win_step, d_done, pl_done, yp_done = map(sem, (
            "conv_step", "conv_done", "st_tr", "st_done", "st_out", "win_step", "d_done", "pl_done", "yp_done"))
        mean_done, cen_done, sq_done, var_done, lnsd_done, lnrs_done, nrm_done, mix_done = map(sem, (
            "mean_done", "cen_done", "sq_done", "var_done", "lnsd_done", "lnrs_done", "nrm_done", "mix_done"))
        mh_done, ml_done, out_done, xb_done, x2_done, sum2_done, sd2_done, rs2_done, hm_done = map(sem, (
            "mh_done", "ml_done", "out_done", "xb_done", "x2_done", "sum2_done", "sd2_done", "rs2_done", "hm_done"))
        x2_out = [sem("x2_out0"), sem("x2_out1")]
        hm_out = [sem("hm_out0"), sem("hm_out1")]
        hmtr_done, hmT_done, lg_done, lg_read, rt_step, rt_done, exp_done = map(sem, (
            "hmtr_done", "hmT_done", "lg_done", "lg_read", "rt_step", "rt_done", "exp_done"))
        counted, rk_done, hot_done, ix_done, plan_done, idx_done = map(sem, (
            "counted", "rk_done", "hot_done", "ix_done", "plan_done", "idx_done"))
        raw_in = [sem(f"raw_in{s}") for s in range(8)]
        high_done, low_dve, low_pool, piece_used = map(sem, ("high_done", "low_dve", "low_pool", "piece_used"))
        gath = [sem("gath0"), sem("gath1")]
        scat = [sem("scat0"), sem("scat1")]
        xe_tr, xe_high, xe_low, silu_done, act_done, h_tr, h_high, h_low, ye_done, cur_done, zero_done = map(sem, (
            "xe_tr", "xe_high", "xe_low", "silu_done", "act_done", "h_tr", "h_high", "h_low", "ye_done", "cur_done",
            "zero_done"))
        f_x = [sem(f"f_x{t}") for t in range(NT)]
        f_in = [sem(f"f_in{s}") for s in range(FB)]
        gf_in, f_acc, f_sum, f_sd, f_rs, f_y = map(sem, ("gf_in", "f_acc", "f_sum", "f_sd", "f_rs", "f_y"))
        f_out = sem("f_out")
        prod_done, help_done, win_done, scaled_done, wl_dve = map(sem, (
            "prod_done", "help_done", "win_done", "scaled_done", "wl_dve"))
        zeros_set, yp_dve = sem("zeros_set"), sem("yp_dve")
        sc_all, cur_seen, placed = sem("scattered"), sem("cur_seen"), sem("placed")

        def x_rows(t):
            return x_prompt[0, t * P:(t + 1) * P, :] if t * P < SEQ else x_sample[0, :, :]

        KINDS = [("gate", 0), ("value", 0), ("gate", 1), ("value", 1), ("gate", 2), ("value", 2), ("pool", 3),
                 ("gate", 3), ("value", 3), ("pool", 2), ("pool", 1), ("pool", 0)]
        CHUNKS = [{"pool": 0, "value": DPOOL, "gate": DPOOL + DCONV}[kind] + c * P for kind, c in KINDS]
        NCH = len(CHUNKS)
        POOL_ORDER = [c for kind, c in KINDS if kind == "pool"]
        J = {kc: j for j, kc in enumerate(KINDS)}
        CUT = HW_ - 220
        PART = {"A": (0, BANK), "B": (BANK, HW_), "C": (BANK, CUT)}
        HELPED = [(1, BANK, HW_), (3, CUT, HW_)]
        help_n = {4: 7, 5: 7, 6: 7, 8: 6, 9: TAPS - 1 - 27}
        DVE_WO = (0, 1, 4, 5, 6)
        POOL_WO = [k for k in range(KD) if k not in DVE_WO]
        def hc_at(tok):
            return tok if tok < SEQ else tok + CS

        PIECES = [(0, "g", 0), (0, "g", 1), (0, "u", 0), (0, "u", 1), (1, "g", 0), (1, "g", 1),
                  (0, "d", 0), (0, "d", 1), (1, "u", 0), (1, "u", 1), (1, "d", 0), (1, "d", 1)]
        NP = len(PIECES)
        assert 8 * HP <= SZ_V + SZ_U + SZ_H + SZ_W
        RAW = [n if n in (0, 1, 6, 7) else n % 6 for n in range(NP)]

        def raw_count(j, n):
            shared = RAW.count(RAW[n])
            return 16 * shared * j + 16 * (RAW[:n + 1].count(RAW[n]))

        POOL_PIECES = (5, 11)

        def low_count(n):
            mine = [m for m in range(NP) if (m in POOL_PIECES) == (n in POOL_PIECES)]
            return (low_pool if n in POOL_PIECES else low_dve), len(mine), mine.index(n) + 1

        def wait_low(eng, j, n):
            s, per, k = low_count(n % NP)
            eng.wait_ge(s, j * per + (per if n >= 0 else 0) + k)

        def pair_loop(eng, body, start=0):
            with eng.Fori(start, PAIRS) as j:
                body(j, False)
            eng.wait_ge(plan_done, 1)
            n_pairs = eng.value_load(eob[0:1, OVERFLOW:OVERFLOW + 1], min_val=PAIRS, max_val=MAX_PAIRS)
            with eng.Fori(PAIRS, MAX_PAIRS) as j:
                with eng.If(n_pairs > j):
                    body(j, True)
                eng.nop()
            return n_pairs

        block = ctx.enter_context(nc.Block())

        @block.sync
        def _(sp):
            def load_x(t):
                sp.dma_start(xa[t][0:ROWS[t], :], x_rows(t)).then_inc(xa_in[t], 16)

            load_x(0)
            sp.dma_start(g1_bc, norm1_g[0].partition_broadcast(P)).then_inc(g1_in, 16)
            load_x(1)
            load_x(2)
            r0 = 0
            for src in (conv_dw[0], conv_dw_b, conv_ln_g, conv_ln_b, pool_scale, state_pool[0, 0], state_conv[0, 0]):
                n = src.shape[0]
                sp.dma_start(rows[r0:r0 + n, :], src).then_inc(rows_in, 16)
                r0 += n

            def load_w_in(j):
                if j >= 3:
                    sp.wait_ge(wl_done, j - 2)
                src = w_in[0, :, CHUNKS[j]:CHUNKS[j] + P].rearrange("(k p) n -> p k n", p=P)
                sp.dma_start(w_raw[j % 3].rearrange("p (k n) -> p k n", k=KD), src).then_inc(w_in_s[j % 3], 16)

            for t in range(3, NT):
                load_x(t)
                if t % 2 == 0:
                    load_w_in(t // 2 - 2)
            sp.dma_start(plin[:, :, :], pool_lin[0].rearrange("g c d -> c g d")).then_inc(consts_in, 16)
            sp.dma_start(w_rt[:, :, 0:GROUPS], w_rg[0].rearrange("(p k) n -> p k n", p=P)).then_inc(consts_in, 16)
            for g in range(GROUPS):
                at_g = GROUPS + g * PER
                sp.dma_start(w_rt[:, :, at_g:at_g + PER],
                             w_re[0, g].rearrange("(p k) n -> p k n", p=P)).then_inc(consts_in, 16)
            sp.dma_start(b_rt[:, 0:GROUPS], b_rg[0].partition_broadcast(P)).then_inc(consts_in, 16)
            sp.dma_start(b_rt[:, GROUPS:LB],
                         b_re[0].rearrange("g e -> (g e)").partition_broadcast(P)).then_inc(consts_in, 16)
            sp.dma_start(g2_bc[:, :], norm2_g[0].partition_broadcast(P)).then_inc(consts_in, 16)
            sp.dma_start(bo_bc[:, :], b_out[0].partition_broadcast(P)).then_inc(consts_in, 16)
            for j in range(3, NCH):
                load_w_in(j)
            def load_w_out(k):
                if k < 3:
                    sp.wait_ge(wl_done, NCH + k - 2)
                elif k == 3:
                    sp.wait_ge(xtr_done, NT)
                elif k - 4 in DVE_WO:
                    sp.wait_ge(wl_dve, DVE_WO.index(k - 4) + 1)
                else:
                    sp.wait_ge(wl_done, NCH + POOL_WO.index(k - 4) + 1)
                sp.dma_start(wo_raw[k % 4], w_out[0, k * P:(k + 1) * P, :]).then_inc(wo_in[k % 4], 16)

            for k in range(4):
                load_w_out(k)
            for k in range(4, KD):
                load_w_out(k)
            dst = (conv_state_prompt[0, 0], conv_state_sample[0, 0], pool_state_prompt[0, 0], pool_state_sample[0, 0])
            for s in range(4):
                sp.wait_ge(st_done, s + 1)
                sp.dma_start(dst[s], states[0:(CS if s < 2 else PS), s, :]).then_inc(st_out, 16)
            def load_residual(t):
                sp.dma_start(xt[t % 2][0:ROWS[t], :], x_rows(t)).then_inc(xt_in[t % 2], 16)

            def weights(j, overflow, a=0, b=NP):
                if overflow:
                    e = [sp.value_load(eob[0:1, bass.ds(2 * j + b_ - E, 1)], min_val=0, max_val=E - 1) for b_ in (0, 1)]
                else:
                    e = [2 * j, 2 * j + 1]
                for n in range(a, b):
                    b_, m, half = PIECES[n]
                    w = {"g": w_eg, "u": w_eu, "d": w_ed}[m]
                    src = w[0, bass.ds(e[b_], 1), :, :].rearrange("a (p k) n -> p (a k n)", p=P)
                    wait_low(sp, j, n - NP // RAW.count(RAW[n]))
                    sp.dma_start(raw[RAW[n]], src[:, half * HP:(half + 1) * HP]).then_inc(raw_in[RAW[n]], 16)

            sp.wait_ge(xtr_done, NT)
            sp.wait_ge(help_done, TAPS)
            sp.wait_ge(var_done, 1)
            load_residual(0)
            load_residual(1)
            for t in range(NT):
                sp.wait_ge(x2_done, t + 1)
                sp.dma_start(x2_dram[t * P:t * P + ROWS[t], :], xt[t % 2][0:ROWS[t], :]).then_inc(x2_out[t % 2], 16)
                sp.wait_ge(hm_done, t + 1)
                sp.dma_start(hm_dram[t * P:t * P + ROWS[t], :], hm[t % 2][0:ROWS[t], :]).then_inc(hm_out[t % 2], 16)
                if t + 2 < NT:
                    sp.wait_ge(x2_out[t % 2], 16 * (t // 2 + 1))
                    load_residual(t + 2)
                if t == NT - 3:
                    sp.wait_ge(mh_done, NT)
                    sp.wait_ge(ml_done, NT)
                    sp.wait_ge(st_tr, 4)
                    weights(0, False, 0, 8)
            weights(0, False, 8)
            n_pairs = pair_loop(sp, weights, 1)
            for s in range(2):
                sp.wait_ge(x2_out[s], 16 * len(range(s, NT, 2)))
            for t in range(NT):
                if t % 2 == 0:
                    last_piece = max(n for n in range(NP) if RAW[n] == t // 2)
                    wait_low(sp, n_pairs - 1, last_piece)
                sp.dma_start(x_in[t][0:ROWS[t], :], x2_dram[t * P:t * P + ROWS[t], :]).then_inc(f_x[t], 16)
            sp.dma_start(gf_bc, norm_f_g.partition_broadcast(P)).then_inc(gf_in, 16)

            def load_y2(t):
                r = ROWS[t]
                sp.dma_start(y_in[t % FB][0:r, :], y2_dram[2 * t * P:2 * (t * P + r), :]
                             .rearrange("(p k) n -> p (k n)", k=2)).then_inc(f_in[t % FB], 16)

            sp.wait_ge(sc_all, 1)
            for t in range(FB):
                load_y2(t)
            for t in range(NT):
                if t + FB < NT:
                    sp.wait_ge(f_acc, 2 * t + 2)
                    load_y2(t + FB)
                sp.wait_ge(f_y, t + 1)
                dst = y_prompt[0, t * P:(t + 1) * P, :] if t * P < SEQ else y_sample[0, :, :]
                sp.dma_start(dst, x_in[t][0:ROWS[t], :]).then_inc(f_out, 16)
            sp.wait_ge(st_out, 64)
            sp.wait_ge(f_out, 16 * NT)

        @block.scalar
        def _(act):
            act.sem_inc(high_done, NP)
            act.sem_inc(silu_done, 2)
            act.sem_inc(ye_done, 2)

            def w_high(j):
                act.wait_ge(w_in_s[j % 3], 16 * (j // 3 + 1))
                if j >= 2:
                    act.wait_ge(z_done, j - 1)
                act.activation(part_h[j % 2], w_raw[j % 3].rearrange("p (k n) -> p k n", k=KD), ACT.Copy).then_inc(wh_done, 1)

            def wo_high(k):
                act.wait_ge(wo_in[k % 4], 16 * (k // 4 + 1))
                act.wait_ge(z_done, NCH)
                act.activation(wo_h[:, k, :], wo_raw[k % 4], ACT.Copy).then_inc(wh_done, 1)

            def x_high(t):
                act.wait_ge(xtr_done, t + 1)
                act.activation(xT_h[:, :, t * P:t * P + ROWS[t]], xa_ps[t % 2][:, :, 0:ROWS[t]],
                               ACT.Copy).then_inc(xh_done, 1)

            act.wait_ge(const_done, 1)
            for t in range(NT):
                r = ROWS[t]
                act.wait_ge(xa_in[t], 16)
                if t:
                    act.wait_ge(sum1_done, t)
                act.activation(junk[0:r, :], xa[t][0:r, :], ACT.Square,
                               accum_out=stat[0:r, 0, t:t + 1]).then_inc(sum1_done, 1)
                act.wait_ge(sum1_done, t + 1)
                act.activation(stat[0:r, 1, t:t + 1], stat[0:r, 0, t:t + 1], ACT.Sqrt, bias=eps[0:r, :],
                               scale=1.0 / D).then_inc(sd1_done, 1)
                if t >= 2:
                    x_high(t - 2)
                if t == 3:
                    act.wait_ge(rows_tr, 1)
                    act.activation(cols[:, :, :], cols_ps, ACT.Copy).then_inc(cols_done, 1)
                if t in (4, 6):
                    w_high(t // 2 - 2)
            x_high(NT - 2)
            x_high(NT - 1)

            def gate(c):
                act.wait_ge(z_done, J["gate", c] + 1)
                if c:
                    act.wait_ge(v_done, c)
                act.activation(sg, z_ps[J["gate", c] % 2][:, 0:T], ACT.Sigmoid).then_inc(sg_done, 1)

            def pool_in(g):
                j = J["pool", g]
                act.wait_ge(z_done, j + 1)
                z = z_ps[j % 2]
                act.activation(u_ext[:, g, PS:PS + SEQ], z[:, 0:SEQ], ACT.Copy)
                act.activation(u_end[:, g, 0, :], z[:, SEQ - PS:SEQ], ACT.Copy)
                act.activation(u_end[:, g, 1, :], z[:, T - PS:T], ACT.Copy)
                act.activation(u_ext[:, g, PS + SEQ + PS:UW], z[:, SEQ:T], ACT.Copy).then_inc(u_done, 1)

            made = [0, 0]

            def products(h, n):
                c, a, b = HELPED[h]
                if made[h] == 0:
                    act.wait_ge(v_done, c + 1)
                for j in range(made[h], made[h] + n):
                    scale = cols[:, c, j:j + 1]
                    if j == 0:
                        act.activation(hc[:, c, a:b], v_ext[:, c, a:b], ACT.Identity, scale=scale,
                                       bias=cols[:, c, R_B:R_B + 1]).then_inc(prod_done, 1)
                    else:
                        if j >= 3:
                            act.wait_ge(help_done, h * TAPS + j - 1)
                        act.activation(taps_pr[h][j % 2][:, 0:b - a], v_ext[:, c, a + j:b + j], ACT.Copy,
                                       scale=scale).then_inc(prod_done, 1)
                made[h] += n

            def window_scale(g):
                i = POOL_ORDER.index(g)
                act.wait_ge(win_done, i + 1)
                src = win[g % 2][:, PS:UW]
                act.activation(src, src, ACT.Copy, scale=1.0 / (2 << g)).then_inc(scaled_done, 1)

            def state_rows(s):
                n = CS if s < 2 else PS
                act.wait_ge(st_tr, s + 1)
                act.activation(states[0:n, s, :], st_ps[s % 2][0:n, :], ACT.Copy).then_inc(st_done, 1)

            def pooled(i):
                g = POOL_ORDER[i]
                act.wait_ge(pl_done, i + 1)
                act.activation(u_ext[:, g, 0:T], z_ps[i % 2][:, 0:T], ACT.Copy,
                               scale=cols[:, g, R_SC:R_SC + 1]).then_inc(yp_done, 1)

            def ln_square(n):
                tok, w = BLOCKS[n]
                act.wait_ge(cen_done, n + 1)
                if n == 0:
                    act.wait_ge(help_done, TAPS)
                if n == 1:
                    act.wait_ge(help_done, 2 * TAPS)
                act.activation(sq[n][:, :, 0:w], hc[:, :, hc_at(tok):hc_at(tok) + w], ACT.Square).then_inc(sq_done, 1)

            def ln_deviation(n):
                tok, w = BLOCKS[n]
                act.wait_ge(var_done, n + 1)
                if n == 0:
                    act.wait_ge(d_done, NG - 1)
                act.activation(ln_sd[n], var_ps[n][:, 0:w], ACT.Sqrt, bias=eps[:, :]).then_inc(lnsd_done, 1)

            act.wait_ge(pad_done, 1)
            for j, (kind, c) in enumerate(KINDS):
                if j == NCH - 1:
                    ln_square(0)
                    window_scale(1)
                if kind == "gate":
                    gate(c)
                elif kind == "pool":
                    pool_in(c)
                if j + 2 < NCH:
                    w_high(j + 2)
                step_j = j + 1
                if step_j in help_n:
                    products(0, help_n[step_j] + (made[0] == 0))
                if step_j == 8:
                    window_scale(3)
                if step_j == 11:
                    window_scale(2)
                    act.wait_ge(v_done, NC)
                    state_rows(0)
                    state_rows(1)
            wo_high(0)
            wo_high(1)
            ln_deviation(0)
            wo_high(2)
            wo_high(3)
            window_scale(0)
            pooled(0)
            wo_high(4)
            pooled(1)
            wo_high(5)
            state_rows(2)
            wo_high(6)
            state_rows(3)
            wo_high(7)

            def ln_swish(n):
                tok, w = BLOCKS[n]
                act.wait_ge(nrm_done, n + 1)
                for c in range(NC):
                    y = hc[:, c, hc_at(tok):hc_at(tok) + w]
                    act.activation(y, y, ACT.Silu, scale=cols[:, c, R_LG:R_LG + 1],
                                   bias=cols[:, c, R_LB:R_LB + 1]).then_inc(mix_done, 1)

            ln_swish(0)

            def mix_high(t):
                r, tok = ROWS[t], t * P
                act.wait_ge(mix_done, NC * (min(tok // BANK, 2) + 1))
                if t >= 2:
                    act.wait_ge(out_done, t - 1)
                act.activation(part_h[t % 2][:, 0:NG, 0:r], u_ext[:, :, tok:tok + r], ACT.Copy)
                act.activation(part_h[t % 2][:, NG:KD, 0:r], hc[:, :, hc_at(tok):hc_at(tok) + r],
                               ACT.Copy).then_inc(mh_done, 1)

            def hm_turned(t):
                act.wait_ge(hmtr_done, t + 1)
                if t:
                    act.wait_ge(lg_done, t)
                act.activation(hmT[:, :, 0:ROWS[t]], x_ps[:, :, 0:ROWS[t]], ACT.Copy).then_inc(hmT_done, 1)

            act.wait_ge(yp_dve, NG - 2)
            mix_high(0)
            mix_high(1)
            act.wait_ge(st_out, 64)
            products(1, TAPS)
            for t in range(NT):
                r = ROWS[t]
                act.wait_ge(x2_done, t + 1)
                if t:
                    act.wait_ge(sum2_done, t)
                if t in (0, 2):
                    act.wait_ge(var_done, t + 1)
                act.activation(junk[0:r, :], xt[t % 2][0:r, :], ACT.Square,
                               accum_out=stat[0:r, 3, t:t + 1]).then_inc(sum2_done, 1)
                act.wait_ge(sum2_done, t + 1)
                act.activation(stat[0:r, 4, t:t + 1], stat[0:r, 3, t:t + 1], ACT.Sqrt, bias=eps[0:r, :],
                               scale=1.0 / D).then_inc(sd2_done, 1)
                if t == 1:
                    mix_high(t + 2)
                    ln_square(1)
                    ln_square(2)
                if t == 2:
                    ln_deviation(1)
                    ln_deviation(2)
                if t >= 1:
                    hm_turned(t - 1)
                if t == 2:
                    ln_swish(1)
                    ln_swish(2)
                if t != 1 and t + 2 < NT:
                    mix_high(t + 2)
            hm_turned(NT - 1)
            act.wait_ge(rt_done, NT)
            act.activation(gdif[:, :, :], gdif[:, :, :], ACT.Exp).then_inc(exp_done, 1)
            act.activation(edif[:, :], edif[:, :], ACT.Exp).then_inc(exp_done, 1)

            def high(j, n):
                act.wait_ge(raw_in[RAW[n]], raw_count(j, n))
                act.wait_ge(piece_used, NP * j + n + 1 + (NP - 4))
                act.activation(we_h[n % 4], raw[RAW[n]], ACT.Copy).then_inc(high_done, 1)

            def rows_high(j, b):
                act.wait_ge(xe_tr, 2 * j + 1 + b)
                act.activation(part_h[b], xe_ps, ACT.Copy).then_inc(xe_high, 1)

            def silu(j, b):
                act.wait_ge(piece_used, NP * (j + 1) + (2, 6)[b])
                act.wait_ge(h_tr, 2 * j + 1 + b)
                act.activation(act_t[b], gate_ps, ACT.Silu).then_inc(silu_done, 1)

            def result(j, b):
                act.wait_ge(piece_used, NP * j + (NP + 8, NP)[b])
                act.wait_ge(scat[b], 16 * (j + 1))
                act.activation(ye[b], ye_ps, ACT.Copy).then_inc(ye_done, 1)

            def body(j, overflow):
                act.activation(warm[:, :], eps[:, :], ACT.Silu)
                high(j, 0)
                high(j, 1)
                rows_high(j, 0)
                high(j, 2)
                result(j, 1)
                for n in (3, 4, 5):
                    high(j, n)
                silu(j, 0)
                rows_high(j, 1)
                for n in (6, 7, 8, 9):
                    high(j, n)
                silu(j, 1)
                high(j, 10)
                high(j, 11)
                result(j, 0)

            n_pairs = pair_loop(act, body)
            result(n_pairs, 1)
            for t in range(NT):
                r = ROWS[t]
                act.wait_ge(f_acc, 2 * t + 2)
                if t:
                    act.wait_ge(f_sum, t)
                act.activation(junk_f[0:r, :], x_in[t][0:r, :], ACT.Square,
                               accum_out=stat[0:r, 0, t:t + 1]).then_inc(f_sum, 1)
                act.wait_ge(f_sum, t + 1)
                act.activation(stat[0:r, 1, t:t + 1], stat[0:r, 0, t:t + 1], ACT.Sqrt, bias=eps[0:r, :],
                               scale=1.0 / D).then_inc(f_sd, 1)

        @block.tensor
        def _(pe):
            def product(out, parts, last):
                for i, (sh, sl_, mh, ml) in enumerate(parts):
                    pe.matmul(out, sh, mh, start=(i == 0), stop=False)
                    pe.matmul(out, sh, ml, start=False, stop=False)
                    ins = pe.matmul(out, sl_, mh, start=False, stop=(i == len(parts) - 1 and last))
                return ins

            pe.wait_ge(const_done, 1)

            def turn_x(t):
                r = ROWS[t]
                pe.wait_ge(xs_done, t + 1)
                if t >= 2:
                    pe.wait_ge(xl_done, t - 1)
                for k in range(KD):
                    ins = pe.transpose(xa_ps[t % 2][:, k, 0:r], xa[t][0:r, k * P:(k + 1) * P], ident[0:r, 0:r])
                ins.then_inc(xtr_done, 1)

            def in_proj(j, n):
                tok, w = BLOCKS[n]
                ins = product(z_ps[j % 2][:, tok:tok + w],
                              [(part_h[j % 2][:, k, :], part_l[j % 2][:, k, :], xT_h[:, k, tok:tok + w],
                                xT_l[:, k, tok:tok + w]) for k in range(KD)], True)
                if n == 2:
                    ins.then_inc(z_done, 1)

            def turn_state(s):
                for c in range(NC):
                    if s < 2:
                        end = CS + SEQ if s == 0 else VW
                        ins = pe.transpose(st_ps[s % 2][0:CS, c * P:(c + 1) * P], v_ext[:, c, end - CS:end], ident[:, :])
                    else:
                        ins = pe.transpose(st_ps[s % 2][0:PS, c * P:(c + 1) * P], u_end[:, c, s - 2, :], ident[:, :])
                ins.then_inc(st_tr, 1)

            def ln_mean(n):
                tok, w = BLOCKS[n]
                for c in range(NC):
                    ins = pe.matmul(mean_ps[n][:, 0:w], mean_w[:, :], hc[:, c, hc_at(tok):hc_at(tok) + w],
                                    start=(c == 0), stop=(c == NC - 1))
                ins.then_inc(mean_done, 1)

            per_block = BANK // P
            for t in range(NT):
                turn_x(t)
                if t == 1:
                    pe.wait_ge(rows_in, 16 * 7)
                    for c in range(NC):
                        ins = pe.transpose(cols_ps[:, c, :], rows[:, c * P:(c + 1) * P], ident[0:NROW, 0:NROW])
                    ins.then_inc(rows_tr, 1)
                if t == per_block + 1:
                    pe.wait_ge(wl_done, 1)
                    pe.wait_ge(xl_done, per_block)
                    in_proj(0, 0)
            for n in (1, 2):
                pe.wait_ge(xl_done, min((n + 1) * per_block, NT))
                in_proj(0, n)
            pe.wait_ge(cols_done, 1)
            for j in range(1, NCH):
                pe.wait_ge(wl_done, j + 1)
                if j >= 2:
                    kind, c = KINDS[j - 2]
                    if kind == "gate":
                        pe.wait_ge(sg_done, c + 1)
                    elif kind == "value":
                        pe.wait_ge(v_done, c + 1)
                    else:
                        pe.wait_ge(u_done, POOL_ORDER.index(c) + 1)
                for n in range(3):
                    in_proj(j, n)
                    if j == NCH - 1 and n == 0:
                        pe.wait_ge(conv_done, 1)
                        pe.wait_ge(st_done, 2)
                        ln_mean(0)
                if j == 9:
                    pe.wait_ge(v_done, NC)
                    turn_state(0)
                    turn_state(1)

            pe.wait_ge(consts_in, 16 * (6 + GROUPS))
            def pool_lin_product(i):
                g = POOL_ORDER[i]
                pe.wait_ge(d_done, i + 1)
                if i >= 2:
                    pe.wait_ge(yp_done, i - 1)
                for n, (tok, w) in enumerate(BLOCKS):
                    off = PS + tok if tok < SEQ else PS + tok + PS
                    ins = pe.matmul(z_ps[i % 2][:, tok:tok + w], plin[:, g, :], u_ext[:, g, off:off + w],
                                    start=True, stop=True)
                ins.then_inc(pl_done, 1)

            def ln_variance(n):
                w = BLOCKS[n][1]
                pe.wait_ge(sq_done, n + 1)
                for c in range(NC):
                    ins = pe.matmul(var_ps[n][:, 0:w], mean_w[:, :], sq[n][:, c, 0:w], start=(c == 0), stop=(c == NC - 1))
                ins.then_inc(var_done, 1)

            ln_variance(0)
            pe.wait_ge(u_done, NG)
            pool_lin_product(0)
            pool_lin_product(1)
            pe.wait_ge(cen_done, 1)
            pe.wait_ge(lnsd_done, 1)
            turn_state(2)
            turn_state(3)
            pool_lin_product(2)
            pool_lin_product(3)
            pe.wait_ge(yp_dve, NG - 2)

            def out_proj(t):
                r = ROWS[t]
                pe.wait_ge(ml_done, t + 1)
                if t == 0:
                    pe.wait_ge(wl_done, NCH + len(POOL_WO))
                    pe.wait_ge(wl_dve, len(DVE_WO))
                if t >= 2:
                    pe.wait_ge(x2_done, t - 1)
                for half in range(2):
                    c0 = half * BANK
                    ins = product(out_ps[t % 2][0:r, c0:c0 + BANK],
                                  [(part_h[t % 2][:, k, 0:r], part_l[t % 2][:, k, 0:r], wo_h[:, k, c0:c0 + BANK],
                                    wo_l[:, k, c0:c0 + BANK]) for k in range(KD)], True)
                ins.then_inc(out_done, 1)

            def turn_hm(t):
                r = ROWS[t]
                pe.wait_ge(hm_done, t + 1)
                if t:
                    pe.wait_ge(hmT_done, t)
                else:
                    pe.wait_ge(st_done, 4)
                for k in range(KD):
                    ins = pe.transpose(x_ps[:, k, 0:r], hm[t % 2][0:r, k * P:(k + 1) * P], ident[0:r, 0:r])
                ins.then_inc(hmtr_done, 1)

            def logits(t):
                r = ROWS[t]
                pe.wait_ge(hmT_done, t + 1)
                if t:
                    pe.wait_ge(lg_read, t)
                else:
                    pe.wait_ge(lnsd_done, 3)
                for k in range(KD):
                    ins = pe.matmul(lg_ps[0:r, :], hmT[:, k, 0:r], w_rt[:, k, :], start=(k == 0), stop=(k == KD - 1))
                ins.then_inc(lg_done, 1)

            def ranks(t):
                pe.wait_ge(counted, t + 1)
                if t:
                    pe.wait_ge(placed, t)
                else:
                    pe.wait_ge(const_done, 1)
                pe.matmul(rk_ps[:, t, :], tri[:, :], MS[:, t, :], start=True, stop=False)
                ins = pe.matmul(rk_ps[:, t, :], ones[:, :], pref[:, t, :], start=False, stop=True)
                if t == NT - 1:
                    ins = pe.matmul(rk_ps[:, NT, :], ones[:, :], pref[:, NT, :], start=True, stop=True)
                ins.then_inc(rk_done, 1)

            def slot_table(kind, a, b):
                hot, out = (hot_own, ix_ps[:, 0:E]) if kind == "own" else (hot_over, ix_ps[:, E:NBLK])
                for s in range(a, b):
                    if kind == "own" and s % 2 == 0:
                        pe.wait_ge(hot_done, s // 2 + 1)
                    ins = pe.matmul(out, hots[s], hot[:, s, :], start=(s == 0), stop=(s == 2 * NT - 1))
                if b == 2 * NT:
                    ins.then_inc(ix_done, 1)

            for t in range(NT + 3):
                if t < NT:
                    out_proj(t)
                elif t == NT:
                    pe.sem_inc(piece_used, NP)
                if t == 1:
                    pe.wait_ge(conv_done, 2)
                    pe.wait_ge(help_done, 2 * TAPS)
                    ln_mean(1)
                    ln_mean(2)
                if t == 2:
                    pe.wait_ge(cen_done, 3)
                    ln_variance(1)
                    ln_variance(2)
                if 3 <= t < NT + 2:
                    logits(t - 2)
                if 1 <= t <= NT:
                    turn_hm(t - 1)
                if t == 2:
                    logits(0)
                if t == NT + 1:
                    slot_table("own", 0, 2 * NT - 6)
                if t >= 3:
                    ranks(t - 3)
            slot_table("own", 2 * NT - 6, 2 * NT)
            pe.sem_inc(h_tr, 2)
            def turn_rows(j, b, first=False):
                pe.wait_ge(gath[b], 16 * (j + 1))
                if not first:
                    pe.wait_ge(xe_low, 2 * j + b)
                for k in range(KD):
                    ins = pe.transpose(xe_ps[:, k, :], xe[b][:, k * P:(k + 1) * P], ident[:, :])
                ins.then_inc(xe_tr, 1)

            def expert_in(j, n, out):
                b, _, half = PIECES[n]
                wait_low(pe, j, n)
                wh = we_h[n % 4].rearrange("p (k n) -> p k n", n=FF)
                wl = we_l[n % 4].rearrange("p (k n) -> p k n", n=FF)
                for i in range(4):
                    k = half * 4 + i
                    pe.matmul(out, part_h[b][:, k, :], wh[:, i, :], start=(k == 0), stop=False)
                    pe.matmul(out, part_h[b][:, k, :], wl[:, i, :], start=False, stop=False)
                    ins = pe.matmul(out, part_l[b][:, k, :], wh[:, i, :], start=False, stop=(k == KD - 1))
                ins.then_inc(piece_used, 1)

            def expert_out(j, n):
                b, _, half = PIECES[n]
                wait_low(pe, j, n)
                wh = we_h[n % 4].rearrange("p (k n) -> p k n", n=D)
                wl = we_l[n % 4].rearrange("p (k n) -> p k n", n=D)
                for i in range(2):
                    k = half * 2 + i
                    for c0 in (0, BANK):
                        out = ye_ps[:, c0:c0 + BANK]
                        pe.matmul(out, hT_h[:, k, :], wh[:, i, c0:c0 + BANK], start=(k == 0), stop=False)
                        pe.matmul(out, hT_h[:, k, :], wl[:, i, c0:c0 + BANK], start=False, stop=False)
                        ins = pe.matmul(out, hT_l[:, k, :], wh[:, i, c0:c0 + BANK], start=False, stop=(k == KF - 1))
                ins.then_inc(piece_used, 1)

            def turn_hidden(j, b):
                pe.wait_ge(act_done, 2 * j + 3 + b)
                pe.wait_ge(h_low, 2 * j + 2 + b)
                for k in range(KF):
                    ins = pe.transpose(h_ps[:, k, :], hid[b][:, k * P:(k + 1) * P], ident[:, :])
                ins.then_inc(h_tr, 1)

            turn_rows(0, 0, first=True)

            def body(j, overflow, first=False):
                pe.wait_ge(xe_low, 2 * j + 1)
                pe.wait_ge(silu_done, 2 * j + 2)
                expert_in(j, 0, gate_ps)
                expert_in(j, 1, gate_ps)
                if first:
                    pe.wait_ge(hot_done, NT + 1)
                    pe.wait_ge(idx_done, 1)
                    slot_table("over", 0, 2 * NT)
                turn_rows(j, 1)
                pe.wait_ge(act_done, 2 * j + 2)
                expert_in(j, 2, up_ps)
                expert_in(j, 3, up_ps)
                pe.wait_ge(xe_low, 2 * j + 2)
                pe.wait_ge(silu_done, 2 * j + 3)
                expert_in(j, 4, gate_ps)
                expert_in(j, 5, gate_ps)
                turn_hidden(j, 0)
                pe.wait_ge(h_low, 2 * j + 3)
                pe.wait_ge(ye_done, 2 * j + 2)
                expert_out(j, 6)
                expert_out(j, 7)
                pe.wait_ge(act_done, 2 * j + 3)
                expert_in(j, 8, up_ps)
                expert_in(j, 9, up_ps)
                turn_rows(j + 1, 0)
                turn_hidden(j, 1)
                pe.wait_ge(h_low, 2 * j + 4)
                pe.wait_ge(ye_done, 2 * j + 4)
                expert_out(j, 10)
                expert_out(j, 11)

            body(0, False, first=True)
            n_pairs = pair_loop(pe, body, 1)

        @block.vector
        def _(dve):
            n_dve = NP - len(POOL_PIECES)
            dve.sem_inc(low_dve, n_dve)
            dve.sem_inc(act_done, 2)
            dve.sem_inc(h_low, 2)
            dve.memset(pref[:, 0, :], 0.0)
            dve.memset(cum[0][:, :], 0.0)
            dve.memset(cum[1][:, :], 0.0)
            dve.memset(gdif[:, :, :], 0.0)
            dve.memset(edif[:, :], 0.0).then_inc(zeros_set, 1)
            dve.wait_ge(zeros_set, 1)
            dve.wait_ge(g1_in, 16)

            def x_scaled(t):
                r = ROWS[t]
                dve.wait_ge(sd1_done, t + 1)
                dve.reciprocal(stat[0:r, 2, t:t + 1], stat[0:r, 1, t:t + 1]).then_inc(rs1_done, 1)
                dve.wait_ge(rs1_done, t + 1)
                dve.scalar_tensor_tensor(xa[t][0:r, :], xa[t][0:r, :], stat[0:r, 2, t:t + 1], g1_bc[0:r, :],
                                         ALU.mult, ALU.mult).then_inc(xs_done, 1)

            def x_low(t):
                r, tok = ROWS[t], t * P
                dve.wait_ge(xh_done, t + 1)
                dve.tensor_tensor(xT_l[:, :, tok:tok + r], xa_ps[t % 2][:, :, 0:r], xT_h[:, :, tok:tok + r].bitcast(F32),
                                  ALU.subtract).then_inc(xl_done, 1)

            for t in range(NT):
                x_scaled(t)
                if t >= 2:
                    x_low(t - 2)
            x_low(NT - 2)
            x_low(NT - 1)

            steps = [0]
            at_tap, last = {}, {}

            def glu(c):
                z = z_ps[J["value", c] % 2]
                dve.wait_ge(sg_done, c + 1)
                dve.wait_ge(z_done, J["value", c] + 1)
                dve.tensor_tensor(v_ext[:, c, CS:CS + SEQ], z[:, 0:SEQ], sg[:, 0:SEQ], ALU.mult).then_inc(conv_step, 1)
                dve.tensor_tensor(v_ext[:, c, CS + SEQ + CS:VW], z[:, SEQ:T], sg[:, SEQ:T],
                                  ALU.mult).then_inc(v_done, 1)
                steps[0] += 1
                dve.wait_ge(v_done, c + 1)
                dve.wait_ge(conv_step, steps[0])

            def taps(n, *parts):
                for _ in range(n):
                    for part, c in parts:
                        a, b = PART[part]
                        j = at_tap.get((part, c), 0)
                        if j:
                            dve.wait_ge(conv_step, last[part, c])
                            dve.scalar_tensor_tensor(hc[:, c, a:b], v_ext[:, c, a + j:b + j], cols[:, c, j:j + 1],
                                                     hc[:, c, a:b], ALU.mult, ALU.add).then_inc(conv_step, 1)
                        else:
                            dve.tensor_scalar(hc[:, c, a:b], v_ext[:, c, a:b], cols[:, c, 0:1],
                                              cols[:, c, R_B:R_B + 1], ALU.mult, ALU.add).then_inc(conv_step, 1)
                        steps[0] += 1
                        at_tap[part, c], last[part, c] = j + 1, steps[0]

            dve.wait_ge(cols_done, 1)
            dve.wait_ge(pad_done, 1)
            glu(0)
            taps(21, ("A", 0), ("B", 0))
            glu(1)
            taps(TAPS - 21, ("A", 0), ("B", 0))
            taps(10, ("A", 1))
            glu(2)
            taps(TAPS - 10, ("A", 1), ("A", 2))
            taps(10, ("A", 2), ("B", 2))
            glu(3)
            taps(TAPS, ("A", 3))
            dve.wait_ge(conv_step, steps[0])
            dve.engine_nop().then_inc(conv_done, 1)

            def ln_center(n):
                tok, w = BLOCKS[n]
                y = hc[:, :, hc_at(tok):hc_at(tok) + w]
                dve.wait_ge(mean_done, n + 1)
                dve.tensor_tensor(y, y, mean_ps[n][:, 0:w].unsqueeze(1).to_broadcast([P, NC, w]),
                                  ALU.subtract).then_inc(cen_done, 1)

            def ln_normal(n):
                tok, w = BLOCKS[n]
                y = hc[:, :, hc_at(tok):hc_at(tok) + w]
                dve.wait_ge(lnsd_done, n + 1)
                dve.reciprocal(ln_sd[n], ln_sd[n]).then_inc(lnrs_done, 1)
                dve.wait_ge(lnrs_done, n + 1)
                dve.wait_ge(cen_done, n + 1)
                dve.tensor_tensor(y, y, ln_sd[n].unsqueeze(1).to_broadcast([P, NC, w]), ALU.mult).then_inc(nrm_done, 1)

            def wo_low(k):
                dve.wait_ge(wh_done, NCH + k + 1)
                dve.tensor_tensor(wo_l[:, k, :], wo_raw[k % 4], wo_h[:, k, :].bitcast(F32), ALU.subtract).then_inc(wl_dve, 1)

            taps(2, ("B", 2), ("C", 3))
            ln_center(0)
            taps(4, ("B", 2), ("C", 3))
            wo_low(0)
            wo_low(1)
            taps(2, ("B", 2), ("C", 3))
            ln_normal(0)
            wo_low(4)
            wo_low(5)
            taps(1, ("B", 2), ("C", 3))
            wo_low(6)
            for i in (2, 3):
                g = POOL_ORDER[i]
                dve.wait_ge(pl_done, i + 1)
                dve.tensor_scalar(u_ext[:, g, 0:T], z_ps[i % 2][:, 0:T], cols[:, g, R_SC:R_SC + 1], None,
                                  ALU.mult).then_inc(yp_dve, 1)

            def mix_low(t):
                r, tok = ROWS[t], t * P
                dve.wait_ge(mh_done, t + 1)
                dve.tensor_tensor(part_l[t % 2][:, 0:NG, 0:r], u_ext[:, :, tok:tok + r],
                                  part_h[t % 2][:, 0:NG, 0:r].bitcast(F32), ALU.subtract)
                dve.tensor_tensor(part_l[t % 2][:, NG:KD, 0:r], hc[:, :, hc_at(tok):hc_at(tok) + r],
                                  part_h[t % 2][:, NG:KD, 0:r].bitcast(F32), ALU.subtract).then_inc(ml_done, 1)

            def residual(t):
                r = ROWS[t]
                dve.wait_ge(out_done, t + 1)
                dve.wait_ge(xb_done, t + 1)
                dve.tensor_tensor(xt[t % 2][0:r, :], out_ps[t % 2][0:r, :], xt[t % 2][0:r, :],
                                  ALU.add).then_inc(x2_done, 1)

            def hm_row(t):
                r = ROWS[t]
                dve.wait_ge(sd2_done, t + 1)
                dve.reciprocal(stat[0:r, 5, t:t + 1], stat[0:r, 4, t:t + 1]).then_inc(rs2_done, 1)
                dve.wait_ge(rs2_done, t + 1)
                if t >= 2:
                    dve.wait_ge(hm_out[t % 2], 16 * (t // 2))
                    dve.wait_ge(hmtr_done, t - 1)
                dve.scalar_tensor_tensor(hm[t % 2][0:r, :].rearrange("p (k q) -> p q k", k=KD),
                                         xt[t % 2][0:r, :].rearrange("p (q k) -> p q k", k=KD), stat[0:r, 5, t:t + 1],
                                         g2_bc[0:r, :].rearrange("p (q k) -> p q k", k=KD),
                                         ALU.mult, ALU.mult).then_inc(hm_done, 1)

            done = [0]

            def step(ins):
                done[0] += 1
                ins.then_inc(rt_step, 1)
                dve.wait_ge(rt_step, done[0])

            def route(t):
                r = ROWS[t]
                dve.wait_ge(lg_done, t + 1)
                dve.tensor_tensor(lgt[0:r, 0:GROUPS], lg_ps[0:r, 0:GROUPS], b_rt[0:r, 0:GROUPS], ALU.add)
                step(dve.tensor_tensor(lgt[0:r, 8:8 + E], lg_ps[0:r, GROUPS:LB], b_rt[0:r, GROUPS:LB], ALU.add))
                dve.engine_nop().then_inc(lg_read, 1)
                step(dve.max(top[0:r, 0, :], lgt[0:r, 0:8]))
                step(dve.max_index(topi[0:r, 0, :], top[0:r, 0, :], lgt[0:r, 0:8]))
                step(dve.tensor_copy(gsel[0:r, :], topi[0:r, 0, 0:1]))
                step(dve.tensor_scalar(pen[0:r, :], grp[0:r, :], gsel[0:r, :], LOWEST, ALU.not_equal, ALU.mult))
                step(dve.tensor_tensor(le[0:r, :], lgt[0:r, 8:8 + E], pen[0:r, :], ALU.add))
                step(dve.max(top[0:r, 1, :], le[0:r, :]))
                step(dve.max_index(topi[0:r, 1, :], top[0:r, 1, :], le[0:r, :]))
                dve.tensor_copy(eid[0:r, t, :], topi[0:r, 1, 0:2])
                dve.tensor_scalar(gdif[0:r, t, :], lgt[0:r, 0:GROUPS], top[0:r, 0, 0:1], None, ALU.subtract)
                step(dve.tensor_scalar(edif[0:r, t:t + 1], top[0:r, 1, 1:2], top[0:r, 1, 0:1], None, ALU.subtract))
                dve.engine_nop().then_inc(rt_done, 1)

            s_r, s_b, s_q, s_o, s_w = (sl[:, i, :] for i in range(5))
            lane = sl[:, 5, :]
            slots_e = eid.rearrange("p t k -> p (t k)")

            def count(t):
                step(dve.tensor_tensor(Mx[:, 2 * t:2 * t + 2, :], iota[:, 0:E].unsqueeze(1).to_broadcast([P, 2, E]),
                                       eid[:, t, :].unsqueeze(2).to_broadcast([P, 2, E]), ALU.is_equal))
                step(dve.tensor_tensor(MS[:, t, :], Mx[:, 2 * t, :], Mx[:, 2 * t + 1, :], ALU.add))
                dve.tensor_tensor(pref[:, t + 1, :], pref[:, t, :], MS[:, t, :], ALU.add).then_inc(counted, 1)
                dve.wait_ge(counted, t + 1)

            def place(t):
                a, b = 2 * t, 2 * t + 2
                dve.wait_ge(rk_done, t + 1)
                if t == NT - 1:
                    step(dve.tensor_copy(rk_n[:, :], rk_ps[:, NT, :]))
                step(dve.tensor_tensor(prod_t, Mx[:, a:b, :], rk_ps[:, t, :].unsqueeze(1).to_broadcast([P, 2, E]),
                                       ALU.mult))
                dve.engine_nop().then_inc(placed, 1)
                step(dve.tensor_reduce(s_r[:, a:b], prod_t, AX_X, ALU.add))
                step(dve.tensor_copy(sl_i[:, 0, a:b], s_r[:, a:b]))
                dve.tensor_scalar(sl_i[:, 1, a:b], sl_i[:, 0, a:b], P - 1, None, ALU.bitwise_and)
                step(dve.tensor_scalar(sl_i[:, 2, a:b], sl_i[:, 0, a:b], 7, None, ALU.arith_shift_right))
                dve.tensor_copy(lane[:, a:b], sl_i[:, 1, a:b])
                step(dve.tensor_copy(s_q[:, a:b], sl_i[:, 2, a:b]))
                step(dve.tensor_scalar(s_o[:, a:b], s_r[:, a:b], float(P), None, ALU.is_ge))
                dve.tensor_scalar(s_w[:, a:b], slots_e[:, a:b], -1.0, float(E - 1), ALU.mult, ALU.add)
                dve.scalar_tensor_tensor(s_b[:, a:b], s_o[:, a:b], float(NBLK), slots_e[:, a:b], ALU.mult, ALU.add)
                step(dve.tensor_tensor(s_q[:, a:b], s_q[:, a:b], slots_e[:, a:b], ALU.add))
                dve.tensor_tensor(hot_own[:, a:b, :], iota[:, 0:E].unsqueeze(1).to_broadcast([P, 2, E]),
                                  s_b[:, a:b].unsqueeze(2).to_broadcast([P, 2, E]), ALU.is_equal)
                for s in (a, b - 1):
                    ins = dve.tensor_scalar(hots[s], iota[:, :], lane[:, s:s + 1], tokv[:, s:s + 1], ALU.is_equal,
                                            ALU.mult)
                ins.then_inc(hot_done, 1)

            dve.wait_ge(consts_in, 16 * (6 + GROUPS))
            dve.wait_ge(const_done, 1)
            mix_low(0)
            mix_low(1)
            taps(TAPS - 10 - 9, ("B", 2), ("C", 3))
            taps(TAPS - (TAPS - 10), ("C", 3))
            dve.wait_ge(conv_step, steps[0])
            dve.engine_nop().then_inc(conv_done, 1)
            for t in range(NT + 3):
                if t < NT:
                    residual(t)
                    hm_row(t)
                if t == 1:
                    mix_low(t + 2)
                    ln_center(1)
                    ln_center(2)
                if t == 2:
                    ln_normal(1)
                    ln_normal(2)
                if t != 1 and t + 2 < NT:
                    mix_low(t + 2)
                if 2 <= t < NT + 2:
                    route(t - 2)
                    count(t - 2)
                if t >= 3:
                    place(t - 3)

            def slots(a, b):
                step(dve.tensor_scalar(idx_f[:, 1, a:b], ix_ps[:, a:b], 0.0, FAR, ALU.is_equal, ALU.mult))
                step(dve.scalar_tensor_tensor(idx_f[:, 0, a:b], ix_ps[:, a:b], -1.0, idx_f[:, 1, a:b], ALU.add, ALU.add))
                step(dve.tensor_copy(s_idx[:, 1 + a:1 + b], idx_f[:, 0, a:b]))
                dve.tensor_scalar(g_idx[:, a:b], s_idx[:, 1 + a:1 + b], 1, None, ALU.logical_shift_right).then_inc(idx_done, 1)

            def overflow_counts():
                step(dve.tensor_scalar(nb[:, :], rk_n[:, :], float(P), None, ALU.is_gt))
                for m in range(2, -(-T // P)):
                    step(dve.scalar_tensor_tensor(nb[:, :], rk_n[:, :], float(m * P), nb[:, :], ALU.is_gt, ALU.add))
                step(dve.tensor_copy(cum[0][:, 16:16 + E], nb[:, :]))
                for i, s in enumerate((1, 2, 4, 8, 16)):
                    src, dst = cum[i % 2], cum[(i + 1) % 2]
                    step(dve.tensor_tensor(dst[:, 16:16 + E], src[:, 16:16 + E], src[:, 16 - s:16 - s + E], ALU.add))
                ends = cum[1][:, 16:16 + E]
                step(dve.tensor_tensor(base[:, :], ends, nb[:, :], ALU.subtract))

            def overflow_blocks():
                step(dve.tensor_tensor(prod, Mx, base[:, :].unsqueeze(1).to_broadcast([P, 2 * NT, E]), ALU.mult))
                step(dve.tensor_reduce(s_b, prod, AX_X, ALU.add))
                step(dve.tensor_tensor(s_b, s_b, s_w, ALU.add))
                step(dve.tensor_tensor(s_b, s_b, s_o, ALU.mult))
                step(dve.tensor_tensor(s_b, s_b, s_q, ALU.add))
                dve.tensor_tensor(hot_over, iota[:, E:NBLK].unsqueeze(1).to_broadcast([P, 2 * NT, OVERFLOW]),
                                  s_b.unsqueeze(2).to_broadcast([P, 2 * NT, OVERFLOW]), ALU.is_equal).then_inc(hot_done, 1)

            def overflow_plan():
                ends = cum[1][:, 16:16 + E]
                step(dve.tensor_tensor(cmp_[:, :, :], ends[0:1, :].unsqueeze(1).to_broadcast([1, OVERFLOW, E]),
                                       iota[0:1, 0:OVERFLOW].unsqueeze(2).to_broadcast([1, OVERFLOW, E]), ALU.is_le))
                step(dve.tensor_reduce(eob_f[:, 0:OVERFLOW], cmp_[:, :, :], AX_X, ALU.add))
                step(dve.tensor_scalar(eob_f[:, 0:OVERFLOW], eob_f[:, 0:OVERFLOW], float(E - 1), None, ALU.min))
                evens = iota[0:1, 0:OVERFLOW:2]
                step(dve.tensor_scalar(cmp_[:, 0, 0:OVERFLOW // 2], evens, ends[0:1, E - 1:E], None, ALU.is_lt))
                step(dve.tensor_reduce(eob_f[:, OVERFLOW:OVERFLOW + 1], cmp_[:, 0, 0:OVERFLOW // 2], AX_X, ALU.add))
                step(dve.tensor_scalar(eob_f[:, OVERFLOW:OVERFLOW + 1], eob_f[:, OVERFLOW:OVERFLOW + 1], float(PAIRS), None,
                                       ALU.add))
                dve.tensor_copy(eob[:, 0:OVERFLOW + 1], eob_f[:, 0:OVERFLOW + 1]).then_inc(plan_done, 1)
                dve.wait_ge(exp_done, 2)
                step(dve.tensor_reduce(gtmp[:, 0, :], gdif[:, :, :], AX_X, ALU.add))
                step(dve.tensor_scalar(gtmp[:, 1, :], edif[:, :], 1.0, None, ALU.add))
                step(dve.tensor_tensor(gtmp[:, 0, :], gtmp[:, 0, :], gtmp[:, 1, :], ALU.mult))
                step(dve.reciprocal(gates[:, 0, :], gtmp[:, 0, :]))
                step(dve.tensor_tensor(gates[:, 1, :], gates[:, 0, :], edif[:, :], ALU.mult))

            dve.memset(ye_ps, 0.0)
            dve.wait_ge(ix_done, 1)
            slots(0, E)

            def low(j, n):
                dve.wait_ge(high_done, NP * (j + 1) + n + 1)
                dve.tensor_tensor(we_l[n % 4], raw[RAW[n]], we_h[n % 4].bitcast(F32), ALU.subtract).then_inc(low_dve, 1)

            def rows_low(j, b):
                dve.wait_ge(xe_high, 2 * j + 1 + b)
                dve.tensor_tensor(part_l[b], xe_ps, part_h[b].bitcast(F32), ALU.subtract).then_inc(xe_low, 1)

            def hidden(j, b):
                dve.wait_ge(silu_done, 2 * j + 3 + b)
                dve.wait_ge(piece_used, NP * (j + 1) + (4, 10)[b])
                dve.tensor_tensor(hid[b].rearrange("p (k q) -> p q k", k=KF),
                                  act_t[b].rearrange("p (q k) -> p q k", k=KF),
                                  up_ps.rearrange("p (q k) -> p q k", k=KF), ALU.mult).then_inc(act_done, 1)

            def hidden_parts(j, b):
                dve.wait_ge(h_tr, 2 * j + 3 + b)
                dve.wait_ge(piece_used, NP * j + (12, 20)[b])
                dve.tensor_copy(hT_h, h_ps).then_inc(h_high, 1)
                dve.wait_ge(h_high, 2 * j + 1 + b)
                dve.tensor_tensor(hT_l, h_ps, hT_h.bitcast(F32), ALU.subtract).then_inc(h_low, 1)

            def body(j, overflow, first=False):
                low(j, 0)
                low(j, 1)
                if first:
                    overflow_counts()
                rows_low(j, 0)
                if first:
                    overflow_blocks()
                low(j, 2)
                low(j, 3)
                if first:
                    dve.wait_ge(ix_done, 2)
                    slots(E, NBLK)
                low(j, 4)
                rows_low(j, 1)
                low(j, 6)
                hidden(j, 0)
                low(j, 7)
                low(j, 8)
                hidden_parts(j, 0)
                if first:
                    overflow_plan()
                low(j, 9)
                low(j, 10)
                hidden(j, 1)
                hidden_parts(j, 1)

            body(0, False, first=True)
            n_pairs = pair_loop(dve, body, 1)
            def combine(t):
                r, s = ROWS[t], t % FB
                dve.wait_ge(f_x[t], 16)
                dve.wait_ge(f_in[s], 16 * (t // FB + 1))
                for k in range(2):
                    dve.scalar_tensor_tensor(x_in[t][0:r, :], y_in[s][0:r, k * D:(k + 1) * D], gates[0:r, k, t:t + 1],
                                             x_in[t][0:r, :], ALU.mult, ALU.add).then_inc(f_acc, 1)
                    dve.wait_ge(f_acc, 2 * t + k + 1)

            def final(t):
                r = ROWS[t]
                dve.wait_ge(f_sd, t + 1)
                dve.reciprocal(stat[0:r, 2, t:t + 1], stat[0:r, 1, t:t + 1]).then_inc(f_rs, 1)
                dve.wait_ge(f_rs, t + 1)
                dve.scalar_tensor_tensor(x_in[t][0:r, :], x_in[t][0:r, :], stat[0:r, 2, t:t + 1], gf_bc[0:r, :],
                                         ALU.mult, ALU.mult).then_inc(f_y, 1)

            for t in range(NT):
                combine(t)
                if t == 0:
                    dve.wait_ge(gf_in, 16)
                else:
                    final(t - 1)
            final(NT - 1)

        @block.gpsimd
        def _(pool):
            done = [0]

            def step(ins):
                done[0] += 1
                ins.then_inc(zero_done, 1)
                pool.wait_ge(zero_done, done[0])

            for m in (ident, tri):
                step(pool.memset(m[:, :], 0.0 if m is ident else 1.0))
            step(pool.affine_select(out=ident[:, :], in_=ident[:, :], compare_op=ALU.not_equal, fill=1.0, base=0,
                                    pattern=[[-1, P]], channel_multiplier=1))
            step(pool.affine_select(out=tri[:, :], in_=tri[:, :], compare_op=ALU.is_gt, fill=0.0, base=0,
                                    pattern=[[1, P]], channel_multiplier=-1))
            pool.memset(ones[:, :], 1.0)
            pool.memset(mean_w[:, :], 1.0 / DCONV)
            pool.memset(eps[:, :], EPS)
            for g in range(GROUPS):
                pool.memset(grp[:, g * PER:(g + 1) * PER], float(g))
            for i in range(PS):
                pool.memset(inv_cnt[:, i:i + 1], 1.0 / (i + 1))
            pool.memset(lgt[:, GROUPS:8], LOWEST)
            pool.memset(eid[:, :, :], 99.0)
            pool.memset(s_idx[:, 0:1], int(FAR))
            pool.memset(g_idx[:, NBLK:NBLK + 2], int(FAR))
            step(pool.iota(iota_i, pattern=[[1, P]], base=0, channel_multiplier=0))
            step(pool.iota(tok_i, pattern=[[2 * P, NT], [1, 2]], base=1, channel_multiplier=2))
            step(pool.tensor_copy(iota[:, :], iota_i))
            step(pool.tensor_copy(tokv[:, :], tok_i))
            pool.sem_inc(const_done, 1)

            def w_low(j):
                pool.wait_ge(wh_done, j + 1)
                pool.tensor_tensor(part_l[j % 2], w_raw[j % 3].rearrange("p (k n) -> p k n", k=KD),
                                   part_h[j % 2].bitcast(F32), ALU.subtract).then_inc(wl_done, 1)

            def wo_low(k):
                pool.wait_ge(wh_done, NCH + k + 1)
                pool.tensor_tensor(wo_l[:, k, :], wo_raw[k % 4], wo_h[:, k, :].bitcast(F32),
                                   ALU.subtract).then_inc(wl_done, 1)

            w_low(0)
            w_low(1)
            pool.wait_ge(cols_done, 1)
            pool.wait_ge(xtr_done, NT)
            for c in range(NC):
                pool.memset(v_ext[:, c, 0:CS], 0.0)
                pool.memset(u_ext[:, c, 0:PS], 0.0)
                pool.tensor_copy(v_ext[:, c, CS + SEQ:CS + SEQ + CS], cols[:, c, R_SV:R_SV + CS])
                step(pool.tensor_copy(u_ext[:, c, PS + SEQ:PS + SEQ + PS], cols[:, c, R_SP:R_SP + PS]))
            pool.sem_inc(pad_done, 1)
            n_win = [0]

            def win_op(ins):
                n_win[0] += 1
                ins.then_inc(win_step, 1)
                pool.wait_ge(win_step, n_win[0])

            def windows(g):
                i, w = POOL_ORDER.index(g), 2 << g
                pool.wait_ge(u_done, i + 1)
                src, lo = u_ext[:, g, :], 0
                for d in range(g + 1):
                    s = 1 << d
                    lo += s
                    win_op(pool.tensor_tensor(win[d % 2][:, lo:UW], src[:, lo:UW], src[:, lo - s:UW - s], ALU.add))
                    src = win[d % 2]
                win_op(pool.tensor_tensor(fix[:, g, 0:w - 1], src[:, PS:PS + w - 1], inv_cnt[:, 0:w - 1], ALU.mult))
                win_op(pool.tensor_tensor(fix[:, g, 0:w - 1], fix[:, g, 0:w - 1], u_ext[:, g, PS:PS + w - 1],
                                          ALU.subtract))
                pool.sem_inc(win_done, 1)

            def difference(g):
                i, w = POOL_ORDER.index(g), 2 << g
                pool.wait_ge(scaled_done, i + 1)
                win_op(pool.tensor_tensor(u_ext[:, g, PS:UW], win[g % 2][:, PS:UW], u_ext[:, g, PS:UW], ALU.subtract))
                pool.tensor_copy(u_ext[:, g, PS:PS + w - 1], fix[:, g, 0:w - 1]).then_inc(d_done, 1)
                pool.wait_ge(d_done, i + 1)

            added = [0, 0]

            def additions(h, n):
                c, a, b = HELPED[h]
                if added[h] == 0:
                    pool.wait_ge(prod_done, h * TAPS + 1)
                    pool.sem_inc(help_done, 1)
                for j in range(added[h] + 1, added[h] + n + 1):
                    pool.wait_ge(prod_done, h * TAPS + j + 1)
                    pool.wait_ge(help_done, h * TAPS + j)
                    pool.tensor_tensor(hc[:, c, a:b], hc[:, c, a:b], taps_pr[h][j % 2][:, 0:b - a],
                                       ALU.add).then_inc(help_done, 1)
                added[h] += n

            for step_j in range(1, NCH):
                if step_j + 1 < NCH:
                    w_low(step_j + 1)
                if step_j in help_n:
                    additions(0, help_n[step_j])
                if step_j == 7:
                    windows(3)
                if step_j == 8:
                    difference(3)
                if step_j == 10:
                    windows(2)
                if step_j == 11:
                    difference(2)
                    windows(1)
            difference(1)
            windows(0)
            wo_low(POOL_WO[0])
            wo_low(POOL_WO[1])
            difference(0)
            wo_low(POOL_WO[2])
            pool.wait_ge(consts_in, 16 * (6 + GROUPS))
            uses = [len(range(s, NT, 2)) for s in range(2)]
            for t in range(NT):
                r = ROWS[t]
                pool.wait_ge(xt_in[t % 2], 16 * (t // 2 + 1))
                pool.tensor_tensor(xt[t % 2][0:r, :], xt[t % 2][0:r, :], bo_bc[0:r, :], ALU.add).then_inc(xb_done, 1)
                if t == 1:
                    additions(1, TAPS - 1)

            pool.sem_inc(low_pool, len(POOL_PIECES))
            for s in range(2):
                pool.wait_ge(hm_out[s], 16 * uses[s])
                pool.wait_ge(x2_out[s], 16 * uses[s])
            pool.memset(xe[0], 0.0)
            pool.memset(xe[1], 0.0)
            pool.wait_ge(hmtr_done, NT)
            pool.memset(ye[0], 0.0)
            step(pool.memset(ye[1], 0.0))
            last_token, last_row = pool.to_reg(T - 1), pool.to_reg(2 * T - 1)

            def gather(b, at=cur):
                pool.indirect_dma_start(out=xe[b], out_offset=None, in_=hm_dram,
                                        in_offset=bass.IndirectOffsetOnAxis(ap=at[:, b:b + 1], axis=0),
                                        bounds_check=last_token, oob_is_err=False).then_inc(gath[b], 16)

            def scatter(b, at):
                pool.indirect_dma_start(out=y2_dram,
                                        out_offset=bass.IndirectOffsetOnAxis(ap=at, axis=0),
                                        in_=ye[b], in_offset=None,
                                        bounds_check=last_row, oob_is_err=False).then_inc(scat[b], 16)

            for b in range(2):
                scatter(b, s_idx[:, 0:1])
            pool.wait_ge(idx_done, 1)
            gather(0, g_idx)
            gather(1, g_idx)

            def low(j, n):
                pool.wait_ge(high_done, NP * (j + 1) + n + 1)
                pool.tensor_tensor(we_l[n % 4], raw[RAW[n]], we_h[n % 4].bitcast(F32), ALU.subtract).then_inc(low_pool, 1)

            def next_rows(j, b):
                pool.wait_ge(xe_tr, 2 * j + 1 + b)
                pool.wait_ge(idx_done, 2)
                pool.tensor_copy(cur[:, b:b + 1], g_idx[:, bass.ds(2 * j + 2 + b, 1)]).then_inc(cur_done, 1)
                pool.wait_ge(cur_done, 4 * j + (1, 3)[b])
                pool.sem_inc(cur_seen, 1)
                gather(b)

            def store_rows(j, b, last=False):
                pool.wait_ge(ye_done, 2 * j + (4, 3)[b])
                pool.wait_ge(scat[b], 16 * (j + 1))
                pool.wait_ge(idx_done, 2)
                pool.tensor_copy(cur[:, 2 + b:3 + b], s_idx[:, bass.ds(2 * j + (1, 0)[b], 1)]).then_inc(cur_done, 1)
                pool.wait_ge(cur_done, 4 * j + (1 if last else (4, 2)[b]))
                pool.sem_inc(cur_seen, 1)
                scatter(b, cur[:, 2 + b:3 + b])

            def body(j, overflow):
                next_rows(j, 0)
                store_rows(j, 1)
                next_rows(j, 1)
                low(j, 5)
                low(j, 11)
                store_rows(j, 0)

            n_pairs = pair_loop(pool, body)
            store_rows(n_pairs, 1, last=True)
            pool.wait_ge(scat[0], 16 * n_pairs + 16)
            pool.wait_ge(scat[1], 16 * n_pairs + 32)
            for b in (0, 1):
                pool.wait_ge(gath[b], 16 * n_pairs + 16)
            pool.sem_inc(sc_all, 1)


_INS = ["x_prompt", "x_sample", "state_pool", "state_conv", "norm1_g", "w_in", "pool_lin", "pool_scale", "conv_dw",
        "conv_dw_b", "conv_ln_g", "conv_ln_b", "w_out", "b_out", "norm2_g", "w_rg", "b_rg", "w_re", "b_re", "w_eg",
        "w_eu", "w_ed", "norm_f_g"]


def kernel(**inputs):
    import numpy as np
    import concourse.bacc as bacc
    from concourse.bass_utils import run_bass_kernel_spmd

    nc = bacc.Bacc("TRN2", target_bir_lowering=False, num_devices=1)
    arrays, args = {}, []
    for name in _INS:
        a = np.ascontiguousarray(inputs[name])
        arrays[f"in_{name}"] = a
        args.append(nc.dram_tensor(f"in_{name}", a.shape, mybir.dt.from_np(a.dtype), kind="ExternalInput").ap())
    sp, sc = inputs["state_pool"].shape, inputs["state_conv"].shape
    batch = inputs["x_prompt"].shape[0]
    shapes = [inputs["x_prompt"].shape, inputs["x_sample"].shape, (sp[0], batch) + tuple(sp[2:]),
              (sc[0], batch) + tuple(sc[2:]), sp, sc]
    outs = [nc.dram_tensor(f"out_{i}", list(s), F32, kind="ExternalOutput").ap() for i, s in enumerate(shapes)]
    trunk_kernel(nc, *args, *outs)
    r = run_bass_kernel_spmd(nc, [arrays], core_ids=[0])
    return tuple(r.results[0][f"out_{i}"] for i in range(len(shapes)))
```
